# Optimizing a Trainium2 kernel written in Bass

```python
import math
import jax
import jax.numpy as jnp
from jax import lax
import numpy as np

D_MODEL = 1024
BATCH = 1
SEQ = 512
DEPTH = 2

GRID_W = 64
CTX_LEN = 256
N_EVEN = (DEPTH + 1) // 2
N_ODD = DEPTH // 2

FOURIER_GROUPS = 4
FOURIER_DIM = 128
FOURIER_WIDTH = FOURIER_GROUPS * FOURIER_DIM
NA_HEADS = 8
NA_HEAD_DIM = 64
NA_WIDTH = NA_HEADS * NA_HEAD_DIM
NA_KH_MAX = 8
NA_KW = 16
AB_IN = FOURIER_WIDTH + 3 * NA_WIDTH
AB_OUT = FOURIER_WIDTH + NA_WIDTH
DIFF_HEADS = 8
DIFF_HEAD_DIM = 64
DIFF_V_DIM = 2 * DIFF_HEAD_DIM
DIFF_QK_WIDTH = DIFF_HEADS * 2 * DIFF_HEAD_DIM
DIFF_V_WIDTH = DIFF_HEADS * DIFF_V_DIM
ROPE_THETA = 10000.0
Q_BLOCK = 128
MLP_HIDDEN = 4 * D_MODEL
NORM_EPS = 1e-6
SUBLN_EPS = 1e-5
NEG_INF = -1e30

kernel_name = 'hybrid_fourier_natten_diffattn_dit'

def rms_norm(x, g, eps=NORM_EPS):
    xf = x.astype(jnp.float32)
    y = xf * lax.rsqrt(jnp.mean(xf * xf, axis=-1, keepdims=True) + eps)
    return (y * g.astype(jnp.float32)).astype(x.dtype)

def modulate(x, g, shift, scale):
    return rms_norm(x, g) * (1.0 + scale) + shift

def squared_relu_mlp(h, w_in, w_out):
    return jnp.square(jax.nn.relu(h @ w_in)) @ w_out

def to_heads(t, n_heads):
    b, l, _ = t.shape
    return t.reshape(b, l, n_heads, -1).transpose(0, 2, 1, 3)

def dense_attention(q, k, v):
    s = jnp.einsum('bhqd,bhkd->bhqk', q, k).astype(jnp.float32) * (q.shape[-1] ** -0.5)
    p = jax.nn.softmax(s, axis=-1).astype(v.dtype)
    return jnp.einsum('bhqk,bhkd->bhqd', p, v)

def fourier_mix(f):
    b, l, _ = f.shape
    z = f.reshape(b, l, FOURIER_GROUPS, FOURIER_DIM).astype(jnp.float32)
    y = jnp.fft.fft2(z, axes=(1, 3), norm='ortho').real
    return y.reshape(b, l, FOURIER_WIDTH).astype(f.dtype)

def neighbourhood_attention(q, k, v, kc, vc, rpb):
    b, n, _ = q.shape
    h, d, w = NA_HEADS, NA_HEAD_DIM, GRID_W
    rows_n = n // w
    kh = min(NA_KH_MAX, rows_n)

    def grid(t):
        return t.reshape(b, rows_n, w, h, d).transpose(0, 3, 1, 2, 4)

    qg = grid(q) * (d ** -0.5)
    kg, vg = grid(k), grid(v)
    kch, vch = to_heads(kc, h), to_heads(vc, h)

    r = jnp.arange(rows_n)
    col = jnp.arange(w)
    row_start = jnp.clip(r - kh // 2, 0, rows_n - kh)
    key_rows = row_start[:, None] + jnp.arange(kh)
    k_win = kg[:, :, key_rows]
    v_win = vg[:, :, key_rows]

    col_start = jnp.clip(col - NA_KW // 2, 0, w - NA_KW)
    in_win = (col[None, :] >= col_start[:, None]) & (col[None, :] < col_start[:, None] + NA_KW)
    dr = key_rows - r[:, None] + (NA_KH_MAX - 1)
    dc = jnp.clip(col[None, :] - col[:, None], -(NA_KW - 1), NA_KW - 1) + (NA_KW - 1)
    bias = rpb[:, dr[:, None, :, None], dc[None, :, None, :]].astype(jnp.float32)

    s_win = jnp.einsum('bhrqd,bhrjkd->bhrqjk', qg, k_win).astype(jnp.float32) + bias
    s_win = jnp.where(in_win[:, None, :], s_win, NEG_INF)
    s_ctx = jnp.einsum('bhrqd,bhkd->bhrqk', qg, kch).astype(jnp.float32)
    s = jnp.concatenate([s_win.reshape(b, h, rows_n, w, kh * w), s_ctx], axis=-1)
    p = jax.nn.softmax(s, axis=-1).astype(v.dtype)
    p_win = p[..., :kh * w].reshape(b, h, rows_n, w, kh, w)
    p_ctx = p[..., kh * w:]
    o = (jnp.einsum('bhrqjk,bhrjkd->bhrqd', p_win, v_win)
         + jnp.einsum('bhrqk,bhkd->bhrqd', p_ctx, vch))
    return o.transpose(0, 2, 3, 1, 4).reshape(b, n, NA_WIDTH)

def fourier_na_mixer(hl, hc, w_in, w_out, rpb, with_ctx_out):
    splits = [FOURIER_WIDTH, FOURIER_WIDTH + NA_WIDTH, FOURIER_WIDTH + 2 * NA_WIDTH]
    fl, ql, kl, vl = jnp.split(hl @ w_in, splits, axis=-1)
    fc, qc, kc, vc = jnp.split(hc @ w_in, splits, axis=-1)
    yl = jnp.concatenate([fourier_mix(fl), neighbourhood_attention(ql, kl, vl, kc, vc, rpb)], axis=-1) @ w_out
    if not with_ctx_out:
        return yl, None
    oc = dense_attention(to_heads(qc, NA_HEADS), to_heads(kc, NA_HEADS), to_heads(vc, NA_HEADS))
    oc = oc.transpose(0, 2, 1, 3).reshape(hc.shape[0], hc.shape[1], NA_WIDTH)
    yc = jnp.concatenate([fourier_mix(fc), oc], axis=-1) @ w_out
    return yl, yc

def axial_rope(t, rows, cols):
    half = t.shape[-1] // 2
    nf = half // 2
    inv_freq = ROPE_THETA ** (-jnp.arange(nf, dtype=jnp.float32) / nf)

    def rotate(u, pos):
        ang = pos.astype(jnp.float32)[:, None] * inv_freq
        cos = jnp.cos(ang)[:, None, None, :]
        sin = jnp.sin(ang)[:, None, None, :]
        u = u.astype(jnp.float32)
        u1, u2 = u[..., :nf], u[..., nf:]
        return jnp.concatenate([u1 * cos - u2 * sin, u1 * sin + u2 * cos], axis=-1)

    out = jnp.concatenate([rotate(t[..., :half], rows), rotate(t[..., half:], cols)], axis=-1)
    return out.astype(t.dtype)

def diff_attn_core(q, k, v, lam):
    s = jnp.einsum('bhiqd,bhikd->bhiqk', q, k).astype(jnp.float32) * (q.shape[-1] ** -0.5)
    p = jax.nn.softmax(s, axis=-1)
    a = (p[:, :, 0] - lam * p[:, :, 1]).astype(v.dtype)
    return jnp.einsum('bhqk,bhkd->bhqd', a, v)

def diff_attention_mixer(hl, hc, w_qkv, w_out, lq1, lk1, lq2, lk2, subln_g, lam_init, rows, cols, with_ctx_out):
    h, d, dv = DIFF_HEADS, DIFF_HEAD_DIM, DIFF_V_DIM

    def project(x_):
        b_, l_, _ = x_.shape
        q, k, v = jnp.split(x_ @ w_qkv, [DIFF_QK_WIDTH, 2 * DIFF_QK_WIDTH], axis=-1)
        return q.reshape(b_, l_, h, 2, d), k.reshape(b_, l_, h, 2, d), v.reshape(b_, l_, h, dv)

    ql, kl, vl = project(hl)
    qc, kc, vc = project(hc)
    ql, kl = axial_rope(ql, rows, cols), axial_rope(kl, rows, cols)
    lam = (jnp.exp(jnp.sum((lq1 * lk1).astype(jnp.float32)))
           - jnp.exp(jnp.sum((lq2 * lk2).astype(jnp.float32))) + lam_init)

    kc_h = kc.transpose(0, 2, 3, 1, 4)
    vc_h = vc.transpose(0, 2, 1, 3)
    k_all = jnp.concatenate([kc_h, kl.transpose(0, 2, 3, 1, 4)], axis=3)
    v_all = jnp.concatenate([vc_h, vl.transpose(0, 2, 1, 3)], axis=2)

    b, n = hl.shape[0], hl.shape[1]
    nb = n // Q_BLOCK
    q_blocks = ql.reshape(b, nb, Q_BLOCK, h, 2, d).transpose(1, 0, 3, 4, 2, 5)
    ol = lax.map(lambda qb: diff_attn_core(qb, k_all, v_all, lam), q_blocks)
    ol = ol.transpose(1, 0, 3, 2, 4).reshape(b, n, h, dv)

    def head_out(o):
        o = rms_norm(o, subln_g, SUBLN_EPS) * (1.0 - lam_init)
        return o.reshape(o.shape[0], o.shape[1], DIFF_V_WIDTH) @ w_out

    yl = head_out(ol)
    if not with_ctx_out:
        return yl, None
    oc = diff_attn_core(qc.transpose(0, 2, 3, 1, 4), kc_h, vc_h, lam).transpose(0, 2, 1, 3)
    return yl, head_out(oc)

def setup_inputs(seed: int = 0) -> dict:
    key = jax.random.key(seed)
    ks = jax.random.split(key, 22)
    D = D_MODEL

    def nrm(k, shape, scale):
        return jax.random.normal(k, shape, jnp.float32) * scale

    return {
        'x': nrm(ks[0], (BATCH, SEQ, D), 1.0),
        'c': nrm(ks[1], (BATCH, D), 1.0),
        'ctx': nrm(ks[2], (BATCH, CTX_LEN, D), 1.0),
        'c_ctx': nrm(ks[3], (D,), 1.0),
        'w_mod': nrm(ks[4], (DEPTH, D, 6 * D), 0.5 * D ** -0.5),
        'b_mod': nrm(ks[5], (DEPTH, 6 * D), 0.02),
        'norm_mix_g': 1.0 + nrm(ks[6], (DEPTH, D), 0.02),
        'norm_mlp_g': 1.0 + nrm(ks[7], (DEPTH, D), 0.02),
        'w_mlp_in': nrm(ks[8], (DEPTH, D, MLP_HIDDEN), D ** -0.5),
        'w_mlp_out': nrm(ks[9], (DEPTH, MLP_HIDDEN, D), MLP_HIDDEN ** -0.5),
        'w_in_ab': nrm(ks[10], (N_EVEN, D, AB_IN), D ** -0.5),
        'w_out_ab': nrm(ks[11], (N_EVEN, AB_OUT, D), AB_OUT ** -0.5),
        'na_rpb': nrm(ks[12], (N_EVEN, NA_HEADS, 2 * NA_KH_MAX - 1, 2 * NA_KW - 1), 0.1),
        'w_qkv_diff': nrm(ks[13], (N_ODD, D, 2 * DIFF_QK_WIDTH + DIFF_V_WIDTH), D ** -0.5),
        'w_out_diff': nrm(ks[14], (N_ODD, DIFF_V_WIDTH, D), DIFF_V_WIDTH ** -0.5),
        'diff_lq1': nrm(ks[15], (N_ODD, DIFF_HEAD_DIM), 0.1),
        'diff_lk1': nrm(ks[16], (N_ODD, DIFF_HEAD_DIM), 0.1),
        'diff_lq2': nrm(ks[17], (N_ODD, DIFF_HEAD_DIM), 0.1),
        'diff_lk2': nrm(ks[18], (N_ODD, DIFF_HEAD_DIM), 0.1),
        'diff_subln_g': 1.0 + nrm(ks[19], (N_ODD, DIFF_V_DIM), 0.02),
        'final_norm_g': 1.0 + nrm(ks[20], (D,), 0.02),
    }

def reference(x, c, ctx, c_ctx, w_mod, b_mod, norm_mix_g, norm_mlp_g, w_mlp_in, w_mlp_out,
              w_in_ab, w_out_ab, na_rpb, w_qkv_diff, w_out_diff, diff_lq1, diff_lk1, diff_lq2, diff_lk2,
              diff_subln_g, final_norm_g):
    n = x.shape[1]
    t = jnp.arange(n)
    rows, cols = t // GRID_W, t % GRID_W
    c_act = jax.nn.silu(c)
    cc_act = jax.nn.silu(c_ctx)
    xl, xc = x, ctx
    for i in range(DEPTH):
        last = i == DEPTH - 1
        ml = jnp.split((c_act @ w_mod[i] + b_mod[i])[:, None, :], 6, axis=-1)
        mc = jnp.split(cc_act @ w_mod[i] + b_mod[i], 6, axis=-1)
        hl = modulate(xl, norm_mix_g[i], ml[0], ml[1])
        hc = modulate(xc, norm_mix_g[i], mc[0], mc[1])
        j = i // 2
        if i % 2 == 0:
            yl, yc = fourier_na_mixer(hl, hc, w_in_ab[j], w_out_ab[j], na_rpb[j], not last)
        else:
            lam_init = 0.8 - 0.6 * math.exp(-0.3 * i)
            yl, yc = diff_attention_mixer(hl, hc, w_qkv_diff[j], w_out_diff[j], diff_lq1[j], diff_lk1[j],
                                          diff_lq2[j], diff_lk2[j], diff_subln_g[j], lam_init,
                                          rows, cols, not last)
        xl = xl + ml[2] * yl
        xl = xl + ml[5] * squared_relu_mlp(modulate(xl, norm_mlp_g[i], ml[3], ml[4]), w_mlp_in[i], w_mlp_out[i])
        if not last:
            xc = xc + mc[2] * yc
            xc = xc + mc[5] * squared_relu_mlp(modulate(xc, norm_mlp_g[i], mc[3], mc[4]), w_mlp_in[i], w_mlp_out[i])
    return rms_norm(xl, final_norm_g)


_drawn_inputs = setup_inputs


def setup_inputs(seed=0):
    import zlib

    import numpy as np

    out = dict(_drawn_inputs(seed))
    spreads = {}
    factors = {'norm_mix_g': 8.0,
     'norm_mlp_g': 4.524,
     'na_rpb': 8.0,
     'diff_lq1': 6.785,
     'diff_lk1': 8.0,
     'diff_lq2': 7.208,
     'diff_lk2': 200.0,
     'diff_subln_g': 200.0,
     'final_norm_g': 25.963}
    for name, (base, spread) in spreads.items():
        noise = np.random.default_rng([zlib.crc32(name.encode()), seed]).standard_normal(out[name].shape)
        drawn = base * np.exp(spread * noise) if base else spread * noise
        out[name] = jnp.asarray(drawn.astype(out[name].dtype))
    for name, factor in factors.items():
        out[name] = (out[name] * factor).astype(out[name].dtype)
    return out
```

```python
from contextlib import ExitStack, contextmanager

import numpy as np

import concourse.bass as bass
from concourse import mybir

F32 = mybir.dt.float32
F32R = mybir.dt.float32r
ALU = mybir.AluOpType
ACT = mybir.ActivationFunctionType
AX = mybir.AxisListType

P = 128
D = 1024
KT = D // P
LAT, CTX = 512, 256
TOK = LAT + CTX
NT = TOK // P
ROWS, COLS = 8, 64
HEADS, HD = 8, 64
HID_BLOCKS = 4
EPS, SUB_EPS = 1e-6, 1e-5
LAM_INIT = 0.8 - 0.6 * float(np.exp(-0.3))
NEG = -1e30

STAGES = [("f", 4), ("q0", 4), ("k0", 4), ("dft", 5), ("v0", 4), ("out0", 8), ("mlp0", 64),
          ("q1", 8), ("k1", 8), ("v1", 8), ("out1", 8), ("mlp1", 64)]
FIRST, UNITS = {}, 0
for _name, _n in STAGES:
    FIRST[_name] = UNITS
    UNITS += _n
SLOTS = 4
AHEAD = 3

WINDOW = [0, 64, 192, 256]
VARIANT = [0, 1, 1, 2]
MOD_AT = [range(0, 3), range(3, 6), range(6, 8), ()]
PROBS = 3


class Steps:

    def __init__(self, eng, sem):
        self.eng, self.sem, self.n = eng, sem, 0

    def wait(self, ins):
        ins.then_inc(self.sem, 1)
        self.n = self.n + 1
        self.eng.wait_ge(self.sem, self.n)

    @contextmanager
    def loop(self, count, per):
        base = self.n
        with self.eng.Fori(0, count) as i:
            self.n = base + i * per
            yield i
        self.n = base + count * per


def build(nc, t):
    ctx = ExitStack()
    with ctx:
        base = 16512

        def at(name, shape, dt, offset):
            return nc.alloc_sbuf_tensor_at(name, shape, dt, offset=offset)

        size = lambda *shape: int(np.prod(shape)) * 4
        x_at = base
        a_at = x_at + size(TOK, KT)
        raw_at = a_at + 2 * size(TOK, KT)
        whi_at = raw_at + size(SLOTS, 1024)
        wlo_at = whi_at + size(SLOTS, 1024)
        con_at = wlo_at + size(SLOTS, 1024)
        rest = con_at + 5632
        mod_at = 229344 - size(4, 512)
        scr = rest + 2 * size(TOK, KT)

        xl = at("xl", [P, KT, LAT], F32, x_at)
        xc = at("xc", [P, KT, CTX], F32, x_at + size(KT, LAT))
        h_hi = at("h_hi", [P, KT, TOK], F32R, a_at)
        h_lo = at("h_lo", [P, KT, TOK], F32R, a_at + size(KT, TOK))
        raw = at("raw", [P, SLOTS, 1024], F32, raw_at)
        w_hi = at("w_hi", [P, SLOTS, 1024], F32R, whi_at)
        w_lo = at("w_lo", [P, SLOTS, 1024], F32R, wlo_at)

        c_off = [con_at]

        def const(name, shape, dt=F32):
            o = c_off[0]
            c_off[0] += (size(*shape[1:]) + 31) // 32 * 32
            assert c_off[0] <= rest
            return at(name, shape, dt, o)

        ident = const("ident", [P, P])
        ones = const("ones", [P, P])
        mods = const("mods", [P, 24, 2, 4])
        b_mod = const("b_mod_sb", [P, 24, 4])
        gains = const("gains", [P, 5, KT])
        gs = const("gs", [P, 4, 2, KT])
        cond = const("cond", [P, KT, 2])
        cact = const("cact", [P, KT, 2])
        ctmp = const("ctmp", [P, KT, 2])
        eps_c = const("eps_c", [P, 2])
        stat = const("stat", [P, 64])
        modr = const("modr", [P, 2, 4])
        dft_hi = const("dft_hi", [P, 256], F32R)
        dft_lo = const("dft_lo", [P, 256], F32R)
        lam_in = const("lam_in", [HD, 4])
        lam_t = const("lam_t", [P, 8])
        subg = const("subg", [P, 2])

        mod_ring = at("mod_ring", [P, 2, 512], F32, mod_at)
        mod_acc = at("mod_acc", [P, 2, 512], F32, mod_at + size(2, 512))

        big = at("mod_big", [P, 3, KT, 512], F32, rest)
        hid_hi = at("hid_hi", [P, KT, TOK], F32R, rest)
        hid_lo = at("hid_lo", [P, KT, TOK], F32R, rest + size(KT, TOK))
        tmp_a = at("tmp_a", [P, 2, TOK], F32, scr)
        tmp_b = at("tmp_b", [P, 2, TOK], F32, scr + size(2, TOK))
        ssum = at("ssum", [P, TOK], F32, scr + size(4, TOK))
        rstd = at("rstd", [P, TOK], F32, scr + size(5, TOK))
        assert scr + size(6, TOK) <= mod_at

        q0 = at("q0", [P, 4, TOK], F32, x_at)
        k0 = at("k0", [P, 4, TOK], F32, x_at + size(4, TOK))
        f_hi = at("f_hi", [P, 4, TOK], F32R, rest)
        f_lo = at("f_lo", [P, 4, TOK], F32R, rest + size(4, TOK))
        y_hi, y_lo = f_hi, f_lo
        u_at = rest + 2 * size(4, TOK)
        u_hi = at("u_hi", [P, NT, 4, 256], F32R, u_at)
        u_lo = at("u_lo", [P, NT, 4, 256], F32R, u_at + size(NT, 4, 256))
        dft_raw = at("dft_raw", [P, 256], F32, u_at)
        assert u_at + 2 * size(NT, 4, 256) <= mod_at
        v0 = at("v0", [P, NT, HEADS, P], F32R, u_at)
        v0s = at("v0s", [P, 3, HEADS, P], F32R, u_at + size(NT, 1024))
        pr_at = u_at + size(NT + 3, 1024)
        prob0 = at("prob0", [P, PROBS, 512], F32, pr_at)
        pt0 = at("pt0", [P, 2, 4, 256], F32R, pr_at + size(PROBS, 512))
        osum = at("osum", [P, 2, TOK], F32, pr_at + size(PROBS, 512) + size(2, 1024))
        assert pr_at + size(PROBS, 512) + size(2, 1024) + size(2, TOK) <= 229360
        o0_hi = at("o0_hi", [P, 4, TOK], F32R, a_at)
        o0_lo = at("o0_lo", [P, 4, TOK], F32R, a_at + size(4, TOK))
        j_at = a_at + size(8, TOK)
        q2a = at("q2a", [P, 2, TOK], F32R, j_at)
        q2b = at("q2b", [P, 2, TOK], F32R, j_at + size(2, TOK))
        k2 = at("k2", [P, 2, TOK], F32R, j_at + size(4, TOK))
        bias = at("bias", [P, 2, 3, 256], F32, j_at + size(6, TOK))
        assert size(8, TOK) + size(6, TOK) + size(2, 768) <= size(16, TOK)
        mask = at("mask", [P, 3, 32], F32, c_off[0]) if c_off[0] + size(96) <= rest else None
        assert mask is not None

        q1 = at("q1", [P, HEADS, LAT], F32, rest)
        k1 = at("k1", [P, HEADS, TOK], F32, rest + size(HEADS, LAT))
        v1 = at("v1", [P, NT, D], F32, rest + size(HEADS, LAT + TOK))
        cs_at = rest + size(HEADS, LAT + TOK) + size(NT, D)
        cosb = at("cosb", [P, LAT], F32, cs_at)
        sinb = at("sinb", [P, LAT], F32, cs_at + size(LAT))
        rt = at("rt", [P, 3, LAT], F32, cs_at + size(2, LAT))
        assert cs_at + size(5, LAT) <= mod_at
        o_raw = at("o_raw", [P, HEADS, LAT], F32, a_at)
        b_at = a_at + size(HEADS, LAT)
        aq2a = at("aq2a", [P, 2, LAT], F32R, b_at)
        aq2b = at("aq2b", [P, 2, LAT], F32R, b_at + size(2, LAT))
        ak2 = at("ak2", [P, 2, TOK], F32R, b_at + size(4, LAT))
        avh = at("avh", [P, NT, P], F32R, b_at + size(4, LAT) + size(2, TOK))
        avl = at("avl", [P, NT, P], F32R, b_at + size(4, LAT) + size(3, TOK))
        aprob = at("aprob", [P, 2, 2, TOK], F32, cs_at)
        c_at = b_at + size(4, LAT) + size(4, TOK)
        at_hi = at("at_hi", [P, NT, 256], F32R, c_at)
        assert c_at + size(NT, 256) <= raw_at
        at_lo = at("at_lo", [P, NT, 256], F32R, x_at + size(KT, LAT))
        assert cs_at + size(4, TOK) <= 229360
        o1_hi = at("o1_hi", [P, HEADS, LAT], F32R, rest)
        o1_lo = at("o1_lo", [P, HEADS, LAT], F32R, rest + size(HEADS, LAT))
        sub_r = at("sub_r", [P, 2, LAT], F32, rest + size(2, HEADS, LAT))
        osq = at("osq", [P, 2, LAT], F32, rest + size(2, HEADS, LAT) + size(2, LAT))
        oneh = at("oneh", [P, HEADS, HEADS], F32, rest + size(2, HEADS, LAT) + size(4, LAT))
        selh = at("selh", [HEADS, HEADS, P], F32, rest + size(2, HEADS, LAT) + size(5, LAT))

        ps = ctx.enter_context(nc.psum_tensor("ps", [P, 8, 512], F32))

        def sem(name):
            return ctx.enter_context(nc.semaphore(name))

        consts_in = sem("consts_in")
        x_in = sem("x_in")
        xr_in = sem("xr_in")
        table_in = sem("table_in")
        shift_in = sem("shift_in")
        oneh_in = sem("oneh_in")
        hi_made = sem("hi_made")
        lo_made = sem("lo_made")
        unit_done = sem("unit_done")
        mod_used = sem("mod_used")
        mod_summed = sem("mod_summed")
        mod_rows = sem("mod_rows")
        mod_done = sem("mod_done")
        exp_c = sem("exp_c")
        ones_ok = sem("ones_ok")
        lam_mm = sem("lam_mm")
        lam_exp = sem("lam_exp")
        lam_ok = sem("lam_ok")
        relu_made = sem("relu_made")
        relu_used = sem("relu_used")
        hid_made = sem("hid_made")
        x_added = sem("x_added")
        sq_made = sem("sq_made")
        sq_summed = sem("sq_summed")
        norm_sum = sem("norm_sum")
        norm_sqrt = sem("norm_sqrt")
        t_made = sem("t_made")
        aff_made = sem("aff_made")
        hh_made = sem("hh_made")
        h_made = sem("h_made")
        out_made = sem("out_made")
        dsteps = sem("dsteps")
        f_hi_s = sem("f_hi_s")
        f_out = sem("f_out")
        qk_out = sem("qk_out")
        dft_hi_s = sem("dft_hi_s")
        dft_lo_s = sem("dft_lo_s")
        u_mm = sem("u_mm")
        u_hi_s = sem("u_hi_s")
        u_lo_s = sem("u_lo_s")
        y_hi_s = sem("y_hi_s")
        y_lo_s = sem("y_lo_s")
        v0_hi_s = sem("v0_hi_s")
        v0_lo_s = sem("v0_lo_s")
        bias_ok = sem("bias_ok")
        jh = sem("jh")
        jl = sem("jl")
        jk = sem("jk")
        js = sem("js")
        s_made = sem("s_made")
        m_made = sem("m_made")
        e_made = sem("e_made")
        p_made = sem("p_made")
        tr_made = sem("tr_made")
        th_made = sem("th_made")
        tl_made = sem("tl_made")
        pv_made = sem("pv_made")
        oc_made = sem("oc_made")
        od_made = sem("od_made")
        ol_made = sem("ol_made")
        rope_read = sem("rope_read")
        rope_done = sem("rope_done")
        kc_out = sem("kc_out")
        v1_out = sem("v1_out")
        jh1 = sem("jh1")
        jl1 = sem("jl1")
        jk1 = sem("jk1")
        js1 = sem("js1")
        vh1 = sem("vh1")
        vl1 = sem("vl1")
        s1 = sem("s1")
        m1 = sem("m1")
        e1 = sem("e1")
        c1 = sem("c1")
        g1 = sem("g1")
        a1 = sem("a1")
        tr1 = sem("tr1")
        th1 = sem("th1")
        tl1 = sem("tl1")
        pv1 = sem("pv1")
        o1 = sem("o1")
        sub_sq = sem("sub_sq")
        sub_mm = sem("sub_mm")
        sub_sqrt = sem("sub_sqrt")
        sub_rec = sem("sub_rec")
        sub_bc = sem("sub_bc")
        sub_t = sem("sub_t")
        sub_hi = sem("sub_hi")
        sub_lo = sem("sub_lo")
        big_in = [sem(f"big_in{i}") for i in range(3)]
        raw_in = [sem(f"raw_in{i}") for i in range(SLOTS)]
        mod_in = [sem(f"mod_in{i}") for i in range(2)]
        bias_in = [sem(f"bias_in{i}") for i in range(2)]
        out_sem = [sem(f"out_sem{i}") for i in range(2)]

        pv_ps = ps[:, 5:8].rearrange("p b (t c) -> p (b t) c", c=256)

        def ps2(b):
            return ps[:, b:b + 2].rearrange("p a b -> p (a b)")[:, 0:TOK]

        def gate(layer, chunk, v, k):
            m = 12 * layer + 2 * chunk + k // 4
            return mods[:, m, v, k % 4:k % 4 + 1]

        def xa(layer, b, i):
            return 40 * layer + 8 + 8 * b + i

        def ha(layer, b, i):
            return 32 * layer + 8 * b + i

        both = ((0, 0, LAT), (1, LAT, CTX))
        V_BANK = [0, 1, 2, 3, 6, 7]
        NORM_TOK = [TOK, TOK, TOK, LAT, LAT]
        PAIRS = LAT // 256

        def parts(n):
            return [(xl, 0, slice(0, LAT))] + ([(xc, 1, slice(LAT, TOK))] if n == TOK else [])

        block = ctx.enter_context(nc.Block())

        @block.sync
        def _(sp):
            for dst, name in ((cond, "cond"), (ident, "ident"), (b_mod, "b_mod"), (gains, "gains"),
                              (mask, "mask"), (lam_in, "lam"), (subg, "subln")):
                sp.dma_start(dst[:], t[name]).then_inc(consts_in, 16)
            for m in range(4):
                if m == 3:
                    sp.wait_ge(mod_summed, 1)
                sp.dma_start(big[:, m % 3], t["w_mod"][m]).then_inc(big_in[m % 3], 16)
                if m == 0:
                    sp.dma_start(xl[:], t["x"]).then_inc(x_in, 16)
                    sp.dma_start(xc[:], t["ctx"]).then_inc(x_in, 16)

            def load_unit(u, s, first=False):
                if not first:
                    sp.wait_ge(lo_made, u - (SLOTS - 1))
                src = t["units"][bass.ds(u, 1)].rearrange("o p n -> p (o n)")
                sp.dma_start(raw[:, s], src).then_inc(raw_in[s], 16)

            def load_mod(m, k, n, wait=True):
                if wait:
                    sp.wait_ge(mod_used, n - 1)
                src = t["w_mod"][bass.ds(m, 1), :, k, :].rearrange("o p n -> p (o n)")
                sp.dma_start(mod_ring[:, k % 2], src).then_inc(mod_in[k % 2], 16)

            for u in range(SLOTS):
                load_unit(u, u, True)
            sp.wait_ge(h_made, KT)
            sp.dma_start(dft_raw[:], t["dft128"]).then_inc(table_in, 16)
            n = 0
            for u in range(FIRST["out0"]):
                load_unit(u + SLOTS, u % SLOTS)
                if u < FIRST["dft"] or u >= FIRST["v0"]:
                    m = 4 + n // KT
                    for k in (range(6) if n % KT == 0 else range(6, 8)):
                        load_mod(m, k, n, n >= 2)
                        n += 1
            assert n == 8 * KT
            for h in range(HEADS):
                if h == 0:
                    sp.wait_ge(unit_done, FIRST["out0"])
                if h == 1:
                    sp.wait_ge(v0_lo_s, NT)
                    for j in range(3):
                        sp.dma_start(v0s[0:64, j].bitcast(F32), v0[64:128, j].bitcast(F32)).then_inc(shift_in, 16)
                        sp.dma_start(v0s[64:128, j].bitcast(F32), v0[0:64, j + 1].bitcast(F32)).then_inc(shift_in, 16)
                if h >= 2:
                    sp.wait_ge(m_made, 6 * (h - 1))
                sp.dma_start(bias[:, h % 2], t["bias"][h]).then_inc(bias_in[h % 2], 16)
            sp.wait_ge(jk, HEADS)
            sp.wait_ge(jl, HEADS)
            sp.dma_start(xl[:], t["x"]).then_inc(xr_in, 16)
            sp.dma_start(xc[:], t["ctx"]).then_inc(xr_in, 16)
            for u in range(FIRST["out0"], FIRST["mlp0"]):
                load_unit(u + SLOTS, u % SLOTS)

            def mlp_loads(layer, b, mod):
                for i in range(16):
                    u = FIRST[f"mlp{layer}"] + i
                    load_unit(u + SLOTS + 16 * b, u % SLOTS)
                    for k in (MOD_AT[i % 4] if mod else ()):
                        load_mod(12 + 4 * b + i // 4, k, 8 * (8 + 4 * b + i // 4) + k)

            with sp.Fori(0, HID_BLOCKS - 1) as b:
                mlp_loads(0, b, True)
            mlp_loads(0, HID_BLOCKS - 1, False)
            sp.wait_ge(h_made, 3 * KT)
            sp.dma_start(cosb[:], t["cos"]).then_inc(table_in, 16)
            sp.dma_start(sinb[:], t["sin"]).then_inc(table_in, 16)
            for u in range(FIRST["q1"], FIRST["out1"]):
                load_unit(u + SLOTS, u % SLOTS)
            sp.wait_ge(o1, HEADS * PAIRS)
            sp.dma_start(oneh[:], t["oneh"]).then_inc(oneh_in, 16)
            sp.dma_start(selh[:], t["selh"]).then_inc(oneh_in, 16)
            for u in range(FIRST["out1"], FIRST["mlp1"]):
                load_unit(u + SLOTS, u % SLOTS)
            with sp.Fori(0, HID_BLOCKS - 1) as b:
                mlp_loads(1, b, False)
            for i in range(16 - SLOTS):
                u = FIRST["mlp1"] + i
                load_unit(u + SLOTS + 48, u % SLOTS)
            for k in range(KT):
                sp.wait_ge(out_made, k + 1)
                sp.dma_start(t["out"][:, k], tmp_b[:, k % 2, 0:LAT]).then_inc(out_sem[k % 2], 16)
            for s in out_sem:
                sp.wait_ge(s, 16 * KT // 2)

        @block.gpsimd
        def _(pool):
            def low(u, s):
                pool.wait_ge(hi_made, u + 1)
                nc.gpsimd.tensor_tensor(w_lo[:, s], raw[:, s], w_hi[:, s].bitcast(F32),
                                        op=ALU.subtract).then_inc(lo_made, 1)

            def lows(first, last):
                for u in range(first + AHEAD, last + AHEAD):
                    low(u, u % SLOTS)

            def norm(i):
                for k in range(KT):
                    pool.wait_ge(hh_made, KT * i + k + 1)
                    nc.gpsimd.tensor_tensor(h_lo[:, k, 0:NORM_TOK[i]], tmp_b[:, k % 2, 0:NORM_TOK[i]],
                                            h_hi[:, k, 0:NORM_TOK[i]].bitcast(F32),
                                            op=ALU.subtract).then_inc(h_made, 1)

            def mlp(layer):
                with pool.Fori(0, HID_BLOCKS - 1) as b:
                    for i in range(16):
                        u = FIRST[f"mlp{layer}"] + AHEAD + i
                        low(u + 16 * b, u % SLOTS)
                for i in range(16 if layer == 0 else 16 - AHEAD):
                    u = FIRST[f"mlp{layer}"] + AHEAD + i
                    low(u + 48, u % SLOTS)

            for u in range(AHEAD):
                low(u, u)
            norm(0)
            lows(FIRST["f"], FIRST["out0"])
            for h in range(HEADS):
                e = 64 * (h % 2)
                pool.wait_ge(bias_in[h % 2], 16 * (h // 2 + 1))
                bv = bias[:, h % 2].rearrange("p v (c r) -> p v c r", r=ROWS)
                for v in range(3):
                    ins = nc.gpsimd.tensor_tensor(bv[:, v], bv[:, v],
                                                  mask[:, v].unsqueeze(2).broadcast_to([P, 32, ROWS]), op=ALU.add)
                ins.then_inc(bias_ok, 1)
                pool.wait_ge(bias_ok, h + 1)
                pool.wait_ge(jh, h + 1)
                nc.gpsimd.tensor_tensor(q2b[e:e + 64, h % 2], q0[e:e + 64, h // 2],
                                        q2a[e:e + 64, h % 2].bitcast(F32), op=ALU.subtract).then_inc(jl, 1)
                pool.wait_ge(jl, h + 1)
            lows(FIRST["out0"], FIRST["mlp0"])
            norm(1)
            mlp(0)
            norm(2)
            lows(FIRST["q1"], FIRST["out1"])
            pool.wait_ge(lo_made, FIRST["out1"] + AHEAD)
            for h in range(HEADS):
                for i in range(2):
                    e = 64 * i
                    if i == 0 and h:
                        pool.wait_ge(vl1, h)
                    pool.wait_ge(jh1, 2 * h + i + 1)
                    nc.gpsimd.tensor_tensor(aq2b[e:e + 64, i], q1[e:e + 64, h],
                                            aq2a[e:e + 64, i].bitcast(F32), op=ALU.subtract).then_inc(jl1, 1)
                    pool.wait_ge(jl1, 2 * h + i + 1)
                pool.wait_ge(vh1, h + 1)
                nc.gpsimd.tensor_tensor(avl[:], v1[:, :, P * h:P * h + P], avh[:].bitcast(F32),
                                        op=ALU.subtract).then_inc(vl1, 1)
            lows(FIRST["out1"], FIRST["mlp1"])
            norm(3)
            mlp(1)

        @block.scalar
        def _(act):
            def high(u, s, n):
                act.wait_ge(raw_in[s], n)
                if isinstance(u, int) and u < SLOTS:
                    pass
                else:
                    act.wait_ge(unit_done, u - (SLOTS - 1))
                nc.scalar.activation(w_hi[:, s], raw[:, s], ACT.Copy).then_inc(hi_made, 1)

            def high_u(u):
                high(u, u % SLOTS, 16 * (u // SLOTS + 1))

            def high_b(u, b):
                high(u + 16 * b, u % SLOTS, 64 * b + 16 * (u // SLOTS + 1))

            def squares(i, m):
                n = KT * i + m
                if n >= 2:
                    act.wait_ge(sq_summed, n - 1)
                for x, _, cols in parts(NORM_TOK[i]):
                    ins = nc.scalar.activation(tmp_b[:, m % 2, cols], x[:, m], ACT.Square)
                ins.then_inc(sq_made, 1)

            def norm(i):
                n = NORM_TOK[i]
                act.wait_ge(norm_sum, i + 1)
                nc.scalar.activation(rstd[:, 0:n], ps[:, 6:8].rearrange("p a b -> p (a b)")[:, 0:n],
                                     ACT.Sqrt, bias=eps_c[:, 0:1], scale=1.0 / D).then_inc(norm_sqrt, 1)
                for k in range(KT):
                    act.wait_ge(t_made, KT * i + k + 1)
                    if i == 4:
                        if k >= 2:
                            act.wait_ge(out_sem[k % 2], 16 * (k // 2))
                        nc.scalar.activation(tmp_b[:, k % 2, 0:n], tmp_a[:, k % 2, 0:n], ACT.Copy,
                                             scale=gains[:, 4, k:k + 1]).then_inc(out_made, 1)
                        continue
                    if k >= 2:
                        act.wait_ge(h_made, KT * i + k - 1)
                    for _, v, cols in parts(n):
                        ins = nc.scalar.activation(tmp_b[:, k % 2, cols], tmp_a[:, k % 2, cols], ACT.Identity,
                                                   scale=gs[:, i, v, k:k + 1],
                                                   bias=gate(i // 2, 3 * (i % 2), v, k))
                    ins.then_inc(aff_made, 1)

            def mlp(layer):
                u0 = FIRST[f"mlp{layer}"]

                def blk(b, last):
                    for i in range(16):
                        u = u0 + i
                        if not (last and layer == 1 and i + AHEAD >= 16):
                            high_b(u + AHEAD, b)
                        if i < 8:
                            act.wait_ge(unit_done, u + 16 * b + 1)
                            a = ha(layer, b, i)
                            if i >= 2:
                                act.wait_ge(relu_used, a - 1)
                            for bank, c0, n in both[:2 - layer]:
                                ins = nc.scalar.activation(tmp_a[:, i % 2, c0:c0 + n],
                                                           ps[:, 2 * (u % 2) + bank, 0:n], ACT.Relu)
                            ins.then_inc(relu_made, 1)
                        elif last:
                            act.wait_ge(x_added, xa(layer, b, i - 8) + 1)
                            squares(2 + 2 * layer, i - 8)

                with act.Fori(0, HID_BLOCKS - 1) as b:
                    blk(b, False)
                blk(HID_BLOCKS - 1, True)

            act.wait_ge(consts_in, 16 * 7)
            nc.scalar.activation(ctmp[:], cond[:], ACT.Exp, scale=-1.0).then_inc(exp_c, 1)
            act.wait_ge(lam_mm, 1)
            nc.scalar.activation(lam_t[:, 2:4], ps[:, 6, 0:2], ACT.Exp).then_inc(lam_exp, 1)
            for u in range(AHEAD):
                high_u(u)
            act.wait_ge(x_in, 32)
            for m in range(KT):
                squares(0, m)
            norm(0)
            for i in range(4):
                u = FIRST["f"] + i
                high_u(u + AHEAD)
                act.wait_ge(unit_done, u + 1)
                for bank, c0, n in both:
                    ins = nc.scalar.activation(f_hi[:, i, c0:c0 + n], ps[:, 2 * (u % 2) + bank, 0:n], ACT.Copy)
                ins.then_inc(f_hi_s, 1)
            for name, dst, scale in (("q0", q0, -1.0 / 8), ("k0", k0, 1.0)):
                for i in range(4):
                    u = FIRST[name] + i
                    high_u(u + AHEAD)
                    act.wait_ge(unit_done, u + 1)
                    for bank, c0, n in both:
                        ins = nc.scalar.activation(dst[:, i, c0:c0 + n], ps[:, 2 * (u % 2) + bank, 0:n],
                                                   ACT.Copy, scale=scale)
                    ins.then_inc(qk_out, 1)
            act.wait_ge(table_in, 16)
            nc.scalar.activation(dft_hi[:], dft_raw[:], ACT.Copy).then_inc(dft_hi_s, 1)
            act.wait_ge(dft_lo_s, 1)
            for n in range(2 * NT):
                act.wait_ge(u_mm, n + 1)
                nc.scalar.activation(u_hi[:, n // 2, 2 * (n % 2):2 * (n % 2) + 2].rearrange("p g c -> p (g c)"),
                                     ps[:, V_BANK[n % 6]], ACT.Copy).then_inc(u_hi_s, 1)
            for i in range(5):
                high_u(FIRST["dft"] + i + AHEAD)
            for g in range(4):
                act.wait_ge(unit_done, FIRST["dft"] + 4)
                nc.scalar.activation(y_hi[:, g, 0:LAT], ps[:, g], ACT.Copy).then_inc(y_hi_s, 1)
            for g in range(2):
                act.wait_ge(unit_done, FIRST["dft"] + 5)
                nc.scalar.activation(y_hi[:, 2 * g:2 * g + 2, LAT:TOK],
                                     ps[:, 6 + g].rearrange("p (g c) -> p g c", g=2), ACT.Copy).then_inc(y_hi_s, 1)
            for i in range(4):
                high_u(FIRST["v0"] + i + AHEAD)
            act.wait_ge(unit_done, FIRST["v0"] + 4)
            for n in range(NT):
                nc.scalar.activation(v0[:, n, :, 0:HD], ps[:, V_BANK[n]].rearrange("p (h d) -> p h d", d=HD),
                                     ACT.Copy).then_inc(v0_hi_s, 1)

            def swaps(h):
                e, o = 64 * (h % 2), 64 - 64 * (h % 2)
                act.wait_ge(jl, h + 1)
                nc.scalar.activation(q2a[o:o + 64, h % 2], q2b[e:e + 64, h % 2].bitcast(F32), ACT.Copy)
                nc.scalar.activation(q2b[o:o + 64, h % 2], q2a[e:e + 64, h % 2].bitcast(F32),
                                     ACT.Copy).then_inc(js, 1)

            def p_high(n):
                c = 4 if n % NT < 4 else 2
                act.wait_ge(tr_made, n + 1)
                if n >= 2:
                    act.wait_ge(pv_made, n - 1)
                nc.scalar.activation(pt0[:, n % 2, 0:c, 0:P], ps[:, 3 + n % 2, 0:128 * c].rearrange("p (c q) -> p c q", c=c),
                                     ACT.Copy).then_inc(th_made, 1)

            def out_half(h):
                e = 64 * (h % 2)
                act.wait_ge(pv_made, 6 * h + 6)
                if h >= 2:
                    act.wait_ge(ol_made, h - 1)
                nc.scalar.activation(osum[e:e + 64, h % 2].rearrange("p (t q) -> p t q", q=P),
                                     pv_ps[64:128, :, 0:P], ACT.Copy).then_inc(oc_made, 1)

            swaps(0)
            N0 = 6 * HEADS
            for n in range(N0 + 3):
                if n < N0:
                    if n % 6 == 3 and n // 6 + 1 < HEADS:
                        swaps(n // 6 + 1)
                    act.wait_ge(m_made, n + 1)
                    if n >= PROBS:
                        act.wait_ge(tr_made, n - PROBS + 1)
                    w = 512 if n % NT < 4 else 256
                    nc.scalar.activation(prob0[:, n % PROBS, 0:w], ps[:, n % 3, 0:w], ACT.Exp, scale=-1.0,
                                         bias=stat[:, n % 4:n % 4 + 1],
                                         accum_out=stat[:, 4 + n % 4:5 + n % 4]).then_inc(e_made, 1)
                if 1 <= n <= N0:
                    p_high(n - 1)
                if n >= 3 and (n - 3) % 6 == 5:
                    out_half((n - 3) // 6)
            for i in range(8):
                u = FIRST["out0"] + i
                high_u(u + AHEAD)
                act.wait_ge(x_added, i + 1)
                squares(1, i)
            norm(1)
            mlp(0)
            norm(2)
            for i in range(16):
                u = FIRST["q1"] + i
                high_u(u + AHEAD)
                if i >= 8:
                    act.wait_ge(unit_done, u + 1)
                    nc.scalar.activation(k1[:, i - 8, LAT:TOK], ps[:, 2 * (u % 2) + 1, 0:CTX], ACT.Copy).then_inc(kc_out, 1)
            for j in range(2):
                for i in range(4):
                    high_u(FIRST["v1"] + 4 * j + i + AHEAD)
                act.wait_ge(unit_done, FIRST["v1"] + 4 * j + 4)
                if j == 0:
                    act.wait_ge(rope_done, 1)
                for n in range(NT):
                    nc.scalar.activation(v1[:, n, 512 * j:512 * j + 512], ps[:, V_BANK[n]], ACT.Copy).then_inc(v1_out, 1)

            def swaps1(h):
                for i in range(2):
                    e, o = 64 * i, 64 - 64 * i
                    act.wait_ge(jl1, 2 * h + i + 1)
                    nc.scalar.activation(aq2a[o:o + 64, i], aq2b[e:e + 64, i].bitcast(F32), ACT.Copy)
                    nc.scalar.activation(aq2b[o:o + 64, i], aq2a[e:e + 64, i].bitcast(F32), ACT.Copy).then_inc(js1, 1)

            def p_high1(n):
                act.wait_ge(tr1, n + 1)
                if n % 2 == 0 and n >= 2:
                    act.wait_ge(pv1, n // 2)
                for j in range(2):
                    ins = nc.scalar.activation(at_hi[:, 3 * j:3 * j + 3, P * (n % 2):P * (n % 2) + P],
                                               ps[:, 4 + j, 0:384].rearrange("p (c q) -> p c q", c=3), ACT.Copy)
                ins.then_inc(th1, 1)

            def out_copy(m):
                act.wait_ge(pv1, m + 1)
                nc.scalar.activation(o_raw[:, m // 2, 256 * (m % 2):256 * (m % 2) + 256], ps[:, 6 + m % 2, 0:256],
                                     ACT.Copy).then_inc(o1, 1)

            swaps1(0)
            N1 = 4 * HEADS
            for n in range(N1 + 2):
                if n < N1:
                    if n % 4 == 0 and n > 0:
                        swaps1(n // 4)
                    for i in range(2):
                        act.wait_ge(m1, 2 * n + i + 1)
                        if n >= 2:
                            act.wait_ge(tr1, n - 1)
                        st = 16 + 4 * (n % 2) + i
                        nc.scalar.activation(aprob[:, n % 2, i], ps2(2 * ((2 * n + i) % 2)), ACT.Exp, scale=-1.0,
                                             bias=stat[:, st:st + 1], accum_out=stat[:, st + 2:st + 3]).then_inc(e1, 1)
                    act.wait_ge(c1, n + 1)
                    nc.scalar.activation(aprob[:, n % 2, 1], aprob[:, n % 2, 1], ACT.Copy,
                                         scale=stat[:, 28 + 2 * (n % 2) + 1:28 + 2 * (n % 2) + 2]).then_inc(g1, 1)
                if 1 <= n <= N1:
                    p_high1(n - 1)
                if n >= 2 and n % 2 == 1:
                    out_copy((n - 3) // 2)
            for h in range(HEADS):
                if h >= 2:
                    act.wait_ge(sub_mm, h - 1)
                elif h == 0:
                    act.wait_ge(o1, HEADS * PAIRS)
                nc.scalar.activation(osq[:, h % 2], o_raw[:, h], ACT.Square).then_inc(sub_sq, 1)
            act.wait_ge(sub_mm, HEADS)
            nc.scalar.activation(sub_r[0:HEADS, 0], ps[0:HEADS, 0], ACT.Sqrt, bias=eps_c[0:HEADS, 1:2],
                                 scale=1.0 / P).then_inc(sub_sqrt, 1)
            for h in range(HEADS):
                act.wait_ge(sub_t, h + 1)
                nc.scalar.activation(o1_hi[:, h], osq[:, h % 2], ACT.Copy, scale=subg[:, 1:2]).then_inc(sub_hi, 1)
            for i in range(8):
                u = FIRST["out1"] + i
                high_u(u + AHEAD)
                act.wait_ge(x_added, 40 + i + 1)
                squares(3, i)
            norm(3)
            mlp(1)
            norm(4)

        @block.vector
        def _(dve):
            st = Steps(dve, dsteps)
            V = nc.vector
            tt = V.tensor_tensor

            def mod_step(m_k, acc_src, k, n=None):
                for v in range(2):
                    if k == 0:
                        ins = V.tensor_scalar(mod_acc[:, v], acc_src, cact[:, 0, v:v + 1], None, ALU.mult)
                    else:
                        dve.wait_ge(dsteps, st.n - 1)
                        ins = V.scalar_tensor_tensor(out=mod_acc[:, v], in0=acc_src, scalar=cact[:, k, v:v + 1],
                                                     in1=mod_acc[:, v], op0=ALU.mult, op1=ALU.add)
                    ins.then_inc(dsteps, 1)
                    st.n = st.n + 1

            def mod_ring_step(k, n, target):
                dve.wait_ge(mod_in[k % 2], target)
                mod_step(None, mod_ring[:, k % 2], k)
                dve.wait_ge(dsteps, st.n)
                dve.sem_inc(mod_used, 1)

            def mod_sum():
                dve.sem_inc(mod_summed, 1)

            def extract(m):
                dve.wait_ge(mod_rows, m + 1)
                idb = ident[:].unsqueeze(1).broadcast_to([P, 4, P])
                acc = mod_acc[:].rearrange("p v (c q) -> p v c q", c=4)
                for v in range(2):
                    ins = tt(acc[:, v], ps[:, 4 + v].rearrange("p (c q) -> p c q", c=4), idb, op=ALU.mult)
                    ins.then_inc(dsteps, 1)
                    st.n = st.n + 1
                dve.wait_ge(dsteps, st.n)
                st.wait(V.tensor_reduce(modr[:], acc, AX.X, ALU.add))
                one = bass.ds(m, 1)
                for v in range(2):
                    ins = tt(mods[:, one, v, :], modr[:, v:v + 1, :], b_mod[:, one, :], op=ALU.add)
                ins.then_inc(mod_done, 1)

            def scales(i):
                m = 12 * (i // 2) + 2 * (1 + 3 * (i % 2))
                dve.wait_ge(mod_done, m + 2)
                for v in range(2):
                    ins = V.scalar_tensor_tensor(out=gs[:, i, v].rearrange("p (a b) -> p a b", a=2),
                                                 in0=mods[:, m:m + 2, v, :], scalar=1.0,
                                                 in1=gains[:, i].rearrange("p (a b) -> p a b", a=2),
                                                 op0=ALU.add, op1=ALU.mult)
                st.wait(ins)

            def sum_squares(i, m):
                n = NORM_TOK[i]
                dve.wait_ge(sq_made, KT * i + m + 1)
                if m == 0:
                    V.tensor_copy(ssum[:, 0:n], tmp_b[:, 0, 0:n]).then_inc(sq_summed, 1)
                else:
                    dve.wait_ge(sq_summed, KT * i + m)
                    tt(ssum[:, 0:n], ssum[:, 0:n], tmp_b[:, m % 2, 0:n], op=ALU.add).then_inc(sq_summed, 1)

            def norm(i):
                n = NORM_TOK[i]
                dve.wait_ge(norm_sqrt, i + 1)
                st.wait(V.reciprocal(rstd[:, 0:n], rstd[:, 0:n]))
                for k in range(KT + 1):
                    if k < KT:
                        if k >= 2:
                            dve.wait_ge(out_made if i == 4 else aff_made, (0 if i == 4 else KT * i) + k - 1)
                        for x, _, cols in parts(n):
                            ins = tt(tmp_a[:, k % 2, cols], x[:, k], rstd[:, cols], op=ALU.mult)
                        ins.then_inc(t_made, 1)
                    if k >= 1 and i < 4:
                        dve.wait_ge(aff_made, KT * i + k)
                        V.tensor_copy(h_hi[:, k - 1, 0:n], tmp_b[:, (k - 1) % 2, 0:n]).then_inc(hh_made, 1)

            def add_x(layer, u_wait, par, i, m, count):
                dve.wait_ge(unit_done, u_wait)
                if not isinstance(count, int) or count:
                    dve.wait_ge(x_added, count)
                for (x, v, _), (bank, _, n) in zip(parts(TOK if layer == 0 else LAT), both):
                    ins = V.scalar_tensor_tensor(out=x[:, i], in0=ps[:, 2 * par + bank, 0:n], scalar=gate(layer, m, v, i),
                                                 in1=x[:, i], op0=ALU.mult, op1=ALU.add)
                ins.then_inc(x_added, 1)

            def hidden(layer, b, i):
                a = ha(layer, b, i)
                n = TOK if layer == 0 else LAT
                dve.wait_ge(relu_made, a + 1)
                if i >= 2:
                    dve.wait_ge(hid_made, a - 1)
                ins = tt(tmp_b[:, i % 2, 0:n], tmp_a[:, i % 2, 0:n], tmp_a[:, i % 2, 0:n], op=ALU.mult)
                ins.then_inc(relu_used, 1)
                dve.wait_ge(relu_used, a + 1)
                st.wait(V.tensor_copy(hid_hi[:, i, 0:n], tmp_b[:, i % 2, 0:n]))
                tt(hid_lo[:, i, 0:n], tmp_b[:, i % 2, 0:n], hid_hi[:, i, 0:n].bitcast(F32),
                   op=ALU.subtract).then_inc(hid_made, 1)

            def mlp(layer):
                u0 = FIRST[f"mlp{layer}"]

                def blk(b, last):
                    for i in range(16):
                        u = u0 + i
                        if i < 8:
                            hidden(layer, b, i)
                        else:
                            add_x(layer, u + 16 * b + 1, u % 2, i - 8, 5, xa(layer, b, i - 8))
                            if last and i > 8:
                                sum_squares(2 + 2 * layer, i - 9)
                        if layer == 0 and not last:
                            g = i // 4
                            for k in MOD_AT[i % 4]:
                                n = 8 * (8 + g) + k
                                mod_ring_step(k, None, 16 * (n // 2 + 1) + 256 * b)
                            if i % 4 == 2:
                                mod_sum()
                            if i % 4 == 3:
                                extract(12 + g + 4 * b)
                    if last:
                        sum_squares(2 + 2 * layer, 7)

                if layer == 0:
                    per = 8 + 4 * (16 + 3)
                else:
                    per = 8
                with st.loop(HID_BLOCKS - 1, per) as b:
                    blk(b, False)
                blk(HID_BLOCKS - 1, True)

            st.wait(V.memset(ones[:], 1.0))
            V.memset(eps_c[:, 0:1], EPS)
            st.wait(V.memset(eps_c[:, 1:2], SUB_EPS))
            dve.sem_inc(ones_ok, 1)
            dve.wait_ge(consts_in, 16 * 7)
            lam = lam_in[:].rearrange("p (a b) -> p a b", b=2)
            tt(lam_t[0:HD, 0:2], lam[:, :, 0], lam[:, :, 1], op=ALU.mult).then_inc(lam_ok, 1)
            dve.wait_ge(exp_c, 1)
            st.wait(V.tensor_scalar(ctmp[:], ctmp[:], 1.0, None, ALU.add))
            st.wait(V.reciprocal(ctmp[:], ctmp[:]))
            st.wait(tt(cact[:], cond[:], ctmp[:], op=ALU.mult))
            V.tensor_scalar(subg[:, 1:2], subg[:, 0:1], 1.0 - LAM_INIT, None, ALU.mult)
            dve.wait_ge(lam_exp, 1)
            st.wait(V.scalar_tensor_tensor(out=lam_t[:, 4:5], in0=lam_t[:, 3:4], scalar=LAM_INIT,
                                           in1=lam_t[:, 2:3], op0=ALU.subtract, op1=ALU.subtract))
            for m in range(4):
                dve.wait_ge(big_in[m % 3], 16 * (m // 3 + 1))
                for k in range(KT):
                    mod_step(None, big[:, m % 3, k], k)
                dve.wait_ge(dsteps, st.n)
                mod_sum()
                if m == 0:
                    for k in range(KT):
                        sum_squares(0, k)
                extract(m)
            scales(0)
            norm(0)

            def l0_mods(j):
                m = 4 + j // 2
                if j % 2 == 0:
                    for k in range(6):
                        n = 8 * (m - 4) + k
                        mod_ring_step(k, n, 16 * (n // 2 + 1))

            def l0_pre(j):
                m = 4 + j // 2
                if j % 2 == 1:
                    for k in (6, 7):
                        n = 8 * (m - 4) + k
                        mod_ring_step(k, n, 16 * (n // 2 + 1))
                    mod_sum()

            def l0_post(j):
                l0_mods(j)
                if j % 2 == 1:
                    extract(4 + j // 2)

            for i in range(12):
                u = FIRST["f"] + i
                l0_pre(i)
                if i < 4:
                    dve.wait_ge(f_hi_s, i + 1)
                    for bank, c0, n in both:
                        ins = tt(f_lo[:, i, c0:c0 + n], ps[:, 2 * (u % 2) + bank, 0:n],
                                 f_hi[:, i, c0:c0 + n].bitcast(F32), op=ALU.subtract)
                    ins.then_inc(f_out, 1)
                l0_post(i)
            dve.wait_ge(dft_hi_s, 1)
            tt(dft_lo[:], dft_raw[:], dft_hi[:].bitcast(F32), op=ALU.subtract).then_inc(dft_lo_s, 1)
            dve.wait_ge(dft_lo_s, 1)
            for n in range(2 * NT):
                sl = slice(2 * (n % 2), 2 * (n % 2) + 2)
                dve.wait_ge(u_hi_s, n + 1)
                tt(u_lo[:, n // 2, sl].rearrange("p g c -> p (g c)"), ps[:, V_BANK[n % 6]],
                   u_hi[:, n // 2, sl].rearrange("p g c -> p (g c)").bitcast(F32), op=ALU.subtract).then_inc(u_lo_s, 1)
            for g in range(4):
                dve.wait_ge(y_hi_s, g + 1)
                tt(y_lo[:, g, 0:LAT], ps[:, g], y_hi[:, g, 0:LAT].bitcast(F32), op=ALU.subtract).then_inc(y_lo_s, 1)
            for g in range(2):
                dve.wait_ge(y_hi_s, 5 + g)
                sl = slice(2 * g, 2 * g + 2)
                tt(y_lo[:, sl, LAT:TOK], ps[:, 6 + g].rearrange("p (g c) -> p g c", g=2),
                   y_hi[:, sl, LAT:TOK].bitcast(F32), op=ALU.subtract).then_inc(y_lo_s, 1)
            for j in range(4):
                l0_pre(12 + j)
                l0_post(12 + j)
            scales(1)
            for n in range(NT):
                dve.wait_ge(v0_hi_s, n + 1)
                tt(v0[:, n, :, HD:P], ps[:, V_BANK[n]].rearrange("p (h d) -> p h d", d=HD),
                   v0[:, n, :, 0:HD].bitcast(F32), op=ALU.subtract).then_inc(v0_lo_s, 1)

            def split(h):
                e, o, p = 64 * (h % 2), 64 - 64 * (h % 2), h % 2
                if h >= 2:
                    dve.wait_ge(s_made, 6 * (h - 1))
                V.tensor_copy(q2a[e:e + 64, p], q0[e:e + 64, h // 2]).then_inc(jh, 1)
                st.wait(V.tensor_copy(k2[e:e + 64, p], k0[e:e + 64, h // 2]))
                tt(k2[o:o + 64, p], k0[e:e + 64, h // 2], k2[e:e + 64, p].bitcast(F32), op=ALU.subtract).then_inc(jk, 1)

            def least(n):
                h, t_ = n // 6, n % 6
                dve.wait_ge(s_made, n + 1)
                w = 256
                if t_ < 4:
                    w = 512
                    if t_ == 0:
                        dve.wait_ge(bias_ok, h + 1)
                    st.wait(tt(ps[:, n % 3, 0:256], ps[:, n % 3, 0:256], bias[:, h % 2, VARIANT[t_]], op=ALU.subtract))
                V.tensor_reduce(stat[:, n % 4:n % 4 + 1], ps[:, n % 3, 0:w], AX.X, ALU.min).then_inc(m_made, 1)

            def normalise(n):
                w = 512 if n % 6 < 4 else 256
                dve.wait_ge(e_made, n + 1)
                st.wait(V.reciprocal(stat[:, 8 + n % 4:9 + n % 4], stat[:, 4 + n % 4:5 + n % 4]))
                V.tensor_scalar(prob0[:, n % PROBS, 0:w], prob0[:, n % PROBS, 0:w], stat[:, 8 + n % 4:9 + n % 4],
                                None, ALU.mult).then_inc(p_made, 1)

            def p_low(n):
                c = 4 if n % 6 < 4 else 2
                dve.wait_ge(th_made, n + 1)
                tt(pt0[:, n % 2, 0:c, P:2 * P], ps[:, 3 + n % 2, 0:P * c].rearrange("p (c q) -> p c q", c=c),
                   pt0[:, n % 2, 0:c, 0:P].bitcast(F32), op=ALU.subtract).then_inc(tl_made, 1)

            def out_sum(h):
                e, p = 64 * (h % 2), h % 2
                dve.wait_ge(oc_made, h + 1)
                o = osum[e:e + 64, p].rearrange("p (t q) -> p t q", q=P)
                st.wait(tt(o, pv_ps[0:64, :, 0:P], o, op=ALU.add))
                tt(o, pv_ps[0:64, :, P:2 * P], o, op=ALU.add).then_inc(od_made, 1)
                dve.wait_ge(od_made, h + 1)
                st.wait(V.tensor_copy(o0_hi[e:e + 64, h // 2], osum[e:e + 64, p]))
                tt(o0_lo[e:e + 64, h // 2], osum[e:e + 64, p], o0_hi[e:e + 64, h // 2].bitcast(F32),
                   op=ALU.subtract).then_inc(ol_made, 1)

            dve.wait_ge(unit_done, FIRST["out0"])
            split(0)
            N0 = 6 * HEADS
            for n in range(N0 + 4):
                if n < N0:
                    if n % 6 == 1 and n // 6 + 1 < HEADS:
                        split(n // 6 + 1)
                    least(n)
                if 1 <= n <= N0:
                    normalise(n - 1)
                if 2 <= n <= N0 + 1:
                    p_low(n - 2)
                if n >= 4 and (n - 4) % 6 == 5:
                    out_sum((n - 4) // 6)
            dve.wait_ge(xr_in, 32)
            for i in range(8):
                u = FIRST["out0"] + i
                add_x(0, u + 1, u % 2, i, 2, i)
                if i:
                    sum_squares(1, i - 1)
            sum_squares(1, 7)
            norm(1)
            mlp(0)
            scales(2)
            norm(2)
            scales(3)
            dve.wait_ge(table_in, 16 * 3)
            swap = [(i + 16) % 32 for i in range(32)]
            for i in range(16):
                u = FIRST["q1"] + i
                src = ps[:, 2 * (u % 2), 0:LAT]
                dst = q1[:, i] if i < 8 else k1[:, i - 8, 0:LAT]
                f = -1.0 / 8 if i < 8 else 1.0
                dve.wait_ge(unit_done, u + 1)
                st.wait(V.stream_shuffle(rt[:, 0], src, swap))
                V.scalar_tensor_tensor(out=rt[:, 1], in0=src, scalar=f, in1=cosb[:], op0=ALU.mult,
                                       op1=ALU.mult).then_inc(rope_read, 1)
                st.wait(V.scalar_tensor_tensor(out=rt[:, 2], in0=rt[:, 0], scalar=f, in1=sinb[:], op0=ALU.mult, op1=ALU.mult))
                dve.wait_ge(rope_read, i + 1)
                st.wait(tt(dst, rt[:, 1], rt[:, 2], op=ALU.add))
            dve.sem_inc(rope_done, 1)

            def split1(h):
                for i in range(2):
                    e, o = 64 * i, 64 - 64 * i
                    V.tensor_copy(aq2a[e:e + 64, i], q1[e:e + 64, h]).then_inc(jh1, 1)
                    st.wait(V.tensor_copy(ak2[e:e + 64, i], k1[e:e + 64, h]))
                    tt(ak2[o:o + 64, i], k1[e:e + 64, h], ak2[e:e + 64, i].bitcast(F32), op=ALU.subtract).then_inc(jk1, 1)

            def split_v(h):
                if h:
                    dve.wait_ge(pv1, 2 * h)
                V.tensor_copy(avh[:], v1[:, :, P * h:P * h + P]).then_inc(vh1, 1)

            def least1(n):
                for i in range(2):
                    s = 2 * n + i
                    dve.wait_ge(s1, s + 1)
                    c = 16 + 4 * (n % 2) + i
                    V.tensor_reduce(stat[:, c:c + 1], ps2(2 * (s % 2)), AX.X, ALU.min).then_inc(m1, 1)

            def coef(n):
                dve.wait_ge(e1, 2 * n + 2)
                c, d = 18 + 4 * (n % 2), 28 + 2 * (n % 2)
                st.wait(V.reciprocal(stat[:, d:d + 2], stat[:, c:c + 2]))
                V.tensor_scalar(stat[:, d + 1:d + 2], stat[:, d + 1:d + 2], lam_t[:, 4:5], None, ALU.mult).then_inc(c1, 1)

            def combine(n):
                d = 28 + 2 * (n % 2)
                dve.wait_ge(g1, n + 1)
                V.scalar_tensor_tensor(out=aprob[:, n % 2, 0], in0=aprob[:, n % 2, 0], scalar=stat[:, d:d + 1],
                                       in1=aprob[:, n % 2, 1], op0=ALU.mult, op1=ALU.add).then_inc(a1, 1)

            def p_low1(n):
                dve.wait_ge(th1, n + 1)
                for j in range(2):
                    sl = (slice(None), slice(3 * j, 3 * j + 3), slice(P * (n % 2), P * (n % 2) + P))
                    ins = tt(at_lo[sl], ps[:, 4 + j, 0:384].rearrange("p (c q) -> p c q", c=3),
                             at_hi[sl].bitcast(F32), op=ALU.subtract)
                ins.then_inc(tl1, 1)

            dve.wait_ge(unit_done, FIRST["out1"])
            dve.wait_ge(v1_out, 2 * NT)
            dve.wait_ge(kc_out, 8)
            N1 = 4 * HEADS
            split1(0)
            split_v(0)
            for n in range(N1 + 2):
                if n < N1:
                    if n % 4 == 0 and n:
                        dve.wait_ge(s1, 2 * n)
                        split1(n // 4)
                    least1(n)
                    coef(n)
                if 1 <= n <= N1:
                    p_low1(n - 1)
                if n < N1:
                    combine(n)
                if n >= 5 and n % 4 == 1 and n // 4 < HEADS:
                    split_v(n // 4)
            dve.wait_ge(sub_sqrt, 1)
            V.reciprocal(sub_r[0:HEADS, 1], sub_r[0:HEADS, 0]).then_inc(sub_rec, 1)
            for h in range(HEADS + 1):
                if h < HEADS:
                    dve.wait_ge(sub_bc, h + 1)
                    if h >= 2:
                        dve.wait_ge(sub_lo, h - 1)
                    tt(osq[:, h % 2], o_raw[:, h], ps[:, 1 + h % 2], op=ALU.mult).then_inc(sub_t, 1)
                if h >= 1:
                    dve.wait_ge(sub_hi, h)
                    V.scalar_tensor_tensor(out=o1_lo[:, h - 1], in0=osq[:, (h - 1) % 2], scalar=subg[:, 1:2],
                                           in1=o1_hi[:, h - 1].bitcast(F32), op0=ALU.mult,
                                           op1=ALU.subtract).then_inc(sub_lo, 1)
            for i in range(8):
                u = FIRST["out1"] + i
                add_x(1, u + 1, u % 2, i, 2, 40 + i)
                if i:
                    sum_squares(3, i - 1)
            sum_squares(3, 7)
            norm(3)
            mlp(1)
            norm(4)

        @block.tensor
        def _(pe):
            mm = nc.tensor.matmul

            def three(out, a, b, start, stop, last=None):
                mm(out, a[0], b[1], start=start, stop=False)
                mm(out, a[1], b[0], start=False, stop=False)
                return mm(out, a[0], b[0], start=False, stop=stop)

            def unit(u, s, par, hi, lo, chunks, k_wait=None):
                pe.wait_ge(lo_made, u + 1)
                for k in range(KT):
                    if k_wait:
                        k_wait(k)
                    w = (w_hi[:, s, P * k:P * k + P], w_lo[:, s, P * k:P * k + P])
                    for bank, c0, n in chunks:
                        ins = three(ps[:, 2 * par + bank, 0:n], w, (hi(k)[:, c0:c0 + n], lo(k)[:, c0:c0 + n]),
                                    k == 0, k == KT - 1)
                ins.then_inc(unit_done, 1)

            h_t = (lambda k: h_hi[:, k], lambda k: h_lo[:, k])
            hid_t = (lambda k: hid_hi[:, k], lambda k: hid_lo[:, k])

            def mod_mm(m):
                pe.wait_ge(mod_summed, m + 1)
                for v in range(2):
                    ins = mm(ps[:, 4 + v], ones[:], mod_acc[:, v], start=True, stop=True)
                ins.then_inc(mod_rows, 1)

            def norm_mm(i):
                pe.wait_ge(sq_summed, KT * (i + 1))
                ins = mm(ps[:, 6, 0:LAT], ones[:], ssum[:, 0:LAT], start=True, stop=True)
                if NORM_TOK[i] == TOK:
                    ins = mm(ps[:, 7, 0:CTX], ones[:], ssum[:, LAT:TOK], start=True, stop=True)
                ins.then_inc(norm_sum, 1)

            def values(u, j, start, stop, banks_free=None):
                s = u % SLOTS
                pe.wait_ge(lo_made, u + 1)
                for n in range(NT):
                    if banks_free:
                        banks_free(n)
                    for kk in range(2):
                        k = 2 * j + kk
                        ins = three(ps[:, V_BANK[n]], (h_hi[:, k, P * n:P * n + P], h_lo[:, k, P * n:P * n + P]),
                                    (w_hi[:, s, 512 * kk:512 * kk + 512], w_lo[:, s, 512 * kk:512 * kk + 512]),
                                    start and kk == 0, stop and kk == 1)
                ins.then_inc(unit_done, 1)

            def mlp(layer):
                u0 = FIRST[f"mlp{layer}"]
                chunks = both[:2 - layer]

                def blk(b, last):
                    for i in range(16):
                        u = u0 + i
                        if i == 0:
                            pe.wait_ge(x_added, xa(layer, b, 0) - 1)
                        elif i == 1:
                            pe.wait_ge(x_added, xa(layer, b, 0))
                        elif i < 8:
                            pe.wait_ge(relu_made, ha(layer, b, i) - 1)
                        elif i < 10:
                            pe.wait_ge(relu_made, ha(layer, b, i) - 1)
                        else:
                            pe.wait_ge(x_added, xa(layer, b, i - 8) - 1)
                        if i < 8:
                            unit(u + 16 * b, u % SLOTS, u % 2, *h_t, chunks)
                        else:
                            unit(u + 16 * b, u % SLOTS, u % 2, *hid_t, chunks,
                                 (lambda k: pe.wait_ge(hid_made, ha(layer, b, k) + 1)) if i == 8 else None)
                        if layer == 0 and not last and i % 4 == 3:
                            pe.wait_ge(mod_done, 12 + 4 * b + i // 4)
                            mod_mm(12 + 4 * b + i // 4)

                with pe.Fori(0, HID_BLOCKS - 1) as b:
                    blk(b, False)
                blk(HID_BLOCKS - 1, True)
                norm_mm(2 + 2 * layer)

            pe.wait_ge(ones_ok, 1)
            pe.wait_ge(lam_ok, 1)
            mm(ps[:, 6, 0:2], ones[0:HD, :], lam_t[0:HD, 0:2], start=True, stop=True).then_inc(lam_mm, 1)
            for m in range(4):
                if m >= 1:
                    pe.wait_ge(mod_done, m)
                mod_mm(m)
            pe.wait_ge(lam_exp, 1)
            norm_mm(0)

            def h_wait(i):
                return lambda k: pe.wait_ge(h_made, KT * i + k + 1)

            for i in range(12):
                u = FIRST["f"] + i
                if 2 <= i < 6:
                    pe.wait_ge(f_out, i - 1)
                elif i >= 6:
                    pe.wait_ge(qk_out, i - 5)
                unit(u, u % SLOTS, u % 2, *h_t, both, h_wait(0) if i == 0 else None)
                if i % 2 == 1:
                    pe.wait_ge(mod_done, 4 + i // 2)
                    mod_mm(4 + i // 2)
            pe.wait_ge(f_out, 4)
            pe.wait_ge(dft_lo_s, 1)
            pe.wait_ge(qk_out, 8)
            for n in range(2 * NT):
                tok = slice(P * (n // 2), P * (n // 2) + P)
                if n >= 6:
                    pe.wait_ge(u_lo_s, n - 5)
                for j in range(2):
                    g = 2 * (n % 2) + j
                    ins = three(ps[:, V_BANK[n % 6], 256 * j:256 * j + 256], (f_hi[:, g, tok], f_lo[:, g, tok]),
                                (dft_hi[:], dft_lo[:]), True, True)
                ins.then_inc(u_mm, 1)
            pe.wait_ge(u_lo_s, 2 * NT)
            for i in range(4):
                u = FIRST["dft"] + i
                s = u % SLOTS
                pe.wait_ge(lo_made, u + 1)
                for g in range(4):
                    c = slice(P * (i // 2), P * (i // 2) + P)
                    for j in range(2):
                        n = 2 * (i % 2) + j
                        ins = three(ps[:, g], (u_hi[:, n, g, c], u_lo[:, n, g, c]),
                                    (w_hi[:, s, 512 * j:512 * j + 512], w_lo[:, s, 512 * j:512 * j + 512]),
                                    i == 0 and j == 0, i == 3 and j == 1)
                ins.then_inc(unit_done, 1)
            u = FIRST["dft"] + 4
            s = u % SLOTS
            pe.wait_ge(lo_made, u + 1)
            for g in range(4):
                for j in range(4):
                    c = slice(P * (j // 2), P * (j // 2) + P)
                    n = 4 + j % 2
                    ins = three(ps[:, 6 + g // 2, 256 * (g % 2):256 * (g % 2) + 256], (u_hi[:, n, g, c], u_lo[:, n, g, c]),
                                (w_hi[:, s, 256 * j:256 * j + 256], w_lo[:, s, 256 * j:256 * j + 256]), j == 0, j == 3)
            ins.then_inc(unit_done, 1)
            def y_free(n):
                pe.wait_ge(y_lo_s, min(n + 1, 4) if n < 4 else n + 1)

            for i in range(4):
                values(FIRST["v0"] + i, i, i == 0, i == 3, y_free if i == 0 else None)
                if i % 2 == 1:
                    pe.wait_ge(mod_done, 10 + i // 2)
                    mod_mm(10 + i // 2)

            def scores(n):
                h, t_ = n // 6, n % 6
                p = h % 2
                if t_ == 0:
                    pe.wait_ge(js, h + 1)
                    pe.wait_ge(jk, h + 1)
                if n >= 3:
                    pe.wait_ge(e_made, n - 2)
                else:
                    pe.wait_ge(v0_lo_s, NT)
                tok = slice(P * t_, P * t_ + P)
                keys = [slice(LAT, TOK)] if t_ >= 4 else [slice(WINDOW[t_], WINDOW[t_] + 256), slice(LAT, TOK)]
                for j, ks in enumerate(keys):
                    o = ps[:, n % 3, 256 * j:256 * j + 256]
                    mm(o, q2b[:, p, tok], k2[:, p, ks], start=True, stop=False)
                    ins = mm(o, q2a[:, p, tok], k2[:, p, ks], start=False, stop=True)
                ins.then_inc(s_made, 1)

            def turn(n):
                c = 4 if n % 6 < 4 else 2
                pe.wait_ge(p_made, n + 1)
                if n >= 2:
                    pe.wait_ge(tl_made, n - 1)
                for j in range(c):
                    ins = nc.tensor.transpose(ps[:, 3 + n % 2, P * j:P * j + P], prob0[:, n % PROBS, P * j:P * j + P], ident[:])
                ins.then_inc(tr_made, 1)

            def weigh(n):
                h, t_ = n // 6, n % 6
                pe.wait_ge(tl_made, n + 1)
                if n == 0:
                    pe.wait_ge(shift_in, 16 * 6)
                if t_ == 0 and h:
                    pe.wait_ge(od_made, h)
                lat = {0: (v0[:, 0], v0[:, 1]), 1: (v0s[:, 0], v0s[:, 1]), 2: (v0s[:, 1], v0s[:, 2]),
                       3: (v0[:, 2], v0[:, 3])}
                vs = (lat[t_] if t_ < 4 else ()) + (v0[:, 4], v0[:, 5])
                for c, v in enumerate(vs):
                    ins = mm(pv_ps[:, t_, :], v[:, h, :], pt0[:, n % 2, c, :], start=c == 0, stop=c == len(vs) - 1)
                ins.then_inc(pv_made, 1)

            N0 = 6 * HEADS
            pe.wait_ge(mod_done, 12)
            scores(0)
            scores(1)
            for n in range(N0 + 1):
                if n + 2 < N0:
                    scores(n + 2)
                if n < N0:
                    turn(n)
                if n >= 1:
                    weigh(n - 1)
            mix_hi = lambda k: y_hi[:, k] if k < 4 else o0_hi[:, k - 4]
            mix_lo = lambda k: y_lo[:, k] if k < 4 else o0_lo[:, k - 4]
            pe.wait_ge(ol_made, HEADS)
            for i in range(8):
                u = FIRST["out0"] + i
                if i >= 2:
                    pe.wait_ge(x_added, i - 1)
                unit(u, u % SLOTS, u % 2, mix_hi, mix_lo, both)
            norm_mm(1)
            pe.wait_ge(h_made, 2 * KT)
            mlp(0)
            for i in range(16):
                u = FIRST["q1"] + i
                if i >= 2:
                    pe.wait_ge(rope_read, i - 1)
                if i >= 10:
                    pe.wait_ge(kc_out, i - 9)
                unit(u, u % SLOTS, u % 2, *h_t, both if i >= 8 else both[:1], h_wait(2) if i == 0 else None)
            pe.wait_ge(rope_read, 16)
            pe.wait_ge(kc_out, 8)
            for j in range(2):
                for i in range(4):
                    values(FIRST["v1"] + 4 * j + i, i, i == 0, i == 3,
                           (lambda n: pe.wait_ge(v1_out, n + 1)) if j == 1 and i == 0 else None)

            def scores1(n):
                h, t_ = n // 4, n % 4
                for i in range(2):
                    s = 2 * n + i
                    if t_ == 0:
                        pe.wait_ge(js1, 2 * h + i + 1)
                        pe.wait_ge(jk1, 2 * h + i + 1)
                    if s >= 2:
                        pe.wait_ge(e1, s - 1)
                    b0 = 2 * (s % 2)
                    tok = slice(P * t_, P * t_ + P)
                    for bank, ks in ((b0, slice(0, LAT)), (b0 + 1, slice(LAT, TOK))):
                        o = ps[:, bank, 0:ks.stop - ks.start]
                        mm(o, aq2b[:, i, tok], ak2[:, i, ks], start=True, stop=False)
                        ins = mm(o, aq2a[:, i, tok], ak2[:, i, ks], start=False, stop=True)
                    ins.then_inc(s1, 1)

            def turn1(n):
                pe.wait_ge(a1, n + 1)
                if n >= 1:
                    pe.wait_ge(tl1, n)
                for c in range(NT):
                    ins = nc.tensor.transpose(ps[:, 4 + c // 3, P * (c % 3):P * (c % 3) + P],
                                              aprob[:, n % 2, 0, P * c:P * c + P], ident[:])
                ins.then_inc(tr1, 1)

            def weigh1(m):
                pe.wait_ge(tl1, 2 * m + 2)
                if m % 2 == 0:
                    pe.wait_ge(vl1, m // 2 + 1)
                if m >= 2:
                    pe.wait_ge(o1, m - 1)
                for c in range(NT):
                    ins = three(ps[:, 6 + m % 2, 0:256], (avh[:, c], avl[:, c]), (at_hi[:, c], at_lo[:, c]), c == 0, c == NT - 1)
                ins.then_inc(pv1, 1)

            pe.wait_ge(v1_out, 2 * NT)
            N1 = 4 * HEADS
            scores1(0)
            for n in range(N1 + 1):
                if n + 1 < N1:
                    scores1(n + 1)
                if n < N1:
                    turn1(n)
                if n >= 2 and n % 2 == 0:
                    weigh1(n // 2 - 1)
            pe.wait_ge(oneh_in, 32)
            for h in range(HEADS):
                pe.wait_ge(sub_sq, h + 1)
                mm(ps[0:HEADS, 0], oneh[:, h], osq[:, h % 2], start=h == 0, stop=h == HEADS - 1).then_inc(sub_mm, 1)
            pe.wait_ge(sub_rec, 1)
            for h in range(HEADS):
                if h >= 2:
                    pe.wait_ge(sub_t, h - 1)
                mm(ps[:, 1 + h % 2], selh[:, h], sub_r[0:HEADS, 1], start=True, stop=True).then_inc(sub_bc, 1)
            pe.wait_ge(sub_lo, HEADS)
            for i in range(8):
                u = FIRST["out1"] + i
                if i >= 2:
                    pe.wait_ge(x_added, 40 + i - 1)
                unit(u, u % SLOTS, u % 2, lambda k: o1_hi[:, k], lambda k: o1_lo[:, k], both[:1])
            norm_mm(3)
            pe.wait_ge(h_made, 4 * KT)
            mlp(1)


_OUT = (P, KT, LAT)


def _order():
    t = np.arange(LAT)
    return (t % ROWS) * COLS + t // ROWS


def _stationary(w):
    n = w.shape[1] // P
    return w.reshape(KT, P, n, P).transpose(2, 1, 0, 3).reshape(n, P, D)


def _moving(w):
    n = w.shape[1] // 512
    return w.reshape(4, 2, P, n, 512).transpose(3, 0, 2, 1, 4).reshape(4 * n, P, D)


def _mlp(w_in, w_out):
    u = []
    for b in range(HID_BLOCKS):
        u += [_stationary(w_in[:, D * b:D * b + D]), _stationary(w_out[D * b:D * b + D])]
    return u


def _dft(n, order, scale):
    a = 2 * np.pi * (np.outer(order, order) % n) / n
    return np.stack([np.cos(a), -np.sin(a)]) * scale


def _tables():
    order = _order()
    cs = _dft(LAT, order, (LAT * P) ** -0.5).reshape(2, 2, 2, P, LAT).transpose(0, 1, 3, 2, 4).reshape(4, P, D)
    cc = _dft(CTX, np.arange(CTX), (CTX * P) ** -0.5).reshape(4, P, CTX).transpose(1, 0, 2).reshape(1, P, D)
    units = np.concatenate([cs, cc]).astype(np.float32)
    a = 2 * np.pi * (np.outer(np.arange(P), np.arange(P)) % P) / P
    dft128 = np.concatenate([np.cos(a), np.sin(a)], axis=1).astype(np.float32)
    nf = HD // 4
    freq = np.float32(10000.0) ** (-np.arange(nf, dtype=np.float32) / np.float32(nf))
    ang = np.zeros((P, LAT), np.float32)
    sign = np.zeros((P, 1), np.float32)
    for p in range(P):
        pos = order // COLS if p % 64 < 32 else order % COLS
        ang[p] = pos.astype(np.float32) * freq[p % nf]
        sign[p] = -1.0 if p % 32 < nf else 1.0
    cos = np.cos(ang.astype(np.float64)).astype(np.float32)
    sin = (np.sin(ang.astype(np.float64)) * sign).astype(np.float32)
    mask = np.zeros((P, 3, 32), np.float32)
    for v, qt in ((0, 0), (1, 1), (2, 3)):
        col = 16 * qt + np.arange(P) // ROWS
        start = np.clip(col - 8, 0, COLS - 16)
        key = WINDOW[qt] // ROWS + np.arange(32)
        ok = (key[None] >= start[:, None]) & (key[None] < start[:, None] + 16)
        mask[:, v] = np.where(ok, 0.0, NEG)
    oneh = np.zeros((P, HEADS, HEADS), np.float32)
    selh = np.zeros((HEADS, HEADS, P), np.float32)
    for h in range(HEADS):
        oneh[:, h, h] = 1.0
        selh[h, h] = 1.0
    return units, dict(dft128=dft128, cos=cos, sin=sin, mask=mask, ident=np.eye(P, dtype=np.float32),
                       oneh=oneh, selh=selh)


def _bias(rpb):
    q = np.arange(P)
    k = np.arange(256)
    out = []
    for v, qt in ((0, 0), (1, 1), (2, 3)):
        qc, qr = 16 * qt + q // ROWS, q % ROWS
        kc, kr = WINDOW[qt] // ROWS + k // ROWS, k % ROWS
        dr = kr[None] - qr[:, None] + 7
        dc = np.clip(kc[None] - qc[:, None], -15, 15) + 15
        out.append(rpb[:, dr, dc])
    return np.stack(out, axis=2)


def _columns(v):
    v = v.reshape(v.shape[:-1] + (v.shape[-1] // P, P))
    return np.moveaxis(v, -1, 0)


def _layout(i):
    order = _order()
    tables, d = _tables()
    w_ab, w_qkv = i["w_in_ab"][0], i["w_qkv_diff"][0]
    units = ([_stationary(w_ab[:, :1536])] + [tables] + [_moving(w_ab[:, 1536:])] + [_stationary(i["w_out_ab"][0])]
             + _mlp(i["w_mlp_in"][0], i["w_mlp_out"][0])
             + [_stationary(w_qkv[:, :2048]), _moving(w_qkv[:, 2048:]), _stationary(i["w_out_diff"][0])]
             + _mlp(i["w_mlp_in"][1], i["w_mlp_out"][1]))
    d["units"] = np.concatenate(units)
    d["x"] = i["x"][0][order].T.reshape(KT, P, LAT).transpose(1, 0, 2)
    d["ctx"] = i["ctx"][0].T.reshape(KT, P, CTX).transpose(1, 0, 2)
    d["w_mod"] = i["w_mod"].reshape(2, KT, P, 12, 512).transpose(0, 3, 2, 1, 4).reshape(24, P, KT, 512)
    d["b_mod"] = _columns(i["b_mod"].reshape(24, 512))
    d["gains"] = _columns(np.stack([i["norm_mix_g"][0], i["norm_mlp_g"][0], i["norm_mix_g"][1], i["norm_mlp_g"][1],
                                    i["final_norm_g"]]))
    d["cond"] = np.stack([_columns(i["c"][0]), _columns(i["c_ctx"])], axis=2)
    d["lam"] = np.stack([i["diff_lq1"][0], i["diff_lk1"][0], i["diff_lq2"][0], i["diff_lk2"][0]], axis=1)
    d["subln"] = np.stack([i["diff_subln_g"][0]] * 2, axis=1)
    d["bias"] = _bias(i["na_rpb"][0])
    return {k: np.ascontiguousarray(v) for k, v in d.items()}


def kernel(**inputs):
    import concourse.bacc as bacc
    from concourse.bass_utils import run_bass_kernel_spmd

    nc = bacc.Bacc("TRN2", target_bir_lowering=False, num_devices=1)
    data = _layout({k: np.asarray(v) for k, v in inputs.items()})
    t = {k: nc.dram_tensor(k + "_dram", v.shape, mybir.dt.from_np(v.dtype), kind="ExternalInput").ap()
         for k, v in data.items()}
    t["out"] = nc.dram_tensor("out_dram", _OUT, F32, kind="ExternalOutput").ap()
    build(nc, t)
    r = run_bass_kernel_spmd(nc, [{k + "_dram": v for k, v in data.items()}], core_ids=[0])
    out = np.asarray(r.results[0]["out_dram"]).transpose(2, 1, 0).reshape(LAT, D)
    back = np.empty_like(out)
    back[_order()] = out
    return back[None]
```

```python
from contextlib import ExitStack, contextmanager

import numpy as np

import concourse.bass as bass
from concourse import mybir

F32 = mybir.dt.float32
F32R = mybir.dt.float32r
ALU = mybir.AluOpType
ACT = mybir.ActivationFunctionType
AX = mybir.AxisListType

P = 128
D = 1024
KT = D // P
LAT, CTX = 512, 256
TOK = LAT + CTX
NT = TOK // P
ROWS, COLS = 8, 64
HEADS, HD = 8, 64
HID_BLOCKS = 4
EPS, SUB_EPS = 1e-6, 1e-5
LAM_INIT = 0.8 - 0.6 * float(np.exp(-0.3))
NEG = -1e30

STAGES = [("f", 4), ("q0", 4), ("k0", 4), ("dft", 5), ("v0", 4), ("out0", 8), ("mlp0", 64),
          ("k1", 8), ("q1", 8), ("v1", 8), ("out1", 8), ("mlp1", 64)]
FIRST, UNITS = {}, 0
for _name, _n in STAGES:
    FIRST[_name] = UNITS
    UNITS += _n
SLOTS = 4
AHEAD = 3

WINDOW = [0, 64, 192, 256]
VARIANT = [0, 1, 1, 2]
RING = 4


def mix_mods(i):
    if i < 4:
        m, ks = {-1: (4, range(8)), 0: (5, ()), 1: (5, range(3)), 2: (5, range(3, 6)), 3: (5, range(6, 8))}[i]
    else:
        m, ks = 4 + i // 2, range(4 * (i % 2), 4 * (i % 2) + 4)
    return [(m, k) for k in ks]


def out_mods(i):
    return [(10 + i // 3, k) for k in MOD_AT[i % 3]] if i < 6 else []


MOD_AT = [range(0, 3), range(3, 6), range(6, 8), ()]
PROBS = 3


class Steps:

    def __init__(self, eng, sem):
        self.eng, self.sem, self.n = eng, sem, 0

    def wait(self, ins):
        ins.then_inc(self.sem, 1)
        self.n = self.n + 1
        self.eng.wait_ge(self.sem, self.n)

    @contextmanager
    def loop(self, count, per):
        base = self.n
        with self.eng.Fori(0, count) as i:
            self.n = base + i * per
            yield i
        self.n = base + count * per


def build(nc, t):
    ctx = ExitStack()
    with ctx:
        base = 16512

        def at(name, shape, dt, offset):
            return nc.alloc_sbuf_tensor_at(name, shape, dt, offset=offset)

        size = lambda *shape: int(np.prod(shape)) * 4
        x_at = base
        a_at = x_at + size(TOK, KT)
        raw_at = a_at + 2 * size(TOK, KT)
        whi_at = raw_at + size(SLOTS, 1024)
        wlo_at = whi_at + size(SLOTS, 1024)
        con_at = wlo_at + size(SLOTS, 1024)
        rest = con_at + 5632
        mod_at = 229344 - size(RING + 2, 512)
        scr = rest + 2 * size(TOK, KT)

        xl = at("xl", [P, KT, LAT], F32, x_at)
        xc = at("xc", [P, KT, CTX], F32, x_at + size(KT, LAT))
        h_hi = at("h_hi", [P, KT, TOK], F32R, a_at)
        h_lo = at("h_lo", [P, KT, TOK], F32R, a_at + size(KT, TOK))
        raw = at("raw", [P, SLOTS, 1024], F32, raw_at)
        w_hi = at("w_hi", [P, SLOTS, 1024], F32R, whi_at)
        w_lo = at("w_lo", [P, SLOTS, 1024], F32R, wlo_at)

        c_off = [con_at]

        def const(name, shape, dt=F32):
            o = c_off[0]
            c_off[0] += (size(*shape[1:]) + 31) // 32 * 32
            assert c_off[0] <= rest
            return at(name, shape, dt, o)

        ident = const("ident", [P, P])
        ones = const("ones", [P, P])
        mods = const("mods", [P, 24, 2, 4])
        b_mod = const("b_mod_sb", [P, 24, 4])
        gains = const("gains", [P, 5, KT])
        gs = const("gs", [P, 4, 2, KT])
        cond = const("cond", [P, KT, 2])
        cact = const("cact", [P, KT, 2])
        eps_c = const("eps_c", [P, 2])
        stat = const("stat", [P, 64])
        modr = const("modr", [P, 2, 4])
        dft_at = c_off[0]
        dft_hi = const("dft_hi", [P, 256], F32R)
        dft_lo = const("dft_lo", [P, 256], F32R)
        lam_in = const("lam_in", [HD, 4])
        lam_t = const("lam_t", [P, 8])
        subg = const("subg", [P, 2])

        ctmp = at("ctmp", [P, KT, 2], F32, mod_at)
        mod_ring = at("mod_ring", [P, RING, 512], F32, mod_at)
        mod_acc = at("mod_acc", [P, 2, 512], F32, mod_at + size(RING, 512))

        big = at("mod_big", [P, 3, KT, 512], F32, rest)
        hid_hi = at("hid_hi", [P, KT, TOK], F32R, rest)
        hid_lo = at("hid_lo", [P, KT, TOK], F32R, rest + size(KT, TOK))
        tmp_a = at("tmp_a", [P, 2, TOK], F32, scr)
        tmp_b = at("tmp_b", [P, 2, TOK], F32, scr + size(2, TOK))
        ssum = at("ssum", [P, TOK], F32, scr + size(4, TOK))
        diag = at("diag", [P, NT, P], F32, scr + size(5, TOK))
        assert scr + size(6, TOK) <= mod_at

        q0 = at("q0", [P, 4, TOK], F32, x_at)
        k0 = at("k0", [P, 4, TOK], F32, x_at + size(4, TOK))
        f_hi = at("f_hi", [P, 4, TOK], F32R, rest)
        f_lo = at("f_lo", [P, 4, TOK], F32R, rest + size(4, TOK))
        y_hi, y_lo = f_hi, f_lo
        u_at = rest + 2 * size(4, TOK)
        u_hi = at("u_hi", [P, NT, 4, 256], F32R, u_at)
        u_lo = at("u_lo", [P, NT, 4, 256], F32R, u_at + size(NT, 4, 256))
        dft_raw = at("dft_raw", [P, 256], F32, u_at)
        assert u_at + 2 * size(NT, 4, 256) <= mod_at + size(512)
        v0 = at("v0", [P, NT, HEADS, P], F32R, u_at)
        v0s = at("v0s", [P, 3, HEADS, P], F32R, u_at + size(NT, 1024))
        pr_at = u_at + size(NT + 3, 1024)
        prob0 = at("prob0", [P, PROBS, 512], F32, pr_at)
        pt0 = at("pt0", [P, 2, 4, 256], F32R, pr_at + size(PROBS, 512))
        osum = at("osum", [P, 2, TOK], F32, pr_at + size(PROBS, 512) + size(2, 1024))
        o0_hi = at("o0_hi", [P, 4, TOK], F32R, a_at)
        o0_lo = at("o0_lo", [P, 4, TOK], F32R, a_at + size(4, TOK))
        j_at = a_at + size(8, TOK)
        q2a = at("q2a", [P, 2, TOK], F32R, j_at)
        q2b = at("q2b", [P, 2, TOK], F32R, j_at + size(2, TOK))
        k2 = at("k2", [P, 2, TOK], F32R, j_at + size(4, TOK))
        bias = at("bias", [P, 2, 3, 256], F32, j_at + size(6, TOK))
        bias_lo = at("bias_lo", [P, 2, 3, 256], F32R, j_at + size(6, TOK))
        tail = pr_at + size(PROBS, 512) + size(2, 1024) + size(2, TOK)
        ident_r = at("ident_r", [P, P], F32R, tail + size(256))
        assert tail + size(256) + size(P) <= 229360
        bias_hi = [at(f"bias_hi{v}", [P, 256], F32R, [dft_at, dft_at + size(256), tail][v]) for v in range(3)]
        assert size(8, TOK) + size(6, TOK) + size(2, 768) <= size(16, TOK)
        mask = at("mask", [P, 3, 32], F32, c_off[0]) if c_off[0] + size(96) <= rest else None
        assert mask is not None

        q1 = at("q1", [P, HEADS, LAT], F32, rest)
        k1 = at("k1", [P, HEADS, TOK], F32, rest + size(HEADS, LAT))
        v1 = at("v1", [P, NT, D], F32, rest + size(HEADS, LAT + TOK))
        cs_at = rest + size(HEADS, LAT + TOK) + size(NT, D)
        cosb = at("cosb", [P, LAT], F32, cs_at)
        sinb = at("sinb", [P, LAT], F32, cs_at + size(LAT))
        rt = at("rt", [P, 3, LAT], F32, cs_at + size(2, LAT))
        o_raw = at("o_raw", [P, HEADS, LAT], F32, a_at)
        b_at = a_at + size(HEADS, LAT)
        c_at = b_at + size(4, LAT) + size(4, TOK)
        odd = [rest, rest + size(HEADS, LAT), dft_at, x_at + size(KT, LAT) + size(NT, 256)]
        q_at = [[b_at + size(i, LAT) for i in range(4)], odd]
        k_at = [b_at + size(4, LAT), c_at + size(NT, 256)]
        aq2a = [[at(f"aq2a_{p}{i}", [P, LAT], F32R, q_at[p][i]) for i in range(2)] for p in range(2)]
        aq2b = [[at(f"aq2b_{p}{i}", [P, LAT], F32R, q_at[p][2 + i]) for i in range(2)] for p in range(2)]
        ak2 = [[at(f"ak2_{p}{i}", [P, TOK], F32R, k_at[p] + size(i, TOK)) for i in range(2)] for p in range(2)]
        avh = at("avh", [P, NT, P], F32R, b_at + size(4, LAT) + size(2, TOK))
        avl = at("avl", [P, NT, P], F32R, b_at + size(4, LAT) + size(3, TOK))
        aprob = at("aprob", [P, 3, 2, TOK], F32, cs_at)
        at_hi = at("at_hi", [P, NT, 256], F32R, c_at)
        assert c_at + size(NT, 256) + size(2, TOK) <= raw_at
        at_lo = at("at_lo", [P, NT, 256], F32R, x_at + size(KT, LAT))
        assert cs_at + size(6, TOK) <= 229360
        o1_hi = at("o1_hi", [P, HEADS, LAT], F32R, rest)
        o1_lo = at("o1_lo", [P, HEADS, LAT], F32R, rest + size(HEADS, LAT))
        sub_r = at("sub_r", [P, 2, LAT], F32, rest + size(2, HEADS, LAT))
        osq = at("osq", [P, 2, LAT], F32, rest + size(2, HEADS, LAT) + size(2, LAT))
        oneh = at("oneh", [P, HEADS, HEADS], F32, rest + size(2, HEADS, LAT) + size(4, LAT))
        selh = at("selh", [HEADS, HEADS, P], F32, rest + size(2, HEADS, LAT) + size(5, LAT))

        ps = ctx.enter_context(nc.psum_tensor("ps", [P, 8, 512], F32))

        def sem(name):
            return ctx.enter_context(nc.semaphore(name))

        consts_in = sem("consts_in")
        x_in = sem("x_in")
        xr_in = sem("xr_in")
        table_in = sem("table_in")
        shift_in = sem("shift_in")
        oneh_in = sem("oneh_in")
        hi_made = sem("hi_made")
        lo_made = sem("lo_made")
        unit_done = sem("unit_done")
        mod_used = sem("mod_used")
        mod_summed = sem("mod_summed")
        mod_rows = sem("mod_rows")
        mod_done = sem("mod_done")
        exp_c = sem("exp_c")
        cact_ok = sem("cact_ok")
        half_summed = sem("half_summed")
        half_out = sem("half_out")
        half_turned = sem("half_turned")
        ones_ok = sem("ones_ok")
        lam_mm = sem("lam_mm")
        lam_exp = sem("lam_exp")
        lam_ok = sem("lam_ok")
        relu_made = sem("relu_made")
        relu_used = sem("relu_used")
        hid_made = sem("hid_made")
        x_added = sem("x_added")
        sq_made = sem("sq_made")
        sq_summed = sem("sq_summed")
        norm_sum = sem("norm_sum")
        norm_sqrt = sem("norm_sqrt")
        norm_diag = sem("norm_diag")
        norm_rows = sem("norm_rows")
        t_made = sem("t_made")
        aff_made = sem("aff_made")
        hh_made = sem("hh_made")
        h_made = sem("h_made")
        out_made = sem("out_made")
        dsteps = sem("dsteps")
        f_hi_s = sem("f_hi_s")
        f_out = sem("f_out")
        qk_out = sem("qk_out")
        dft_hi_s = sem("dft_hi_s")
        dft_lo_s = sem("dft_lo_s")
        u_mm = sem("u_mm")
        u_hi_s = sem("u_hi_s")
        u_lo_s = sem("u_lo_s")
        y_hi_s = sem("y_hi_s")
        y_lo_s = sem("y_lo_s")
        v0_hi_s = sem("v0_hi_s")
        v0_lo_s = sem("v0_lo_s")
        bias_ok = sem("bias_ok")
        jh = sem("jh")
        jl = sem("jl")
        jk = sem("jk")
        js = sem("js")
        s_made = sem("s_made")
        m_made = sem("m_made")
        e_made = sem("e_made")
        p_made = sem("p_made")
        tr_made = sem("tr_made")
        th_made = sem("th_made")
        tl_made = sem("tl_made")
        pv_made = sem("pv_made")
        ident_ok = sem("ident_ok")
        bh_made = sem("bh_made")
        bl_made = sem("bl_made")
        kh0 = sem("kh0")
        oh_made = sem("oh_made")
        oc_made = sem("oc_made")
        od_made = sem("od_made")
        ol_made = sem("ol_made")
        rope_read = sem("rope_read")
        rope_done = sem("rope_done")
        kc_out = sem("kc_out")
        v1_out = sem("v1_out")
        jh1 = sem("jh1")
        jl1 = sem("jl1")
        jk1 = sem("jk1")
        kh1 = sem("kh1")
        js1 = sem("js1")
        vh1 = sem("vh1")
        vl1 = sem("vl1")
        s1 = sem("s1")
        m1 = sem("m1")
        e1 = sem("e1")
        c1 = sem("c1")
        g1 = sem("g1")
        a1 = sem("a1")
        tr1 = sem("tr1")
        th1 = sem("th1")
        tl1 = sem("tl1")
        pv1 = sem("pv1")
        o1 = sem("o1")
        sub_sq = sem("sub_sq")
        sub_mm = sem("sub_mm")
        sub_sqrt = sem("sub_sqrt")
        sub_rec = sem("sub_rec")
        sub_bc = sem("sub_bc")
        sub_t = sem("sub_t")
        sub_hi = sem("sub_hi")
        sub_lo = sem("sub_lo")
        big_in = [[sem(f"big_in{i}{j}") for j in range(2)] for i in range(3)]
        raw_in = [sem(f"raw_in{i}") for i in range(SLOTS)]
        mod_in = [sem(f"mod_in{i}") for i in range(RING)]
        bias_in = [sem(f"bias_in{i}") for i in range(2)]
        out_sem = [sem(f"out_sem{i}") for i in range(2)]

        pv_ps = ps[:, 5:8].rearrange("p b (t c) -> p (b t) c", c=256)

        def ps2(b):
            return ps[:, b:b + 2].rearrange("p a b -> p (a b)")[:, 0:TOK]

        def gate(layer, chunk, v, k):
            m = 12 * layer + 2 * chunk + k // 4
            return mods[:, m, v, k % 4:k % 4 + 1]

        def xa(layer, b, i):
            return 40 * layer + 8 + 8 * b + i

        def ha(layer, b, i):
            return 32 * layer + 8 * b + i

        both = ((0, 0, LAT), (1, LAT, CTX))
        V_BANK = [0, 1, 2, 3, 6, 7]
        NORM_TOK = [TOK, TOK, TOK, LAT, LAT]
        PAIRS = LAT // 256

        def parts(n):
            return [(xl, 0, slice(0, LAT))] + ([(xc, 1, slice(LAT, TOK))] if n == TOK else [])

        block = ctx.enter_context(nc.Block())

        @block.sync
        def _(sp):
            for dst, name in ((cond, "cond"), (ident, "ident"), (b_mod, "b_mod"), (gains, "gains"),
                              (mask, "mask"), (lam_in, "lam"), (subg, "subln")):
                sp.dma_start(dst[:], t[name]).then_inc(consts_in, 16)
            for m in range(4):
                if m == 3:
                    sp.wait_ge(half_summed, 1)
                for j in range(2):
                    sl = slice(4 * j, 4 * j + 4)
                    sp.dma_start(big[:, m % 3, sl], t["w_mod"][m][:, sl]).then_inc(big_in[m % 3][j], 16)
                if m == 1:
                    sp.dma_start(xl[:], t["x"]).then_inc(x_in, 16)
                    sp.dma_start(xc[:], t["ctx"]).then_inc(x_in, 16)

            def load_unit(u, s, first=False):
                if not first:
                    sp.wait_ge(lo_made, u - (SLOTS - 1))
                src = t["units"][bass.ds(u, 1)].rearrange("o p n -> p (o n)")
                sp.dma_start(raw[:, s], src).then_inc(raw_in[s], 16)

            def load_mod(m, k):
                n = 8 * (m - 4) + k
                if not isinstance(n, int) or n >= RING:
                    sp.wait_ge(mod_used, n - (RING - 1))
                src = t["w_mod"][bass.ds(m, 1), :, k, :].rearrange("o p n -> p (o n)")
                sp.dma_start(mod_ring[:, k % RING], src).then_inc(mod_in[k % RING], 16)

            for u in range(SLOTS):
                load_unit(u, u, True)
            for m, k in mix_mods(-1)[:RING]:
                load_mod(m, k)
            sp.wait_ge(h_made, KT)
            sp.dma_start(dft_raw[:], t["dft128"]).then_inc(table_in, 16)
            for u in range(FIRST["out0"]):
                load_unit(u + SLOTS, u % SLOTS)
                for m, k in (mix_mods(-1)[RING:] if u == 0 else mix_mods(u - 1) if u <= FIRST["dft"] else ()):
                    load_mod(m, k)
            for h in range(HEADS):
                if h == 0:
                    sp.wait_ge(unit_done, FIRST["out0"])
                if h == 1:
                    sp.wait_ge(v0_lo_s, NT)
                    for j in range(3):
                        sp.dma_start(v0s[0:64, j].bitcast(F32), v0[64:128, j].bitcast(F32)).then_inc(shift_in, 16)
                        sp.dma_start(v0s[64:128, j].bitcast(F32), v0[0:64, j + 1].bitcast(F32)).then_inc(shift_in, 16)
                if h >= 2:
                    sp.wait_ge(s_made, 6 * (h - 1) - 2)
                sp.dma_start(bias[:, h % 2], t["bias"][h]).then_inc(bias_in[h % 2], 16)
            sp.wait_ge(jk, HEADS)
            sp.wait_ge(jl, HEADS)
            sp.dma_start(xl[:], t["x"]).then_inc(xr_in, 16)
            sp.dma_start(xc[:], t["ctx"]).then_inc(xr_in, 16)
            sp.wait_ge(ol_made, HEADS)
            for i in range(FIRST["mlp0"] - FIRST["out0"]):
                u = FIRST["out0"] + i
                load_unit(u + SLOTS, u % SLOTS)
                for m, k in out_mods(i):
                    load_mod(m, k)

            def mlp_loads(layer, b, mod):
                for i in range(16):
                    u = FIRST[f"mlp{layer}"] + i
                    load_unit(u + SLOTS + 16 * b, u % SLOTS)
                    for k in (MOD_AT[i % 4] if mod else ()):
                        load_mod(12 + 4 * b + i // 4, k)

            with sp.Fori(0, HID_BLOCKS - 1) as b:
                mlp_loads(0, b, True)
            mlp_loads(0, HID_BLOCKS - 1, False)
            sp.wait_ge(h_made, 3 * KT)
            sp.dma_start(cosb[:], t["cos"]).then_inc(table_in, 16)
            sp.dma_start(sinb[:], t["sin"]).then_inc(table_in, 16)
            for u in range(FIRST["k1"], FIRST["out1"]):
                load_unit(u + SLOTS, u % SLOTS)
            sp.wait_ge(o1, HEADS * PAIRS)
            sp.dma_start(oneh[:], t["oneh"]).then_inc(oneh_in, 16)
            sp.dma_start(selh[:], t["selh"]).then_inc(oneh_in, 16)
            for u in range(FIRST["out1"], FIRST["mlp1"]):
                load_unit(u + SLOTS, u % SLOTS)
            with sp.Fori(0, HID_BLOCKS - 1) as b:
                mlp_loads(1, b, False)
            for i in range(16 - SLOTS):
                u = FIRST["mlp1"] + i
                load_unit(u + SLOTS + 48, u % SLOTS)
            for k in range(KT):
                sp.wait_ge(out_made, k + 1)
                sp.dma_start(t["out"][:, k], tmp_b[:, k % 2, 0:LAT]).then_inc(out_sem[k % 2], 16)
            for s in out_sem:
                sp.wait_ge(s, 16 * KT // 2)

        @block.gpsimd
        def _(pool):
            def low(u, s):
                pool.wait_ge(hi_made, u + 1)
                nc.gpsimd.tensor_tensor(w_lo[:, s], raw[:, s], w_hi[:, s].bitcast(F32),
                                        op=ALU.subtract).then_inc(lo_made, 1)

            def lows(first, last):
                for u in range(first + AHEAD, last + AHEAD):
                    low(u, u % SLOTS)

            def norm(i):
                pool.wait_ge(h_made, KT * i + 1)
                for k in range(1, KT):
                    pool.wait_ge(hh_made, KT * i + k + 1)
                    nc.gpsimd.tensor_tensor(h_lo[:, k, 0:NORM_TOK[i]], tmp_b[:, k % 2, 0:NORM_TOK[i]],
                                            h_hi[:, k, 0:NORM_TOK[i]].bitcast(F32),
                                            op=ALU.subtract).then_inc(h_made, 1)

            def mlp(layer):
                with pool.Fori(0, HID_BLOCKS - 1) as b:
                    for i in range(16):
                        u = FIRST[f"mlp{layer}"] + AHEAD + i
                        low(u + 16 * b, u % SLOTS)
                for i in range(16 if layer == 0 else 16 - AHEAD):
                    u = FIRST[f"mlp{layer}"] + AHEAD + i
                    low(u + 48, u % SLOTS)

            for u in range(AHEAD):
                low(u, u)
            norm(0)
            lows(FIRST["f"], FIRST["out0"])
            def out_low(h):
                e = 64 * (h % 2)
                pool.wait_ge(oh_made, 3 * h + 3)
                nc.gpsimd.tensor_tensor(o0_lo[e:e + 64, h // 2], osum[e:e + 64, h % 2],
                                        o0_hi[e:e + 64, h // 2].bitcast(F32), op=ALU.subtract).then_inc(ol_made, 1)
                pool.wait_ge(ol_made, h + 1)

            for h in range(HEADS):
                e = 64 * (h % 2)
                pool.wait_ge(bias_in[h % 2], 16 * (h // 2 + 1))
                bv = bias[:, h % 2].rearrange("p v (c r) -> p v c r", r=ROWS)
                for v in range(3):
                    ins = nc.gpsimd.tensor_tensor(bv[:, v], mask[:, v].unsqueeze(2).broadcast_to([P, 32, ROWS]),
                                                  bv[:, v], op=ALU.subtract)
                ins.then_inc(bias_ok, 1)
                pool.wait_ge(bias_ok, h + 1)
                pool.wait_ge(jh, h + 1)
                nc.gpsimd.tensor_tensor(q2b[e:e + 64, h % 2], q0[e:e + 64, h // 2],
                                        q2a[e:e + 64, h % 2].bitcast(F32), op=ALU.subtract).then_inc(jl, 1)
                pool.wait_ge(jl, h + 1)
                for v in range(3):
                    pool.wait_ge(bh_made, 3 * h + v + 1)
                    nc.gpsimd.tensor_tensor(bias_lo[:, h % 2, v], bias[:, h % 2, v], bias_hi[v][:].bitcast(F32),
                                            op=ALU.subtract).then_inc(bl_made, 1)
                pool.wait_ge(bl_made, 3 * h + 3)
                if h >= 2:
                    out_low(h - 2)
            for h in (HEADS - 2, HEADS - 1):
                out_low(h)
            lows(FIRST["out0"], FIRST["mlp0"])
            norm(1)
            mlp(0)
            norm(2)
            lows(FIRST["k1"], FIRST["out1"])
            pool.wait_ge(lo_made, FIRST["out1"] + AHEAD)

            def queries1(h):
                for i in range(2):
                    e = 64 * i
                    if h == 1 and i == 0:
                        pool.wait_ge(jk1, 2)
                    if h >= 2 and i == 0:
                        pool.wait_ge(s1, 8 * (h - 1))
                    nc.gpsimd.tensor_copy(aq2a[h % 2][i][e:e + 64], q1[e:e + 64, h]).then_inc(jh1, 1)
                    pool.wait_ge(jh1, 2 * h + i + 1)
                    nc.gpsimd.tensor_tensor(aq2b[h % 2][i][e:e + 64], q1[e:e + 64, h],
                                            aq2a[h % 2][i][e:e + 64].bitcast(F32), op=ALU.subtract).then_inc(jl1, 1)
                    pool.wait_ge(jl1, 2 * h + i + 1)

            def values1(h):
                if h:
                    pool.wait_ge(pv1, 2 * h)
                nc.gpsimd.tensor_copy(avh[:], v1[:, :, P * h:P * h + P]).then_inc(vh1, 1)
                pool.wait_ge(vh1, h + 1)
                nc.gpsimd.tensor_tensor(avl[:], v1[:, :, P * h:P * h + P], avh[:].bitcast(F32),
                                        op=ALU.subtract).then_inc(vl1, 1)
                pool.wait_ge(vl1, h + 1)

            pool.wait_ge(unit_done, FIRST["out1"])
            pool.wait_ge(rope_done, 1)
            queries1(0)
            for h in range(HEADS):
                if h + 1 < HEADS:
                    queries1(h + 1)
                if h == 0:
                    pool.wait_ge(v1_out, 2 * NT)
                values1(h)
            lows(FIRST["out1"], FIRST["mlp1"])
            norm(3)
            mlp(1)

        @block.scalar
        def _(act):
            def high(u, s, n):
                act.wait_ge(raw_in[s], n)
                if isinstance(u, int) and u < SLOTS:
                    pass
                else:
                    act.wait_ge(unit_done, u - (SLOTS - 1))
                nc.scalar.activation(w_hi[:, s], raw[:, s], ACT.Copy).then_inc(hi_made, 1)

            def high_u(u):
                high(u, u % SLOTS, 16 * (u // SLOTS + 1))

            def high_b(u, b):
                high(u + 16 * b, u % SLOTS, 64 * b + 16 * (u // SLOTS + 1))

            def squares(i, m):
                n = KT * i + m
                if n >= 2:
                    act.wait_ge(sq_summed, n - 1)
                for x, _, cols in parts(NORM_TOK[i]):
                    ins = nc.scalar.activation(tmp_b[:, m % 2, cols], x[:, m], ACT.Square)
                ins.then_inc(sq_made, 1)

            def norm_root(i):
                n = NORM_TOK[i]
                act.wait_ge(norm_sum, i + 1)
                nc.scalar.activation(stat[:, 40:40 + n // P], ps[:, 6, 0:n // P],
                                     ACT.Sqrt, bias=eps_c[:, 0:1], scale=1.0 / D).then_inc(norm_sqrt, 1)

            def norm(i, root=True):
                n = NORM_TOK[i]
                if root:
                    norm_root(i)
                for k in range(KT):
                    act.wait_ge(t_made, KT * i + k + 1)
                    if i == 4:
                        if k >= 2:
                            act.wait_ge(out_sem[k % 2], 16 * (k // 2))
                        nc.scalar.activation(tmp_b[:, k % 2, 0:n], tmp_a[:, k % 2, 0:n], ACT.Copy,
                                             scale=gains[:, 4, k:k + 1]).then_inc(out_made, 1)
                        continue
                    if k >= 2:
                        act.wait_ge(h_made, KT * i + k - 1)
                    for _, v, cols in parts(n):
                        ins = nc.scalar.activation(tmp_b[:, k % 2, cols], tmp_a[:, k % 2, cols], ACT.Identity,
                                                   scale=gs[:, i, v, k:k + 1],
                                                   bias=gate(i // 2, 3 * (i % 2), v, k))
                    ins.then_inc(aff_made, 1)

            def mlp(layer):
                u0 = FIRST[f"mlp{layer}"]

                def blk(b, last):
                    for i in range(16):
                        u = u0 + i
                        if not (last and layer == 1 and i + AHEAD >= 16):
                            high_b(u + AHEAD, b)
                        if i < 8:
                            act.wait_ge(unit_done, u + 16 * b + 1)
                            a = ha(layer, b, i)
                            if i >= 2:
                                act.wait_ge(relu_used, a - 1)
                            for bank, c0, n in both[:2 - layer]:
                                ins = nc.scalar.activation(tmp_a[:, i % 2, c0:c0 + n],
                                                           ps[:, 2 * (u % 2) + bank, 0:n], ACT.Relu)
                            ins.then_inc(relu_made, 1)
                        elif last:
                            act.wait_ge(x_added, xa(layer, b, i - 8) + 1)
                            squares(2 + 2 * layer, i - 8)

                with act.Fori(0, HID_BLOCKS - 1) as b:
                    blk(b, False)
                blk(HID_BLOCKS - 1, True)

            act.wait_ge(consts_in, 16 * 7)
            nc.scalar.activation(ctmp[:], cond[:], ACT.Exp, scale=-1.0).then_inc(exp_c, 1)
            act.wait_ge(lam_mm, 1)
            nc.scalar.activation(lam_t[:, 2:4], ps[:, 6, 0:2], ACT.Exp).then_inc(lam_exp, 1)

            def half_rows(m):
                act.wait_ge(half_summed, m + 1)
                if m >= 2:
                    act.wait_ge(half_turned, m - 1)
                nc.scalar.activation(mod_acc[0:2, m % 2], ps[0:2, m % 2], ACT.Copy).then_inc(half_out, 1)

            half_rows(0)
            half_rows(1)
            act.wait_ge(x_in, 32)
            for m in range(KT):
                squares(0, m)
            half_rows(2)
            norm_root(0)
            high_u(0)
            high_u(1)
            half_rows(3)
            high_u(2)
            norm(0, root=False)
            for i in range(4):
                u = FIRST["f"] + i
                high_u(u + AHEAD)
                act.wait_ge(unit_done, u + 1)
                for bank, c0, n in both:
                    ins = nc.scalar.activation(f_hi[:, i, c0:c0 + n], ps[:, 2 * (u % 2) + bank, 0:n], ACT.Copy)
                ins.then_inc(f_hi_s, 1)
            for name, dst, scale in (("q0", q0, -1.0 / 8), ("k0", k0, 1.0)):
                for i in range(4):
                    u = FIRST[name] + i
                    high_u(u + AHEAD)
                    act.wait_ge(unit_done, u + 1)
                    for bank, c0, n in both:
                        ins = nc.scalar.activation(dst[:, i, c0:c0 + n], ps[:, 2 * (u % 2) + bank, 0:n],
                                                   ACT.Copy, scale=scale)
                    ins.then_inc(qk_out, 1)
            act.wait_ge(table_in, 16)
            nc.scalar.activation(dft_hi[:], dft_raw[:], ACT.Copy).then_inc(dft_hi_s, 1)
            act.wait_ge(dft_lo_s, 1)
            for n in range(2 * NT):
                act.wait_ge(u_mm, n + 1)
                nc.scalar.activation(u_hi[:, n // 2, 2 * (n % 2):2 * (n % 2) + 2].rearrange("p g c -> p (g c)"),
                                     ps[:, V_BANK[n % 6]], ACT.Copy).then_inc(u_hi_s, 1)
            for i in range(5):
                high_u(FIRST["dft"] + i + AHEAD)
            for g in range(4):
                act.wait_ge(unit_done, FIRST["dft"] + 4)
                nc.scalar.activation(y_hi[:, g, 0:LAT], ps[:, g], ACT.Copy).then_inc(y_hi_s, 1)
            for g in range(2):
                act.wait_ge(unit_done, FIRST["dft"] + 5)
                nc.scalar.activation(y_hi[:, 2 * g:2 * g + 2, LAT:TOK],
                                     ps[:, 6 + g].rearrange("p (g c) -> p g c", g=2), ACT.Copy).then_inc(y_hi_s, 1)
            for i in range(4):
                high_u(FIRST["v0"] + i + AHEAD)
            act.wait_ge(unit_done, FIRST["v0"] + 4)
            for n in range(NT):
                nc.scalar.activation(v0[:, n, :, 0:HD], ps[:, V_BANK[n]].rearrange("p (h d) -> p h d", d=HD),
                                     ACT.Copy).then_inc(v0_hi_s, 1)

            def swaps(h):
                e, o = 64 * (h % 2), 64 - 64 * (h % 2)
                act.wait_ge(jl, h + 1)
                nc.scalar.activation(q2a[o:o + 64, h % 2], q2b[e:e + 64, h % 2].bitcast(F32), ACT.Copy)
                nc.scalar.activation(q2b[o:o + 64, h % 2], q2a[e:e + 64, h % 2].bitcast(F32),
                                     ACT.Copy).then_inc(js, 1)

            def p_high(n):
                c = 4 if n % NT < 4 else 2
                act.wait_ge(tr_made, n + 1)
                if n >= 2:
                    act.wait_ge(pv_made, n - 1)
                nc.scalar.activation(pt0[:, n % 2, 0:c, 0:P], ps[:, 3 + n % 2, 0:128 * c].rearrange("p (c q) -> p c q", c=c),
                                     ACT.Copy).then_inc(th_made, 1)

            def bias_high(h, v):
                if h:
                    act.wait_ge(s_made, 6 * h - 2)
                act.wait_ge(bias_ok, h + 1)
                nc.scalar.activation(bias_hi[v][:], bias[:, h % 2, v], ACT.Copy).then_inc(bh_made, 1)

            def out_half(r):
                h, j, e = r // 3, r % 3, 64 * (r // 3 % 2)
                act.wait_ge(pv_made, 2 * r + 2)
                if h >= 2 and j == 0:
                    act.wait_ge(ol_made, h - 1)
                nc.scalar.activation(osum[e:e + 64, h % 2, 256 * j:256 * j + 256].rearrange("p (t q) -> p t q", q=P),
                                     pv_ps[64:128, 2 * j:2 * j + 2, 0:P], ACT.Copy).then_inc(oc_made, 1)

            def out_high(r):
                h, j, e = r // 3, r % 3, 64 * (r // 3 % 2)
                act.wait_ge(od_made, r + 1)
                sl = slice(256 * j, 256 * j + 256)
                nc.scalar.activation(o0_hi[e:e + 64, h // 2, sl], osum[e:e + 64, h % 2, sl], ACT.Copy).then_inc(oh_made, 1)

            act.wait_ge(unit_done, FIRST["out0"])
            act.wait_ge(mod_done, 10)
            nc.scalar.activation(ident_r[:], ident[:], ACT.Copy).then_inc(ident_ok, 1)
            for v in range(3):
                bias_high(0, v)
            swaps(0)
            N0 = 6 * HEADS
            for n in range(N0 + 5):
                h, t_ = n // 6, n % 6
                if n < N0:
                    act.wait_ge(m_made, n + 1)
                    if n >= PROBS:
                        act.wait_ge(tr_made, n - PROBS + 1)
                    w = 512 if t_ < 4 else 256
                    nc.scalar.activation(prob0[:, n % PROBS, 0:w], ps[:, n % 3, 0:w], ACT.Exp, scale=-1.0,
                                         bias=stat[:, n % 4:n % 4 + 1],
                                         accum_out=stat[:, 4 + n % 4:5 + n % 4]).then_inc(e_made, 1)
                if 1 <= n <= N0:
                    p_high(n - 1)
                if h + 1 < HEADS and t_ == 2:
                    swaps(h + 1)
                if h + 1 < HEADS and 2 <= t_ < 5:
                    bias_high(h + 1, t_ - 2)
                if n >= 5 and n % 2 == 1:
                    out_high((n - 5) // 2)
                if n >= 3 and n % 2 == 1 and n < N0 + 3:
                    out_half((n - 3) // 2)
            for i in range(8):
                u = FIRST["out0"] + i
                high_u(u + AHEAD)
                act.wait_ge(x_added, i + 1)
                squares(1, i)
            norm(1)
            mlp(0)
            norm(2)
            for i in range(16):
                u = FIRST["k1"] + i
                high_u(u + AHEAD)
                if i < 8:
                    act.wait_ge(unit_done, u + 1)
                    nc.scalar.activation(k1[:, i, LAT:TOK], ps[:, 2 * (u % 2) + 1, 0:CTX], ACT.Copy).then_inc(kc_out, 1)
            for j in range(2):
                for i in range(4):
                    high_u(FIRST["v1"] + 4 * j + i + AHEAD)
                act.wait_ge(unit_done, FIRST["v1"] + 4 * j + 4)
                if j == 0:
                    act.wait_ge(rope_done, 1)
                for n in range(NT):
                    nc.scalar.activation(v1[:, n, 512 * j:512 * j + 512], ps[:, V_BANK[n]], ACT.Copy).then_inc(v1_out, 1)

            def keys_high1(h, i):
                e = 64 * i
                if h >= 2 and i == 0:
                    act.wait_ge(s1, 8 * (h - 1))
                nc.scalar.activation(ak2[h % 2][i][e:e + 64], k1[e:e + 64, h], ACT.Copy).then_inc(kh1, 1)

            def swaps1(h, i):
                e, o, a, b = 64 * i, 64 - 64 * i, aq2a[h % 2][i], aq2b[h % 2][i]
                act.wait_ge(jl1, 2 * h + i + 1)
                nc.scalar.activation(a[o:o + 64], b[e:e + 64].bitcast(F32), ACT.Copy)
                nc.scalar.activation(b[o:o + 64], a[e:e + 64].bitcast(F32), ACT.Copy).then_inc(js1, 1)

            def p_high1(n):
                act.wait_ge(tr1, n + 1)
                if n % 2 == 0 and n >= 2:
                    act.wait_ge(pv1, n // 2)
                for j in range(2):
                    ins = nc.scalar.activation(at_hi[:, 3 * j:3 * j + 3, P * (n % 2):P * (n % 2) + P],
                                               ps[:, 4 + j, 0:384].rearrange("p (c q) -> p c q", c=3), ACT.Copy)
                ins.then_inc(th1, 1)

            def out_copy(m):
                act.wait_ge(pv1, m + 1)
                nc.scalar.activation(o_raw[:, m // 2, 256 * (m % 2):256 * (m % 2) + 256], ps[:, 6 + m % 2, 0:256],
                                     ACT.Copy).then_inc(o1, 1)

            def exps(n, i):
                act.wait_ge(m1, 2 * n + i + 1)
                if n >= 3 and i == 0:
                    act.wait_ge(tr1, n - 2)
                c = 16 + 2 * (n % 3) + i
                nc.scalar.activation(aprob[:, n % 3, i], ps2(2 * i), ACT.Exp, scale=-1.0,
                                     bias=stat[:, c:c + 1], accum_out=stat[:, c + 6:c + 7]).then_inc(e1, 1)

            def scale_second(n):
                act.wait_ge(c1, n + 1)
                c = 29 + 2 * (n % 3)
                nc.scalar.activation(aprob[:, n % 3, 1], aprob[:, n % 3, 1], ACT.Copy,
                                     scale=stat[:, c:c + 1]).then_inc(g1, 1)

            for i in range(2):
                keys_high1(0, i)
            for i in range(2):
                swaps1(0, i)
            N1 = 4 * HEADS
            for n in range(N1 + 5):
                h = n // 4
                if 1 <= n <= N1:
                    scale_second(n - 1)
                if n < N1:
                    exps(n, 0)
                if 2 <= n <= N1 + 1:
                    p_high1(n - 2)
                if n < N1:
                    exps(n, 1)
                if h + 1 < HEADS and n % 4 < 2:
                    keys_high1(h + 1, n % 4)
                if h + 1 < HEADS and 1 <= n % 4 < 3:
                    swaps1(h + 1, n % 4 - 1)
                if n >= 5 and n % 2 == 1:
                    out_copy((n - 5) // 2)
            for h in range(HEADS):
                if h >= 2:
                    act.wait_ge(sub_mm, h - 1)
                elif h == 0:
                    act.wait_ge(o1, HEADS * PAIRS)
                nc.scalar.activation(osq[:, h % 2], o_raw[:, h], ACT.Square).then_inc(sub_sq, 1)
            act.wait_ge(sub_mm, HEADS)
            nc.scalar.activation(sub_r[0:HEADS, 0], ps[0:HEADS, 0], ACT.Sqrt, bias=eps_c[0:HEADS, 1:2],
                                 scale=1.0 / P).then_inc(sub_sqrt, 1)
            for h in range(HEADS):
                act.wait_ge(sub_t, h + 1)
                nc.scalar.activation(o1_hi[:, h], osq[:, h % 2], ACT.Copy, scale=subg[:, 1:2]).then_inc(sub_hi, 1)
            for i in range(8):
                u = FIRST["out1"] + i
                high_u(u + AHEAD)
                act.wait_ge(x_added, 40 + i + 1)
                squares(3, i)
            norm(3)
            mlp(1)
            norm(4)

        @block.vector
        def _(dve):
            st = Steps(dve, dsteps)
            V = nc.vector
            tt = V.tensor_tensor

            def mod_step(k, target):
                dve.wait_ge(mod_in[k % RING], target)
                w = mod_ring[:, k % RING]
                for v in range(2):
                    if k == 0:
                        ins = V.tensor_scalar(mod_acc[:, v], w, cact[:, 0, v:v + 1], None, ALU.mult)
                    else:
                        dve.wait_ge(dsteps, st.n - 1)
                        ins = V.scalar_tensor_tensor(out=mod_acc[:, v], in0=w, scalar=cact[:, k, v:v + 1],
                                                     in1=mod_acc[:, v], op0=ALU.mult, op1=ALU.add)
                    ins.then_inc(dsteps, 1)
                    st.n = st.n + 1
                dve.wait_ge(dsteps, st.n)
                dve.sem_inc(mod_used, 1)
                if k == KT - 1:
                    dve.sem_inc(mod_summed, 1)

            def mod_steps(steps):
                for m, k in steps:
                    mod_step(k, 16 * ((8 * (m - 4) + k) // RING + 1))

            def extract(m):
                dve.wait_ge(mod_rows, m - 3)
                idb = ident[:].unsqueeze(1).broadcast_to([P, 4, P])
                acc = mod_acc[:].rearrange("p v (c q) -> p v c q", c=4)
                for v in range(2):
                    ins = tt(acc[:, v], ps[:, 4 + v].rearrange("p (c q) -> p c q", c=4), idb, op=ALU.mult)
                    ins.then_inc(dsteps, 1)
                    st.n = st.n + 1
                dve.wait_ge(dsteps, st.n)
                st.wait(V.tensor_reduce(modr[:], acc, AX.X, ALU.add))
                one = bass.ds(m, 1)
                for v in range(2):
                    ins = tt(mods[:, one, v, :], modr[:, v:v + 1, :], b_mod[:, one, :], op=ALU.add)
                ins.then_inc(mod_done, 1)

            def scales(i):
                m = 12 * (i // 2) + 2 * (1 + 3 * (i % 2))
                dve.wait_ge(mod_done, m + 2)
                for v in range(2):
                    ins = V.scalar_tensor_tensor(out=gs[:, i, v].rearrange("p (a b) -> p a b", a=2),
                                                 in0=mods[:, m:m + 2, v, :], scalar=1.0,
                                                 in1=gains[:, i].rearrange("p (a b) -> p a b", a=2),
                                                 op0=ALU.add, op1=ALU.mult)
                st.wait(ins)

            def sum_squares(i, m):
                n = NORM_TOK[i]
                dve.wait_ge(sq_made, KT * i + m + 1)
                if m == 0:
                    V.tensor_copy(ssum[:, 0:n], tmp_b[:, 0, 0:n]).then_inc(sq_summed, 1)
                else:
                    dve.wait_ge(sq_summed, KT * i + m)
                    tt(ssum[:, 0:n], ssum[:, 0:n], tmp_b[:, m % 2, 0:n], op=ALU.add).then_inc(sq_summed, 1)

            def norm_root(i):
                n = NORM_TOK[i]
                dve.wait_ge(norm_sqrt, i + 1)
                st.wait(V.reciprocal(stat[:, 48:48 + n // P], stat[:, 40:40 + n // P]))
                for c in range(n // P):
                    ins = V.tensor_scalar(diag[:, c], ident[:], stat[:, 48 + c:49 + c], None, ALU.mult)
                ins.then_inc(norm_diag, 1)

            def norm(i, root=True):
                n = NORM_TOK[i]
                if root:
                    norm_root(i)
                dve.wait_ge(norm_rows, i + 1)
                for k in range(KT + 1):
                    if k < KT:
                        if k >= 2:
                            dve.wait_ge(out_made if i == 4 else aff_made, (0 if i == 4 else KT * i) + k - 1)
                        for (x, v, cols), (bank, _, w) in zip(parts(n), both):
                            ins = tt(tmp_a[:, k % 2, cols], x[:, k], ps[:, 6 + bank, 0:w], op=ALU.mult)
                        ins.then_inc(t_made, 1)
                    if k >= 1 and i < 4:
                        dve.wait_ge(aff_made, KT * i + k)
                        V.tensor_copy(h_hi[:, k - 1, 0:n], tmp_b[:, (k - 1) % 2, 0:n]).then_inc(hh_made, 1)
                    if k == 1 and i < 4:
                        dve.wait_ge(hh_made, KT * i + 1)
                        tt(h_lo[:, 0, 0:n], tmp_b[:, 0, 0:n], h_hi[:, 0, 0:n].bitcast(F32),
                           op=ALU.subtract).then_inc(h_made, 1)

            def add_x(layer, u_wait, par, i, m, count):
                dve.wait_ge(unit_done, u_wait)
                if not isinstance(count, int) or count:
                    dve.wait_ge(x_added, count)
                for (x, v, _), (bank, _, n) in zip(parts(TOK if layer == 0 else LAT), both):
                    ins = V.scalar_tensor_tensor(out=x[:, i], in0=ps[:, 2 * par + bank, 0:n], scalar=gate(layer, m, v, i),
                                                 in1=x[:, i], op0=ALU.mult, op1=ALU.add)
                ins.then_inc(x_added, 1)

            def hidden(layer, b, i):
                a = ha(layer, b, i)
                n = TOK if layer == 0 else LAT
                dve.wait_ge(relu_made, a + 1)
                if i >= 2:
                    dve.wait_ge(hid_made, a - 1)
                ins = tt(tmp_b[:, i % 2, 0:n], tmp_a[:, i % 2, 0:n], tmp_a[:, i % 2, 0:n], op=ALU.mult)
                ins.then_inc(relu_used, 1)
                dve.wait_ge(relu_used, a + 1)
                st.wait(V.tensor_copy(hid_hi[:, i, 0:n], tmp_b[:, i % 2, 0:n]))
                tt(hid_lo[:, i, 0:n], tmp_b[:, i % 2, 0:n], hid_hi[:, i, 0:n].bitcast(F32),
                   op=ALU.subtract).then_inc(hid_made, 1)

            def mlp(layer):
                u0 = FIRST[f"mlp{layer}"]

                def blk(b, last):
                    for i in range(16):
                        u = u0 + i
                        def steps():
                            for k in MOD_AT[i % 4]:
                                mod_step(k, 16 * ((8 * (8 + i // 4) + k) // RING + 1) + 8 * 16 * b)

                        mod = layer == 0 and not last
                        if mod and i == 0:
                            steps()
                        if i < 8:
                            hidden(layer, b, i)
                        else:
                            add_x(layer, u + 16 * b + 1, u % 2, i - 8, 5, xa(layer, b, i - 8))
                            if last and i > 8:
                                sum_squares(2 + 2 * layer, i - 9)
                        if mod:
                            if i:
                                steps()
                            if i % 4 == 3:
                                extract(12 + i // 4 + 4 * b)
                    if last:
                        sum_squares(2 + 2 * layer, 7)

                if layer == 0:
                    per = 8 + 4 * (16 + 3)
                else:
                    per = 8
                with st.loop(HID_BLOCKS - 1, per) as b:
                    blk(b, False)
                blk(HID_BLOCKS - 1, True)

            st.wait(V.memset(ones[:], 1.0))
            V.memset(eps_c[:, 0:1], EPS)
            st.wait(V.memset(eps_c[:, 1:2], SUB_EPS))
            dve.sem_inc(ones_ok, 1)
            dve.wait_ge(consts_in, 16 * 7)
            lam = lam_in[:].rearrange("p (a b) -> p a b", b=2)
            tt(lam_t[0:HD, 0:2], lam[:, :, 0], lam[:, :, 1], op=ALU.mult).then_inc(lam_ok, 1)
            dve.wait_ge(exp_c, 1)
            st.wait(V.tensor_scalar(ctmp[:], ctmp[:], 1.0, None, ALU.add))
            st.wait(V.reciprocal(ctmp[:], ctmp[:]))
            tt(cact[:], cond[:], ctmp[:], op=ALU.mult).then_inc(cact_ok, 1)
            dve.wait_ge(cact_ok, 1)
            V.tensor_scalar(subg[:, 1:2], subg[:, 0:1], 1.0 - LAM_INIT, None, ALU.mult)
            dve.wait_ge(lam_exp, 1)
            st.wait(V.scalar_tensor_tensor(out=lam_t[:, 4:5], in0=lam_t[:, 3:4], scalar=LAM_INIT,
                                           in1=lam_t[:, 2:3], op0=ALU.subtract, op1=ALU.subtract))
            def half_add(m):
                dve.wait_ge(half_turned, m + 1)
                tt(mods[:, m], ps[:, 2 + m % 2, 0:8].rearrange("p (c v) -> p v c", v=2),
                   b_mod[:, m].unsqueeze(1).broadcast_to([P, 2, 4]), op=ALU.add).then_inc(mod_done, 1)

            half_add(0)
            for k in range(KT):
                sum_squares(0, k)
            half_add(1)
            norm_root(0)
            half_add(2)
            half_add(3)
            scales(0)
            norm(0, root=False)
            mod_steps(mix_mods(-1))
            for i in range(12):
                u = FIRST["f"] + i
                if i < 4:
                    dve.wait_ge(f_hi_s, i + 1)
                    for bank, c0, n in both:
                        ins = tt(f_lo[:, i, c0:c0 + n], ps[:, 2 * (u % 2) + bank, 0:n],
                                 f_hi[:, i, c0:c0 + n].bitcast(F32), op=ALU.subtract)
                    ins.then_inc(f_out, 1)
                if i == 1:
                    extract(4)
                elif i >= 4 and i % 2 == 0:
                    extract(3 + i // 2)
                mod_steps(mix_mods(i))
            dve.wait_ge(dft_hi_s, 1)
            tt(dft_lo[:], dft_raw[:], dft_hi[:].bitcast(F32), op=ALU.subtract).then_inc(dft_lo_s, 1)
            dve.wait_ge(dft_lo_s, 1)
            for n in range(2 * NT):
                sl = slice(2 * (n % 2), 2 * (n % 2) + 2)
                dve.wait_ge(u_hi_s, n + 1)
                tt(u_lo[:, n // 2, sl].rearrange("p g c -> p (g c)"), ps[:, V_BANK[n % 6]],
                   u_hi[:, n // 2, sl].rearrange("p g c -> p (g c)").bitcast(F32), op=ALU.subtract).then_inc(u_lo_s, 1)
            extract(9)
            scales(1)
            for g in range(4):
                dve.wait_ge(y_hi_s, g + 1)
                tt(y_lo[:, g, 0:LAT], ps[:, g], y_hi[:, g, 0:LAT].bitcast(F32), op=ALU.subtract).then_inc(y_lo_s, 1)
            for g in range(2):
                dve.wait_ge(y_hi_s, 5 + g)
                sl = slice(2 * g, 2 * g + 2)
                tt(y_lo[:, sl, LAT:TOK], ps[:, 6 + g].rearrange("p (g c) -> p g c", g=2),
                   y_hi[:, sl, LAT:TOK].bitcast(F32), op=ALU.subtract).then_inc(y_lo_s, 1)
            for n in range(NT):
                dve.wait_ge(v0_hi_s, n + 1)
                tt(v0[:, n, :, HD:P], ps[:, V_BANK[n]].rearrange("p (h d) -> p h d", d=HD),
                   v0[:, n, :, 0:HD].bitcast(F32), op=ALU.subtract).then_inc(v0_lo_s, 1)

            def heads_high(h):
                e, p = 64 * (h % 2), h % 2
                if h >= 2:
                    dve.wait_ge(s_made, 6 * (h - 1))
                V.tensor_copy(q2a[e:e + 64, p], q0[e:e + 64, h // 2]).then_inc(jh, 1)
                V.tensor_copy(k2[e:e + 64, p], k0[e:e + 64, h // 2]).then_inc(kh0, 1)

            def keys_low(h):
                e, o, p = 64 * (h % 2), 64 - 64 * (h % 2), h % 2
                dve.wait_ge(kh0, h + 1)
                tt(k2[o:o + 64, p], k0[e:e + 64, h // 2], k2[e:e + 64, p].bitcast(F32), op=ALU.subtract).then_inc(jk, 1)

            def least(n):
                dve.wait_ge(s_made, n + 1)
                w = 512 if n % 6 < 4 else 256
                V.tensor_reduce(stat[:, n % 4:n % 4 + 1], ps[:, n % 3, 0:w], AX.X, ALU.min).then_inc(m_made, 1)

            def normalise(n):
                w = 512 if n % 6 < 4 else 256
                dve.wait_ge(e_made, n + 1)
                st.wait(V.reciprocal(stat[:, 8 + n % 4:9 + n % 4], stat[:, 4 + n % 4:5 + n % 4]))
                V.tensor_scalar(prob0[:, n % PROBS, 0:w], prob0[:, n % PROBS, 0:w], stat[:, 8 + n % 4:9 + n % 4],
                                None, ALU.mult).then_inc(p_made, 1)

            def p_low(n):
                c = 4 if n % 6 < 4 else 2
                dve.wait_ge(th_made, n + 1)
                tt(pt0[:, n % 2, 0:c, P:2 * P], ps[:, 3 + n % 2, 0:P * c].rearrange("p (c q) -> p c q", c=c),
                   pt0[:, n % 2, 0:c, 0:P].bitcast(F32), op=ALU.subtract).then_inc(tl_made, 1)

            def out_sum(r):
                h, j, e = r // 3, r % 3, 64 * (r // 3 % 2)
                dve.wait_ge(oc_made, r + 1)
                o = osum[e:e + 64, h % 2, 256 * j:256 * j + 256].rearrange("p (t q) -> p t q", q=P)
                st.wait(tt(o, pv_ps[0:64, 2 * j:2 * j + 2, 0:P], o, op=ALU.add))
                tt(o, pv_ps[0:64, 2 * j:2 * j + 2, P:2 * P], o, op=ALU.add).then_inc(od_made, 1)

            dve.wait_ge(unit_done, FIRST["out0"])
            heads_high(0)
            keys_low(0)
            N0 = 6 * HEADS
            for n in range(N0 + 3):
                h, t_ = n // 6, n % 6
                if n < N0:
                    least(n)
                if 1 <= n <= N0:
                    normalise(n - 1)
                if 2 <= n <= N0 + 1:
                    p_low(n - 2)
                if n >= 4 and n % 2 == 0:
                    out_sum((n - 4) // 2)
                if h + 1 < HEADS and t_ == 0:
                    heads_high(h + 1)
                if h + 1 < HEADS and t_ == 1:
                    keys_low(h + 1)
            dve.wait_ge(xr_in, 32)
            for i in range(8):
                u = FIRST["out0"] + i
                add_x(0, u + 1, u % 2, i, 2, i)
                if i:
                    sum_squares(1, i - 1)
                if i in (3, 6):
                    extract(9 + i // 3)
                mod_steps(out_mods(i))
            sum_squares(1, 7)
            norm(1)
            mlp(0)
            scales(2)
            norm(2)
            scales(3)
            dve.wait_ge(table_in, 16 * 3)
            swap = [(i + 16) % 32 for i in range(32)]
            for i in range(16):
                u = FIRST["k1"] + i
                src = ps[:, 2 * (u % 2), 0:LAT]
                dst = k1[:, i, 0:LAT] if i < 8 else q1[:, i - 8]
                f = 1.0 if i < 8 else -1.0 / 8
                dve.wait_ge(unit_done, u + 1)
                st.wait(V.stream_shuffle(rt[:, 0], src, swap))
                V.scalar_tensor_tensor(out=rt[:, 1], in0=src, scalar=f, in1=cosb[:], op0=ALU.mult,
                                       op1=ALU.mult).then_inc(rope_read, 1)
                st.wait(V.scalar_tensor_tensor(out=rt[:, 2], in0=rt[:, 0], scalar=f, in1=sinb[:], op0=ALU.mult, op1=ALU.mult))
                dve.wait_ge(rope_read, i + 1)
                st.wait(tt(dst, rt[:, 1], rt[:, 2], op=ALU.add))
            dve.sem_inc(rope_done, 1)

            def keys_low1(h, i):
                e, o = 64 * i, 64 - 64 * i
                dve.wait_ge(kh1, 2 * h + i + 1)
                tt(ak2[h % 2][i][o:o + 64], k1[e:e + 64, h], ak2[h % 2][i][e:e + 64].bitcast(F32),
                   op=ALU.subtract).then_inc(jk1, 1)

            def least1(n):
                for i in range(2):
                    dve.wait_ge(s1, 2 * n + i + 1)
                    c = 16 + 2 * (n % 3) + i
                    V.tensor_reduce(stat[:, c:c + 1], ps2(2 * i), AX.X, ALU.min).then_inc(m1, 1)

            def coef(n):
                dve.wait_ge(e1, 2 * n + 2)
                c, d = 22 + 2 * (n % 3), 28 + 2 * (n % 3)
                st.wait(V.reciprocal(stat[:, d:d + 2], stat[:, c:c + 2]))
                V.tensor_scalar(stat[:, d + 1:d + 2], stat[:, d + 1:d + 2], lam_t[:, 4:5], None, ALU.mult).then_inc(c1, 1)

            def combine(n):
                d = 28 + 2 * (n % 3)
                dve.wait_ge(g1, n + 1)
                V.scalar_tensor_tensor(out=aprob[:, n % 3, 0], in0=aprob[:, n % 3, 0], scalar=stat[:, d:d + 1],
                                       in1=aprob[:, n % 3, 1], op0=ALU.mult, op1=ALU.add).then_inc(a1, 1)

            def p_low1(n):
                dve.wait_ge(th1, n + 1)
                for j in range(2):
                    sl = (slice(None), slice(3 * j, 3 * j + 3), slice(P * (n % 2), P * (n % 2) + P))
                    ins = tt(at_lo[sl], ps[:, 4 + j, 0:384].rearrange("p (c q) -> p c q", c=3),
                             at_hi[sl].bitcast(F32), op=ALU.subtract)
                ins.then_inc(tl1, 1)

            dve.wait_ge(unit_done, FIRST["out1"])
            dve.wait_ge(v1_out, 2 * NT)
            dve.wait_ge(kc_out, 8)
            N1 = 4 * HEADS
            for i in range(2):
                keys_low1(0, i)
            for n in range(N1 + 2):
                if n < N1:
                    least1(n)
                if 1 <= n <= N1:
                    combine(n - 1)
                if n >= 2:
                    p_low1(n - 2)
                if n < N1:
                    coef(n)
                if n // 4 + 1 < HEADS and 1 <= n % 4 < 3:
                    keys_low1(n // 4 + 1, n % 4 - 1)
            dve.wait_ge(sub_sqrt, 1)
            V.reciprocal(sub_r[0:HEADS, 1], sub_r[0:HEADS, 0]).then_inc(sub_rec, 1)
            for h in range(HEADS + 1):
                if h < HEADS:
                    dve.wait_ge(sub_bc, h + 1)
                    if h >= 2:
                        dve.wait_ge(sub_lo, h - 1)
                    tt(osq[:, h % 2], o_raw[:, h], ps[:, 1 + h % 2], op=ALU.mult).then_inc(sub_t, 1)
                if h >= 1:
                    dve.wait_ge(sub_hi, h)
                    V.scalar_tensor_tensor(out=o1_lo[:, h - 1], in0=osq[:, (h - 1) % 2], scalar=subg[:, 1:2],
                                           in1=o1_hi[:, h - 1].bitcast(F32), op0=ALU.mult,
                                           op1=ALU.subtract).then_inc(sub_lo, 1)
            for i in range(8):
                u = FIRST["out1"] + i
                add_x(1, u + 1, u % 2, i, 2, 40 + i)
                if i:
                    sum_squares(3, i - 1)
            sum_squares(3, 7)
            norm(3)
            mlp(1)
            norm(4)

        @block.tensor
        def _(pe):
            mm = nc.tensor.matmul

            def three(out, a, b, start, stop, last=None):
                mm(out, a[0], b[1], start=start, stop=False)
                mm(out, a[1], b[0], start=False, stop=False)
                return mm(out, a[0], b[0], start=False, stop=stop)

            def unit(u, s, par, hi, lo, chunks, k_wait=None):
                pe.wait_ge(lo_made, u + 1)
                for k in range(KT):
                    if k_wait:
                        k_wait(k)
                    w = (w_hi[:, s, P * k:P * k + P], w_lo[:, s, P * k:P * k + P])
                    for bank, c0, n in chunks:
                        ins = three(ps[:, 2 * par + bank, 0:n], w, (hi(k)[:, c0:c0 + n], lo(k)[:, c0:c0 + n]),
                                    k == 0, k == KT - 1)
                ins.then_inc(unit_done, 1)

            def unit_pair(u, s, par, hi, lo, chunks, second_free, k_wait):
                order = [(0, 0), (0, 1), (1, 0), (1, 1)] + [(j, k) for k in range(2, 6) for j in range(2)]
                for j, k in order + [(0, 6), (0, 7), (1, 6), (1, 7)]:
                    if k == 0:
                        if j:
                            second_free()
                        pe.wait_ge(lo_made, u + j + 1)
                    if j == 0:
                        k_wait(k)
                    w = (w_hi[:, (s + j) % SLOTS, P * k:P * k + P], w_lo[:, (s + j) % SLOTS, P * k:P * k + P])
                    for bank, c0, n in chunks:
                        ins = three(ps[:, 2 * ((par + j) % 2) + bank, 0:n], w, (hi(k)[:, c0:c0 + n], lo(k)[:, c0:c0 + n]),
                                    k == 0, k == KT - 1)
                    if k == KT - 1:
                        ins.then_inc(unit_done, 1)

            def h_wait(i):
                return lambda k: pe.wait_ge(h_made, KT * i + k + 1)

            h_t = (lambda k: h_hi[:, k], lambda k: h_lo[:, k])
            hid_t = (lambda k: hid_hi[:, k], lambda k: hid_lo[:, k])

            def mod_mm(m):
                pe.wait_ge(mod_summed, m - 3)
                for v in range(2):
                    ins = mm(ps[:, 4 + v], ones[:], mod_acc[:, v], start=True, stop=True)
                ins.then_inc(mod_rows, 1)

            def norm_sums(i):
                pe.wait_ge(sq_summed, KT * (i + 1))
                for c in range(NORM_TOK[i] // P):
                    ins = mm(ps[:, 6, c:c + 1], ssum[:, P * c:P * c + P], ones[:, 0:1], start=True, stop=True)
                ins.then_inc(norm_sum, 1)

            def norm_spread(i):
                pe.wait_ge(norm_diag, i + 1)
                for _, v, cols in parts(NORM_TOK[i]):
                    ins = mm(ps[:, 6 + v, 0:cols.stop - cols.start], ones[:],
                             diag[:].rearrange("p c q -> p (c q)")[:, cols], start=True, stop=True)
                ins.then_inc(norm_rows, 1)

            def norm_mm(i):
                norm_sums(i)
                norm_spread(i)

            def values(u, j, start, stop, banks_free=None):
                s = u % SLOTS
                pe.wait_ge(lo_made, u + 1)
                for n in range(NT):
                    if banks_free:
                        banks_free(n)
                    for kk in range(2):
                        k = 2 * j + kk
                        ins = three(ps[:, V_BANK[n]], (h_hi[:, k, P * n:P * n + P], h_lo[:, k, P * n:P * n + P]),
                                    (w_hi[:, s, 512 * kk:512 * kk + 512], w_lo[:, s, 512 * kk:512 * kk + 512]),
                                    start and kk == 0, stop and kk == 1)
                ins.then_inc(unit_done, 1)

            def mlp(layer):
                u0 = FIRST[f"mlp{layer}"]
                chunks = both[:2 - layer]

                def blk(b, last):
                    for i in range(16):
                        u = u0 + i
                        if i == 0:
                            pe.wait_ge(x_added, xa(layer, b, 0) - 1)
                            unit_pair(u + 16 * b, u % SLOTS, u % 2, *h_t, chunks,
                                      lambda: pe.wait_ge(x_added, xa(layer, b, 0)), h_wait(1 + 2 * layer))
                        elif i == 1:
                            continue
                        elif i < 8:
                            pe.wait_ge(relu_made, ha(layer, b, i) - 1)
                        elif i < 10:
                            pe.wait_ge(relu_made, ha(layer, b, i) - 1)
                        else:
                            pe.wait_ge(x_added, xa(layer, b, i - 8) - 1)
                        if 2 <= i < 8:
                            unit(u + 16 * b, u % SLOTS, u % 2, *h_t, chunks)
                        elif i >= 8:
                            unit(u + 16 * b, u % SLOTS, u % 2, *hid_t, chunks,
                                 (lambda k: pe.wait_ge(hid_made, ha(layer, b, k) + 1)) if i == 8 else None)
                        if layer == 0 and not last and i % 4 == 3:
                            pe.wait_ge(mod_done, 12 + 4 * b + i // 4)
                            mod_mm(12 + 4 * b + i // 4)

                with pe.Fori(0, HID_BLOCKS - 1) as b:
                    blk(b, False)
                blk(HID_BLOCKS - 1, True)
                norm_mm(2 + 2 * layer)

            pe.wait_ge(ones_ok, 1)
            pe.wait_ge(lam_ok, 1)
            mm(ps[:, 6, 0:2], ones[0:HD, :], lam_t[0:HD, 0:2], start=True, stop=True).then_inc(lam_mm, 1)

            def half_mm(m):
                if m == 0:
                    pe.wait_ge(cact_ok, 1)
                if m >= 2:
                    pe.wait_ge(half_out, m - 1)
                for k in range(KT):
                    if k % 4 == 0:
                        pe.wait_ge(big_in[m % 3][k // 4], 16 * (m // 3 + 1))
                    ins = mm(ps[0:2, m % 2], cact[:, k], big[:, m % 3, k], start=k == 0, stop=k == KT - 1)
                ins.then_inc(half_summed, 1)

            def half_turn(m):
                pe.wait_ge(half_out, m + 1)
                if m >= 2:
                    pe.wait_ge(mod_done, m - 1)
                for c in range(4):
                    ins = mm(ps[:, 2 + m % 2, 2 * c:2 * c + 2], mod_acc[0:2, m % 2, P * c:P * c + P], ident[0:2, 0:2],
                             start=True, stop=True)
                ins.then_inc(half_turned, 1)

            half_mm(0)
            half_mm(1)
            half_turn(0)
            half_mm(2)
            half_turn(1)
            norm_sums(0)
            half_mm(3)
            norm_spread(0)
            half_turn(2)
            half_turn(3)
            pe.wait_ge(mod_done, 4)

            for i in range(12):
                u = FIRST["f"] + i
                if 2 <= i < 6:
                    pe.wait_ge(f_out, i - 1)
                elif i >= 6:
                    pe.wait_ge(qk_out, i - 5)
                if i == 0:
                    unit_pair(u, u % SLOTS, u % 2, *h_t, both, lambda: None, h_wait(0))
                elif i >= 2:
                    unit(u, u % SLOTS, u % 2, *h_t, both)
                if i == 1:
                    mod_mm(4)
                elif i >= 4 and i % 2 == 0:
                    pe.wait_ge(mod_done, 3 + i // 2)
                    mod_mm(3 + i // 2)
            pe.wait_ge(f_out, 4)
            pe.wait_ge(dft_lo_s, 1)
            pe.wait_ge(qk_out, 8)
            for n in range(2 * NT):
                tok = slice(P * (n // 2), P * (n // 2) + P)
                if n >= 6:
                    pe.wait_ge(u_lo_s, n - 5)
                for j in range(2):
                    g = 2 * (n % 2) + j
                    ins = three(ps[:, V_BANK[n % 6], 256 * j:256 * j + 256], (f_hi[:, g, tok], f_lo[:, g, tok]),
                                (dft_hi[:], dft_lo[:]), True, True)
                ins.then_inc(u_mm, 1)
            pe.wait_ge(mod_done, 9)
            mod_mm(9)
            pe.wait_ge(u_lo_s, 2 * NT)
            for i in range(4):
                u = FIRST["dft"] + i
                s = u % SLOTS
                pe.wait_ge(lo_made, u + 1)
                for g in range(4):
                    c = slice(P * (i // 2), P * (i // 2) + P)
                    for j in range(2):
                        n = 2 * (i % 2) + j
                        ins = three(ps[:, g], (u_hi[:, n, g, c], u_lo[:, n, g, c]),
                                    (w_hi[:, s, 512 * j:512 * j + 512], w_lo[:, s, 512 * j:512 * j + 512]),
                                    i == 0 and j == 0, i == 3 and j == 1)
                ins.then_inc(unit_done, 1)
            u = FIRST["dft"] + 4
            s = u % SLOTS
            pe.wait_ge(lo_made, u + 1)
            for g in range(4):
                for j in range(4):
                    c = slice(P * (j // 2), P * (j // 2) + P)
                    n = 4 + j % 2
                    ins = three(ps[:, 6 + g // 2, 256 * (g % 2):256 * (g % 2) + 256], (u_hi[:, n, g, c], u_lo[:, n, g, c]),
                                (w_hi[:, s, 256 * j:256 * j + 256], w_lo[:, s, 256 * j:256 * j + 256]), j == 0, j == 3)
            ins.then_inc(unit_done, 1)
            def y_free(n):
                pe.wait_ge(y_lo_s, min(n + 1, 4) if n < 4 else n + 1)

            for i in range(4):
                values(FIRST["v0"] + i, i, i == 0, i == 3, y_free if i == 0 else None)

            def scores(n):
                h, t_ = n // 6, n % 6
                p = h % 2
                if t_ == 0:
                    pe.wait_ge(js, h + 1)
                    pe.wait_ge(jk, h + 1)
                if n >= 3:
                    pe.wait_ge(e_made, n - 2)
                else:
                    pe.wait_ge(v0_lo_s, NT)
                tok = slice(P * t_, P * t_ + P)
                keys = [slice(LAT, TOK)] if t_ >= 4 else [slice(WINDOW[t_], WINDOW[t_] + 256), slice(LAT, TOK)]
                if t_ < 4:
                    v = VARIANT[t_]
                    pe.wait_ge(bl_made, 3 * h + v + 1)
                    mm(ps[:, n % 3, 0:256], ident_r[:], bias_lo[:, p, v], start=True, stop=False)
                    mm(ps[:, n % 3, 0:256], ident_r[:], bias_hi[v][:], start=False, stop=False)
                for j, ks in enumerate(keys):
                    o = ps[:, n % 3, 256 * j:256 * j + 256]
                    mm(o, q2b[:, p, tok], k2[:, p, ks], start=t_ >= 4 or j == 1, stop=False)
                    ins = mm(o, q2a[:, p, tok], k2[:, p, ks], start=False, stop=True)
                ins.then_inc(s_made, 1)

            def turn(n):
                c = 4 if n % 6 < 4 else 2
                pe.wait_ge(p_made, n + 1)
                if n >= 2:
                    pe.wait_ge(tl_made, n - 1)
                for j in range(c):
                    ins = nc.tensor.transpose(ps[:, 3 + n % 2, P * j:P * j + P], prob0[:, n % PROBS, P * j:P * j + P], ident[:])
                ins.then_inc(tr_made, 1)

            def weigh(n):
                h, t_ = n // 6, n % 6
                pe.wait_ge(tl_made, n + 1)
                if n == 0:
                    pe.wait_ge(shift_in, 16 * 6)
                if t_ % 2 == 0 and h:
                    pe.wait_ge(od_made, n // 2 - 2)
                lat = {0: (v0[:, 0], v0[:, 1]), 1: (v0s[:, 0], v0s[:, 1]), 2: (v0s[:, 1], v0s[:, 2]),
                       3: (v0[:, 2], v0[:, 3])}
                vs = (lat[t_] if t_ < 4 else ()) + (v0[:, 4], v0[:, 5])
                for c, v in enumerate(vs):
                    ins = mm(pv_ps[:, t_, :], v[:, h, :], pt0[:, n % 2, c, :], start=c == 0, stop=c == len(vs) - 1)
                ins.then_inc(pv_made, 1)

            N0 = 6 * HEADS
            pe.wait_ge(mod_done, 10)
            pe.wait_ge(ident_ok, 1)
            scores(0)
            scores(1)
            for n in range(N0 + 1):
                if n + 2 < N0:
                    scores(n + 2)
                if n < N0:
                    turn(n)
                if n >= 1:
                    weigh(n - 1)
            mix_hi = lambda k: y_hi[:, k] if k < 4 else o0_hi[:, k - 4]
            mix_lo = lambda k: y_lo[:, k] if k < 4 else o0_lo[:, k - 4]
            pe.wait_ge(ol_made, HEADS)
            for i in range(8):
                u = FIRST["out0"] + i
                if i >= 2:
                    pe.wait_ge(x_added, i - 1)
                unit(u, u % SLOTS, u % 2, mix_hi, mix_lo, both)
                if i in (3, 6):
                    pe.wait_ge(mod_done, 9 + i // 3)
                    mod_mm(9 + i // 3)
            norm_mm(1)
            mlp(0)
            unit_pair(FIRST["k1"], FIRST["k1"] % SLOTS, FIRST["k1"] % 2, *h_t, both, lambda: None, h_wait(2))
            for i in range(2, 16):
                u = FIRST["k1"] + i
                pe.wait_ge(rope_read, i - 1)
                if i < 10:
                    pe.wait_ge(kc_out, i - 1)
                unit(u, u % SLOTS, u % 2, *h_t, both if i < 8 else both[:1])
            pe.wait_ge(rope_read, 16)
            for j in range(2):
                for i in range(4):
                    values(FIRST["v1"] + 4 * j + i, i, i == 0, i == 3,
                           (lambda n: pe.wait_ge(v1_out, n + 1)) if j == 1 and i == 0 else None)

            def scores1(n):
                h, t_ = n // 4, n % 4
                for i in range(2):
                    s = 2 * n + i
                    if t_ == 0:
                        pe.wait_ge(js1, 2 * h + i + 1)
                        pe.wait_ge(jk1, 2 * h + i + 1)
                    if s >= 2:
                        pe.wait_ge(e1, s - 1)
                    b0 = 2 * (s % 2)
                    tok = slice(P * t_, P * t_ + P)
                    for bank, ks in ((b0, slice(0, LAT)), (b0 + 1, slice(LAT, TOK))):
                        o = ps[:, bank, 0:ks.stop - ks.start]
                        mm(o, aq2b[h % 2][i][:, tok], ak2[h % 2][i][:, ks], start=True, stop=False)
                        ins = mm(o, aq2a[h % 2][i][:, tok], ak2[h % 2][i][:, ks], start=False, stop=True)
                    ins.then_inc(s1, 1)

            def turn1(n):
                pe.wait_ge(a1, n + 1)
                if n >= 1:
                    pe.wait_ge(tl1, n)
                for c in range(NT):
                    ins = nc.tensor.transpose(ps[:, 4 + c // 3, P * (c % 3):P * (c % 3) + P],
                                              aprob[:, n % 3, 0, P * c:P * c + P], ident[:])
                ins.then_inc(tr1, 1)

            def weigh1(m):
                pe.wait_ge(tl1, 2 * m + 2)
                if m % 2 == 0:
                    pe.wait_ge(vl1, m // 2 + 1)
                if m >= 2:
                    pe.wait_ge(o1, m - 1)
                for c in range(NT):
                    ins = three(ps[:, 6 + m % 2, 0:256], (avh[:, c], avl[:, c]), (at_hi[:, c], at_lo[:, c]), c == 0, c == NT - 1)
                ins.then_inc(pv1, 1)

            pe.wait_ge(v1_out, 2 * NT)
            N1 = 4 * HEADS
            scores1(0)
            for n in range(N1 + 4):
                if n >= 4 and n % 2 == 0:
                    weigh1((n - 4) // 2)
                if n + 1 < N1:
                    scores1(n + 1)
                if 1 <= n <= N1:
                    turn1(n - 1)
            pe.wait_ge(oneh_in, 32)
            for h in range(HEADS):
                pe.wait_ge(sub_sq, h + 1)
                mm(ps[0:HEADS, 0], oneh[:, h], osq[:, h % 2], start=h == 0, stop=h == HEADS - 1).then_inc(sub_mm, 1)
            pe.wait_ge(sub_rec, 1)
            for h in range(HEADS):
                if h >= 2:
                    pe.wait_ge(sub_t, h - 1)
                mm(ps[:, 1 + h % 2], selh[:, h], sub_r[0:HEADS, 1], start=True, stop=True).then_inc(sub_bc, 1)
            pe.wait_ge(sub_lo, HEADS)
            for i in range(8):
                u = FIRST["out1"] + i
                if i >= 2:
                    pe.wait_ge(x_added, 40 + i - 1)
                unit(u, u % SLOTS, u % 2, lambda k: o1_hi[:, k], lambda k: o1_lo[:, k], both[:1])
            norm_mm(3)
            mlp(1)


_OUT = (P, KT, LAT)


def _order():
    t = np.arange(LAT)
    return (t % ROWS) * COLS + t // ROWS


def _stationary(w):
    n = w.shape[1] // P
    return w.reshape(KT, P, n, P).transpose(2, 1, 0, 3).reshape(n, P, D)


def _moving(w):
    n = w.shape[1] // 512
    return w.reshape(4, 2, P, n, 512).transpose(3, 0, 2, 1, 4).reshape(4 * n, P, D)


def _mlp(w_in, w_out):
    u = []
    for b in range(HID_BLOCKS):
        u += [_stationary(w_in[:, D * b:D * b + D]), _stationary(w_out[D * b:D * b + D])]
    return u


def _dft(n, order, scale):
    a = 2 * np.pi * (np.outer(order, order) % n) / n
    return np.stack([np.cos(a), -np.sin(a)]) * scale


def _tables():
    order = _order()
    cs = _dft(LAT, order, (LAT * P) ** -0.5).reshape(2, 2, 2, P, LAT).transpose(0, 1, 3, 2, 4).reshape(4, P, D)
    cc = _dft(CTX, np.arange(CTX), (CTX * P) ** -0.5).reshape(4, P, CTX).transpose(1, 0, 2).reshape(1, P, D)
    units = np.concatenate([cs, cc]).astype(np.float32)
    a = 2 * np.pi * (np.outer(np.arange(P), np.arange(P)) % P) / P
    dft128 = np.concatenate([np.cos(a), np.sin(a)], axis=1).astype(np.float32)
    nf = HD // 4
    freq = np.float32(10000.0) ** (-np.arange(nf, dtype=np.float32) / np.float32(nf))
    ang = np.zeros((P, LAT), np.float32)
    sign = np.zeros((P, 1), np.float32)
    for p in range(P):
        pos = order // COLS if p % 64 < 32 else order % COLS
        ang[p] = pos.astype(np.float32) * freq[p % nf]
        sign[p] = -1.0 if p % 32 < nf else 1.0
    cos = np.cos(ang.astype(np.float64)).astype(np.float32)
    sin = (np.sin(ang.astype(np.float64)) * sign).astype(np.float32)
    mask = np.zeros((P, 3, 32), np.float32)
    for v, qt in ((0, 0), (1, 1), (2, 3)):
        col = 16 * qt + np.arange(P) // ROWS
        start = np.clip(col - 8, 0, COLS - 16)
        key = WINDOW[qt] // ROWS + np.arange(32)
        ok = (key[None] >= start[:, None]) & (key[None] < start[:, None] + 16)
        mask[:, v] = np.where(ok, 0.0, -NEG)
    oneh = np.zeros((P, HEADS, HEADS), np.float32)
    selh = np.zeros((HEADS, HEADS, P), np.float32)
    for h in range(HEADS):
        oneh[:, h, h] = 1.0
        selh[h, h] = 1.0
    return units, dict(dft128=dft128, cos=cos, sin=sin, mask=mask, ident=np.eye(P, dtype=np.float32),
                       oneh=oneh, selh=selh)


def _bias(rpb):
    q = np.arange(P)
    k = np.arange(256)
    out = []
    for v, qt in ((0, 0), (1, 1), (2, 3)):
        qc, qr = 16 * qt + q // ROWS, q % ROWS
        kc, kr = WINDOW[qt] // ROWS + k // ROWS, k % ROWS
        dr = kr[None] - qr[:, None] + 7
        dc = np.clip(kc[None] - qc[:, None], -15, 15) + 15
        out.append(rpb[:, dr, dc])
    return np.stack(out, axis=2)


def _columns(v):
    v = v.reshape(v.shape[:-1] + (v.shape[-1] // P, P))
    return np.moveaxis(v, -1, 0)


def _layout(i):
    order = _order()
    tables, d = _tables()
    w_ab, w_qkv = i["w_in_ab"][0], i["w_qkv_diff"][0]
    units = ([_stationary(w_ab[:, :1536])] + [tables] + [_moving(w_ab[:, 1536:])] + [_stationary(i["w_out_ab"][0])]
             + _mlp(i["w_mlp_in"][0], i["w_mlp_out"][0])
             + [_stationary(w_qkv[:, D:2 * D]), _stationary(w_qkv[:, :D]), _moving(w_qkv[:, 2048:]), _stationary(i["w_out_diff"][0])]
             + _mlp(i["w_mlp_in"][1], i["w_mlp_out"][1]))
    d["units"] = np.concatenate(units)
    d["x"] = i["x"][0][order].T.reshape(KT, P, LAT).transpose(1, 0, 2)
    d["ctx"] = i["ctx"][0].T.reshape(KT, P, CTX).transpose(1, 0, 2)
    d["w_mod"] = i["w_mod"].reshape(2, KT, P, 12, 512).transpose(0, 3, 2, 1, 4).reshape(24, P, KT, 512)
    d["b_mod"] = _columns(i["b_mod"].reshape(24, 512))
    d["gains"] = _columns(np.stack([i["norm_mix_g"][0], i["norm_mlp_g"][0], i["norm_mix_g"][1], i["norm_mlp_g"][1],
                                    i["final_norm_g"]]))
    d["cond"] = np.stack([_columns(i["c"][0]), _columns(i["c_ctx"])], axis=2)
    d["lam"] = np.stack([i["diff_lq1"][0], i["diff_lk1"][0], i["diff_lq2"][0], i["diff_lk2"][0]], axis=1)
    d["subln"] = np.stack([i["diff_subln_g"][0]] * 2, axis=1)
    d["bias"] = _bias(i["na_rpb"][0])
    return {k: np.ascontiguousarray(v) for k, v in d.items()}


def kernel(**inputs):
    import concourse.bacc as bacc
    from concourse.bass_utils import run_bass_kernel_spmd

    nc = bacc.Bacc("TRN2", target_bir_lowering=False, num_devices=1)
    data = _layout({k: np.asarray(v) for k, v in inputs.items()})
    t = {k: nc.dram_tensor(k + "_dram", v.shape, mybir.dt.from_np(v.dtype), kind="ExternalInput").ap()
         for k, v in data.items()}
    t["out"] = nc.dram_tensor("out_dram", _OUT, F32, kind="ExternalOutput").ap()
    build(nc, t)
    r = run_bass_kernel_spmd(nc, [{k + "_dram": v for k, v in data.items()}], core_ids=[0])
    out = np.asarray(r.results[0]["out_dram"]).transpose(2, 1, 0).reshape(LAT, D)
    back = np.empty_like(out)
    back[_order()] = out
    return back[None]
```

```python
from contextlib import ExitStack, contextmanager

import numpy as np

import concourse.bass as bass
from concourse import mybir

F32 = mybir.dt.float32
F32R = mybir.dt.float32r
ALU = mybir.AluOpType
ACT = mybir.ActivationFunctionType
AX = mybir.AxisListType

P = 128
D = 1024
KT = D // P
LAT, CTX = 512, 256
TOK = LAT + CTX
NT = TOK // P
ROWS, COLS = 8, 64
HEADS, HD = 8, 64
HID_BLOCKS = 4
EPS, SUB_EPS = 1e-6, 1e-5
LAM_INIT = 0.8 - 0.6 * float(np.exp(-0.3))
NEG = -1e30

STAGES = [("f", 4), ("q0", 4), ("k0", 4), ("dft", 5), ("v0", 4), ("out0", 8), ("mlp0", 64),
          ("k1", 8), ("q1", 8), ("v1", 8), ("out1", 8), ("mlp1", 64)]
FIRST, UNITS = {}, 0
for _name, _n in STAGES:
    FIRST[_name] = UNITS
    UNITS += _n
SLOTS = 4
AHEAD = 3

WINDOW = [0, 64, 192, 256]
VARIANT = [0, 1, 1, 2]
SPLIT_HALF = 10
RING = 4


def mix_mods(i):
    if i < 4:
        m, ks = {-1: (4, range(4)), 0: (4, (4, 5)), 1: (4, (6, 7)), 2: (5, range(3)), 3: (5, range(3, 8))}[i]
    else:
        m, ks = 4 + i // 2, range(4 * (i % 2), 4 * (i % 2) + 4)
    return [(m, k) for k in ks]


def out_mods(i):
    ms = [(10, range(4)), (10, range(4, 8)), (11, range(3)), (11, range(3, 6)), (11, range(6, 8))]
    return [(ms[i][0], k) for k in ms[i][1]] if i < 5 else []


MOD_AT = [range(0, 4), range(4, 8), (), ()]
PROBS = 3


class Steps:

    def __init__(self, eng, sem):
        self.eng, self.sem, self.n = eng, sem, 0

    def wait(self, ins):
        ins.then_inc(self.sem, 1)
        self.n = self.n + 1
        self.eng.wait_ge(self.sem, self.n)

    @contextmanager
    def loop(self, count, per):
        base = self.n
        with self.eng.Fori(0, count) as i:
            self.n = base + i * per
            yield i
        self.n = base + count * per


def build(nc, t):
    ctx = ExitStack()
    with ctx:
        base = 16512

        def at(name, shape, dt, offset):
            return nc.alloc_sbuf_tensor_at(name, shape, dt, offset=offset)

        size = lambda *shape: int(np.prod(shape)) * 4
        x_at = base
        a_at = x_at + size(TOK, KT)
        raw_at = a_at + 2 * size(TOK, KT)
        whi_at = raw_at + size(SLOTS, 1024)
        wlo_at = whi_at + size(SLOTS, 1024)
        con_at = wlo_at + size(SLOTS, 1024)
        rest = con_at + 5632
        mod_at = 229344 - size(RING + 4, 512)
        scr = rest + 2 * size(TOK, KT)

        xl = at("xl", [P, KT, LAT], F32, x_at)
        xc = at("xc", [P, KT, CTX], F32, x_at + size(KT, LAT))
        h_hi = at("h_hi", [P, KT, TOK], F32R, a_at)
        h_lo = at("h_lo", [P, KT, TOK], F32R, a_at + size(KT, TOK))
        raw = at("raw", [P, SLOTS, 1024], F32, raw_at)
        w_hi = at("w_hi", [P, SLOTS, 1024], F32R, whi_at)
        w_lo = at("w_lo", [P, SLOTS, 1024], F32R, wlo_at)

        c_off = [con_at]

        def const(name, shape, dt=F32):
            o = c_off[0]
            c_off[0] += (size(*shape[1:]) + 31) // 32 * 32
            assert c_off[0] <= rest
            return at(name, shape, dt, o)

        ident = const("ident", [P, P])
        ones_r = const("ones", [P, P], F32R)
        mods = const("mods", [P, 24, 2, 4])
        b_mod = const("b_mod_sb", [P, 24, 4])
        gains = const("gains", [P, 5, KT])
        gs = const("gs", [P, 4, 2, KT])
        cond = const("cond", [P, KT, 2])
        cact = const("cact", [P, KT, 2])
        eps_c = const("eps_c", [P, 2])
        stat = const("stat", [P, 64])
        modr = const("modr", [P, 2, 4])
        dft_at = c_off[0]
        dft_hi = const("dft_hi", [P, 256], F32R)
        dft_lo = const("dft_lo", [P, 256], F32R)
        lam_in = const("lam_in", [HD, 4])
        lam_t = const("lam_t", [P, 8])
        subg = const("subg", [P, 2])

        ctmp = at("ctmp", [P, KT, 2], F32, mod_at)
        mod_ring = at("mod_ring", [P, RING, 512], F32, mod_at)
        mod_acc = at("mod_acc", [P, 2, 512], F32, mod_at + size(RING, 512))
        acc_lo = at("acc_lo", [P, 2, 512], F32R, mod_at + size(RING, 512))
        acc_hi = at("acc_hi", [P, 2, 512], F32R, mod_at + size(RING + 2, 512))

        big = at("mod_big", [P, 3, KT, 512], F32, rest)
        hid_hi = at("hid_hi", [P, KT, TOK], F32R, rest)
        hid_lo = at("hid_lo", [P, KT, TOK], F32R, rest + size(KT, TOK))
        out_t = at("out_t", [P, KT, LAT], F32, rest)
        tmp_a = at("tmp_a", [P, 2, TOK], F32, scr)
        tmp_b = at("tmp_b", [P, 2, TOK], F32, scr + size(2, TOK))
        ssum = at("ssum", [P, TOK], F32, scr + size(4, TOK))
        diag = at("diag", [P, NT, P], F32, scr + size(5, TOK))
        assert scr + size(6, TOK) <= mod_at

        q0 = at("q0", [P, 4, TOK], F32, x_at)
        k0 = at("k0", [P, 4, TOK], F32, x_at + size(4, TOK))
        f_hi = at("f_hi", [P, 4, TOK], F32R, rest)
        f_lo = at("f_lo", [P, 4, TOK], F32R, rest + size(4, TOK))
        y_hi, y_lo = f_hi, f_lo
        u_at = rest + 2 * size(4, TOK)
        u_hi = at("u_hi", [P, NT, 4, 256], F32R, u_at)
        u_lo = at("u_lo", [P, NT, 4, 256], F32R, u_at + size(NT, 4, 256))
        dft_raw = at("dft_raw", [P, 256], F32, u_at)
        assert u_at + 2 * size(NT, 4, 256) <= mod_at + size(RING, 512)
        v0 = at("v0", [P, NT, HEADS, P], F32R, u_at)
        v0s = at("v0s", [P, 3, HEADS, P], F32R, u_at + size(NT, 1024))
        pr_at = u_at + size(NT + 3, 1024)
        prob0 = at("prob0", [P, PROBS, 512], F32, pr_at)
        pt0 = at("pt0", [P, 2, 4, 256], F32R, pr_at + size(PROBS, 512))
        osum = at("osum", [P, 2, TOK], F32, pr_at + size(PROBS, 512) + size(2, 1024))
        o0_hi = at("o0_hi", [P, 4, TOK], F32R, a_at)
        o0_lo = at("o0_lo", [P, 4, TOK], F32R, a_at + size(4, TOK))
        j_at = a_at + size(8, TOK)
        q2a = at("q2a", [P, 2, TOK], F32R, j_at + size(2, TOK))
        q2b = at("q2b", [P, 2, TOK], F32R, j_at + size(4, TOK))
        k2 = at("k2", [P, 2, TOK], F32R, j_at + size(6, TOK))
        bias = at("bias", [P, 2, 3, 256], F32, j_at)
        bias_lo = at("bias_lo", [P, 2, 3, 256], F32R, j_at)
        tail_at = pr_at + size(PROBS, 512) + size(2, 1024) + size(2, TOK)
        ident_r = at("ident_r", [P, P], F32R, tail_at + size(256))
        assert tail_at + size(256) + size(P) <= 229360
        bias_hi = [at(f"bias_hi{v}", [P, 256], F32R, [dft_at, dft_at + size(256), tail_at][v]) for v in range(3)]
        assert size(8, TOK) + size(6, TOK) + size(2, 768) <= size(16, TOK)
        mask = const("mask", [P, 3, 32])

        q1 = at("q1", [P, HEADS, LAT], F32, rest)
        k1 = at("k1", [P, HEADS, TOK], F32, rest + size(HEADS, LAT))
        v1 = at("v1", [P, NT, D], F32, rest + size(HEADS, LAT + TOK))
        cs_at = rest + size(HEADS, LAT + TOK) + size(NT, D)
        cosb = at("cosb", [P, LAT], F32, cs_at)
        sinb = at("sinb", [P, LAT], F32, cs_at + size(LAT))
        rt = at("rt", [P, 3, LAT], F32, cs_at + size(2, LAT))
        o_raw = at("o_raw", [P, HEADS, LAT], F32, a_at + size(4, LAT))
        b_at = a_at + size(HEADS, LAT)
        c_at = b_at + size(4, LAT) + size(4, TOK)
        odd = [rest, rest + size(HEADS, LAT), dft_at, x_at + size(KT, LAT) + size(NT, 256)]
        q_at = [[a_at + size(i, LAT) for i in range(4)], odd]
        k_at = [b_at + size(4, LAT), c_at + size(NT, 256)]
        aq2a = [[at(f"aq2a_{p}{i}", [P, LAT], F32R, q_at[p][i]) for i in range(2)] for p in range(2)]
        aq2b = [[at(f"aq2b_{p}{i}", [P, LAT], F32R, q_at[p][2 + i]) for i in range(2)] for p in range(2)]
        ak2 = [[at(f"ak2_{p}{i}", [P, TOK], F32R, k_at[p] + size(i, TOK)) for i in range(2)] for p in range(2)]
        avh = at("avh", [P, NT, P], F32R, b_at + size(4, LAT) + size(2, TOK))
        avl = at("avl", [P, NT, P], F32R, b_at + size(4, LAT) + size(3, TOK))
        aprob = at("aprob", [P, 3, 2, TOK], F32, cs_at)
        at_hi = at("at_hi", [P, NT, 256], F32R, c_at)
        assert c_at + size(NT, 256) + size(2, TOK) <= raw_at
        at_lo = at("at_lo", [P, NT, 256], F32R, x_at + size(KT, LAT))
        assert cs_at + size(6, TOK) <= 229360
        o1_hi = at("o1_hi", [P, HEADS, LAT], F32R, rest)
        o1_lo = at("o1_lo", [P, HEADS, LAT], F32R, rest + size(HEADS, LAT))
        k1_at = rest + size(HEADS, LAT)
        sq_at = [rest + size(i + 1, LAT) for i in range(HEADS - 1)] + [k1_at + size(TOK)]
        osq = [at(f"osq{i}", [P, LAT], F32, sq_at[i]) for i in range(HEADS)]
        oneh = at("oneh", [P, HEADS, HEADS], F32, k1_at + size(TOK) + size(LAT))
        selh = at("selh", [HEADS, HEADS, P], F32, k1_at + size(6, TOK))
        v1_at = rest + size(HEADS, LAT + TOK)
        sub_r = at("sub_r", [P, 2, LAT], F32, v1_at)
        sub_last = at("sub_last", [1, 2, LAT], F32, v1_at + size(4, LAT))
        sub_x = at("sub_x", [P, 2, LAT], F32, v1_at + size(2, LAT))

        ps = ctx.enter_context(nc.psum_tensor("ps", [P, 8, 512], F32))

        ones = ones_r[:].bitcast(F32)

        def sem(name):
            return ctx.enter_context(nc.semaphore(name))

        consts_in = sem("consts_in")
        x_in = sem("x_in")
        xr_in = sem("xr_in")
        table_in = sem("table_in")
        oneh_in = sem("oneh_in")
        hi_made = sem("hi_made")
        lo_made = sem("lo_made")
        unit_done = sem("unit_done")
        mod_used = sem("mod_used")
        mod_summed = sem("mod_summed")
        mod_rows = sem("mod_rows")
        mod_done = sem("mod_done")
        exp_c = sem("exp_c")
        cact_ok = sem("cact_ok")
        half_summed = sem("half_summed")
        half_out = sem("half_out")
        half_turned = sem("half_turned")
        ones_ok = sem("ones_ok")
        lam_mm = sem("lam_mm")
        lam_exp = sem("lam_exp")
        lam_ok = sem("lam_ok")
        relu_made = sem("relu_made")
        relu_used = sem("relu_used")
        hid_made = sem("hid_made")
        x_added = sem("x_added")
        first_done = sem("first_done")
        first_added = sem("first_added")
        first_t = sem("first_t")
        sq_made = sem("sq_made")
        sq_summed = sem("sq_summed")
        norm_sum = sem("norm_sum")
        norm_sqrt = sem("norm_sqrt")
        norm_diag = sem("norm_diag")
        norm_rows = sem("norm_rows")
        t_made = sem("t_made")
        aff_made = sem("aff_made")
        hh_made = sem("hh_made")
        h_made = sem("h_made")
        out_made = sem("out_made")
        out_stored = sem("out_stored")
        dsteps = sem("dsteps")
        f_hi_s = sem("f_hi_s")
        f_out = sem("f_out")
        qk_out = sem("qk_out")
        dft_hi_s = sem("dft_hi_s")
        dft_lo_s = sem("dft_lo_s")
        u_mm = sem("u_mm")
        u_hi_s = sem("u_hi_s")
        u_lo_s = sem("u_lo_s")
        y_hi_s = sem("y_hi_s")
        y_lo_s = sem("y_lo_s")
        v0_hi_s = sem("v0_hi_s")
        v0_lo_s = sem("v0_lo_s")
        bias_ok = sem("bias_ok")
        jh = sem("jh")
        jl = sem("jl")
        jk = sem("jk")
        js = sem("js")
        s_made = sem("s_made")
        m_made = sem("m_made")
        e_made = sem("e_made")
        p_made = sem("p_made")
        tr_made = sem("tr_made")
        th_made = sem("th_made")
        tl_made = sem("tl_made")
        pv_made = sem("pv_made")
        ident_ok = sem("ident_ok")
        bh_made = sem("bh_made")
        bl_made = sem("bl_made")
        kh0 = sem("kh0")
        oh_made = sem("oh_made")
        oc_made = sem("oc_made")
        od_made = sem("od_made")
        ol_made = sem("ol_made")
        rope_read = sem("rope_read")
        rope_done = sem("rope_done")
        kc_out = sem("kc_out")
        v1_out = sem("v1_out")
        jh1 = sem("jh1")
        jl1 = sem("jl1")
        jk1 = sem("jk1")
        kh1 = sem("kh1")
        js1 = sem("js1")
        vh1 = sem("vh1")
        vl1 = sem("vl1")
        s1 = sem("s1")
        m1 = sem("m1")
        e1 = sem("e1")
        c1 = sem("c1")
        g1 = sem("g1")
        a1 = sem("a1")
        tr1 = sem("tr1")
        th1 = sem("th1")
        tl1 = sem("tl1")
        pv1 = sem("pv1")
        o1 = sem("o1")
        sub_sq = sem("sub_sq")
        sub_mm = sem("sub_mm")
        sub_sqrt = sem("sub_sqrt")
        sub_rec = sem("sub_rec")
        sub_bc = sem("sub_bc")
        sub_t = sem("sub_t")
        sub_hi = sem("sub_hi")
        sub_lo = sem("sub_lo")
        big_in = [[sem(f"big_in{i}{j}") for j in range(2)] for i in range(3)]
        shift_in = [sem(f"shift_in{j}") for j in range(3)]
        sqp_made = [sem(f"sqp_made{j}") for j in range(2)]
        sqp_summed = [sem(f"sqp_summed{j}") for j in range(2)]
        raw_in = [sem(f"raw_in{i}") for i in range(SLOTS)]
        mod_in = [sem(f"mod_in{i}") for i in range(RING)]
        bias_in = [sem(f"bias_in{i}") for i in range(2)]

        pv_ps = ps[:, 5:8].rearrange("p b (t c) -> p (b t) c", c=256)

        def ps2(b):
            return ps[:, b:b + 2].rearrange("p a b -> p (a b)")[:, 0:TOK]

        def gate(layer, chunk, v, k):
            m = 12 * layer + 2 * chunk + k // 4
            return mods[:, m, v, k % 4:k % 4 + 1]

        def xa(layer, b, i):
            return 40 * layer + 8 + 8 * b + i

        def ha(layer, b, i):
            return 32 * layer + 8 * b + i

        both = ((0, 0, LAT), (1, LAT, CTX))
        V_BANK = [0, 1, 2, 3, 6, 7]
        NORM_TOK = [TOK, TOK, TOK, LAT, LAT]
        PAIRS = LAT // 256

        def parts(n):
            return [(xl, 0, slice(0, LAT))] + ([(xc, 1, slice(LAT, TOK))] if n == TOK else [])

        ADDED = {1: 0, 2: 32, 3: 40, 4: 72}

        def part(i, j):
            if i < 3:
                return (xl, 0, slice(0, LAT), slice(0, LAT)) if j == 0 else (xc, 1, slice(0, CTX), slice(LAT, TOK))
            half = slice(256 * j, 256 * j + 256)
            return xl, 0, half, half

        def width(s):
            return s.stop - s.start

        block = ctx.enter_context(nc.Block())

        @block.sync
        def _(sp):
            for dst, name in ((cond, "cond"), (ident, "ident"), (b_mod, "b_mod"), (gains, "gains"),
                              (mask, "mask"), (lam_in, "lam"), (subg, "subln")):
                sp.dma_start(dst[:], t[name]).then_inc(consts_in, 16)
            for m in range(4):
                if m == 3:
                    sp.wait_ge(half_summed, 1)
                for j in range(2):
                    sl = slice(4 * j, 4 * j + 4)
                    sp.dma_start(big[:, m % 3, sl], t["w_mod"][m][:, sl]).then_inc(big_in[m % 3][j], 16)
                if m == 1:
                    sp.dma_start(xl[:], t["x"]).then_inc(x_in, 16)
                    sp.dma_start(xc[:], t["ctx"]).then_inc(x_in, 16)

            def load_unit(u, s, first=False):
                if not first:
                    sp.wait_ge(lo_made, u - (SLOTS - 1))
                src = t["units"][bass.ds(u, 1)].rearrange("o p n -> p (o n)")
                sp.dma_start(raw[:, s], src).then_inc(raw_in[s], 16)

            def load_mod(m, k):
                n = 8 * (m - 4) + k
                if not isinstance(n, int) or n >= RING:
                    sp.wait_ge(mod_used, n - (RING - 1))
                src = t["w_mod"][bass.ds(m, 1), :, k, :].rearrange("o p n -> p (o n)")
                sp.dma_start(mod_ring[:, k % RING], src).then_inc(mod_in[k % RING], 16)

            for u in range(SLOTS):
                load_unit(u, u, True)
            for m, k in mix_mods(-1):
                load_mod(m, k)
            sp.wait_ge(h_made, KT)
            sp.dma_start(dft_raw[:], t["dft128"]).then_inc(table_in, 16)
            for u in range(FIRST["out0"]):
                load_unit(u + SLOTS, u % SLOTS)
                for m, k in (mix_mods(u - 1) if 1 <= u <= FIRST["dft"] else ()):
                    load_mod(m, k)
            sp.wait_ge(unit_done, FIRST["v0"] + 1)
            for h in range(2):
                sp.dma_start(bias[:, h], t["bias"][h]).then_inc(bias_in[h], 16)
            for j in range(3):
                sp.wait_ge(v0_lo_s, j + 2)
                sp.dma_start(v0s[0:64, j].bitcast(F32), v0[64:128, j].bitcast(F32)).then_inc(shift_in[j], 16)
                sp.dma_start(v0s[64:128, j].bitcast(F32), v0[0:64, j + 1].bitcast(F32)).then_inc(shift_in[j], 16)
            for h in range(2, HEADS):
                sp.wait_ge(s_made, 6 * (h - 1) - 2)
                sp.dma_start(bias[:, h % 2], t["bias"][h]).then_inc(bias_in[h % 2], 16)
            sp.wait_ge(jk, HEADS)
            sp.wait_ge(jl, HEADS)
            sp.dma_start(xl[:], t["x"]).then_inc(xr_in, 16)
            sp.dma_start(xc[:], t["ctx"]).then_inc(xr_in, 16)
            sp.wait_ge(ol_made, HEADS)
            for i in range(FIRST["mlp0"] - FIRST["out0"]):
                u = FIRST["out0"] + i
                load_unit(u + SLOTS, u % SLOTS)
                for m, k in out_mods(i):
                    load_mod(m, k)

            def mlp_loads(layer, b, mod):
                for i in range(16):
                    u = FIRST[f"mlp{layer}"] + i
                    load_unit(u + SLOTS + 16 * b, u % SLOTS)
                    for k in (MOD_AT[i % 4] if mod else ()):
                        load_mod(12 + 4 * b + i // 4, k)

            with sp.Fori(0, HID_BLOCKS - 1) as b:
                mlp_loads(0, b, True)
            mlp_loads(0, HID_BLOCKS - 1, False)
            sp.wait_ge(h_made, 3 * KT)
            sp.dma_start(cosb[:], t["cos"]).then_inc(table_in, 16)
            sp.dma_start(sinb[:], t["sin"]).then_inc(table_in, 16)
            for u in range(FIRST["k1"], FIRST["out1"]):
                load_unit(u + SLOTS, u % SLOTS)
            sp.wait_ge(jk1, 4)
            sp.dma_start(oneh[:], t["oneh"]).then_inc(oneh_in, 16)
            sp.wait_ge(jk1, 2 * HEADS)
            sp.dma_start(selh[:], t["selh"]).then_inc(oneh_in, 16)
            for u in range(FIRST["out1"], FIRST["mlp1"]):
                load_unit(u + SLOTS, u % SLOTS)
            with sp.Fori(0, HID_BLOCKS - 1) as b:
                mlp_loads(1, b, False)
            for i in range(16 - SLOTS):
                u = FIRST["mlp1"] + i
                load_unit(u + SLOTS + 48, u % SLOTS)
            for k in range(KT):
                sp.wait_ge(out_made, KT + k + 1)
                sp.dma_start(t["out"][:, k], out_t[:, k]).then_inc(out_stored, 16)
            sp.wait_ge(out_stored, 16 * KT)

        @block.gpsimd
        def _(pool):
            def low(u, s):
                pool.wait_ge(hi_made, u + 1)
                nc.gpsimd.tensor_tensor(w_lo[:, s], raw[:, s], w_hi[:, s].bitcast(F32),
                                        op=ALU.subtract).then_inc(lo_made, 1)

            def lows(first, last):
                for u in range(first + AHEAD, last + AHEAD):
                    low(u, u % SLOTS)

            def norm(i):
                pool.wait_ge(h_made, KT * i + 1)
                for k in range(1, KT):
                    pool.wait_ge(hh_made, KT * i + k + 1)
                    nc.gpsimd.tensor_tensor(h_lo[:, k, 0:NORM_TOK[i]], tmp_b[:, k % 2, 0:NORM_TOK[i]],
                                            h_hi[:, k, 0:NORM_TOK[i]].bitcast(F32),
                                            op=ALU.subtract).then_inc(h_made, 1)

            def mlp(layer):
                with pool.Fori(0, HID_BLOCKS - 1) as b:
                    for i in range(16):
                        u = FIRST[f"mlp{layer}"] + AHEAD + i
                        low(u + 16 * b, u % SLOTS)
                for i in range(15 if layer == 0 else 16 - AHEAD):
                    u = FIRST[f"mlp{layer}"] + AHEAD + i
                    low(u + 48, u % SLOTS)

            for u in range(AHEAD):
                low(u, u)
            norm(0)
            lows(FIRST["f"], FIRST["out0"])
            def out_low(h):
                e = 64 * (h % 2)
                pool.wait_ge(oh_made, 3 * h + 3)
                nc.gpsimd.tensor_tensor(o0_lo[e:e + 64, h // 2], osum[e:e + 64, h % 2],
                                        o0_hi[e:e + 64, h // 2].bitcast(F32), op=ALU.subtract).then_inc(ol_made, 1)
                pool.wait_ge(ol_made, h + 1)

            for h in range(HEADS):
                e = 64 * (h % 2)
                pool.wait_ge(bias_in[h % 2], 16 * (h // 2 + 1))
                bv = bias[:, h % 2].rearrange("p v (c r) -> p v c r", r=ROWS)
                for v in range(3):
                    ins = nc.gpsimd.tensor_tensor(bv[:, v], mask[:, v].unsqueeze(2).broadcast_to([P, 32, ROWS]),
                                                  bv[:, v], op=ALU.subtract)
                ins.then_inc(bias_ok, 1)
                pool.wait_ge(bias_ok, h + 1)
                def queries_low():
                    if h == 0:
                        pool.wait_ge(unit_done, FIRST["out0"])
                    pool.wait_ge(jh, h + 1)
                    nc.gpsimd.tensor_tensor(q2b[e:e + 64, h % 2], q0[e:e + 64, h // 2],
                                            q2a[e:e + 64, h % 2].bitcast(F32), op=ALU.subtract).then_inc(jl, 1)
                    pool.wait_ge(jl, h + 1)

                def bias_low():
                    for v in range(3):
                        pool.wait_ge(bh_made, 3 * h + v + 1)
                        nc.gpsimd.tensor_tensor(bias_lo[:, h % 2, v], bias[:, h % 2, v], bias_hi[v][:].bitcast(F32),
                                                op=ALU.subtract).then_inc(bl_made, 1)
                    pool.wait_ge(bl_made, 3 * h + 3)

                if h:
                    queries_low()
                bias_low()
                if h == 0:
                    queries_low()
                if h >= 2:
                    out_low(h - 2)
            for h in (HEADS - 2, HEADS - 1):
                out_low(h)
            lows(FIRST["out0"], FIRST["mlp0"] - 1)
            norm(1)
            lows(FIRST["mlp0"] - 1, FIRST["mlp0"])
            mlp(0)
            norm(2)
            lows(FIRST["k1"] - 1, FIRST["k1"])
            lows(FIRST["k1"], FIRST["out1"] - 1)
            pool.wait_ge(lo_made, FIRST["out1"] + AHEAD - 1)

            def queries1(h):
                for i in range(2):
                    e = 64 * i
                    if h == 1 and i == 0:
                        pool.wait_ge(jk1, 2)
                    if h >= 2 and i == 0:
                        pool.wait_ge(s1, 8 * (h - 1))
                    nc.gpsimd.tensor_copy(aq2a[h % 2][i][e:e + 64], q1[e:e + 64, h]).then_inc(jh1, 1)
                    pool.wait_ge(jh1, 2 * h + i + 1)
                    nc.gpsimd.tensor_tensor(aq2b[h % 2][i][e:e + 64], q1[e:e + 64, h],
                                            aq2a[h % 2][i][e:e + 64].bitcast(F32), op=ALU.subtract).then_inc(jl1, 1)
                    pool.wait_ge(jl1, 2 * h + i + 1)

            def values1(h):
                if h:
                    pool.wait_ge(pv1, 2 * h)
                nc.gpsimd.tensor_copy(avh[:], v1[:, :, P * h:P * h + P]).then_inc(vh1, 1)
                pool.wait_ge(vh1, h + 1)
                nc.gpsimd.tensor_tensor(avl[:], v1[:, :, P * h:P * h + P], avh[:].bitcast(F32),
                                        op=ALU.subtract).then_inc(vl1, 1)
                pool.wait_ge(vl1, h + 1)

            pool.wait_ge(unit_done, FIRST["v1"] + 6)
            pool.wait_ge(rope_done, 1)
            queries1(0)
            lows(FIRST["out1"] - 1, FIRST["out1"])
            pool.wait_ge(lo_made, FIRST["out1"] + AHEAD)
            for h in range(HEADS):
                if h + 1 < HEADS:
                    queries1(h + 1)
                if h == 0:
                    pool.wait_ge(v1_out, 2 * NT)
                values1(h)
                if h:
                    pool.wait_ge(o1, PAIRS * h)
                    nc.gpsimd.tensor_tensor(osq[h - 1][:], o_raw[:, h - 1], o_raw[:, h - 1], op=ALU.mult).then_inc(sub_sq, 1)
            lows(FIRST["out1"], FIRST["mlp1"] - 1)
            norm(3)
            lows(FIRST["mlp1"] - 1, FIRST["mlp1"])
            mlp(1)

        @block.scalar
        def _(act):
            def high(u, s, n):
                act.wait_ge(raw_in[s], n)
                if not isinstance(u, int) or u >= SLOTS:
                    act.wait_ge(unit_done, u - (SLOTS - 1))
                nc.scalar.activation(w_hi[:, s], raw[:, s], ACT.Copy).then_inc(hi_made, 1)

            def high_u(u):
                high(u, u % SLOTS, 16 * (u // SLOTS + 1))

            def high_b(u, b):
                high(u + 16 * b, u % SLOTS, 64 * b + 16 * (u // SLOTS + 1))

            def squares(i, m):
                if i:
                    act.wait_ge(x_added, ADDED[i] + m + 1)
                if m >= 2:
                    act.wait_ge(sq_summed, 6 * i + m - 1)
                elif i:
                    act.wait_ge(sqp_summed[1], 2 * i)
                for x, _, cols in parts(NORM_TOK[i]):
                    ins = nc.scalar.activation(tmp_b[:, m % 2, cols], x[:, m], ACT.Square)
                ins.then_inc(sq_made, 1)

            def squares_part(i, m, j):
                x, _, cols, tok = part(i, j)
                if i and j == 0:
                    act.wait_ge(first_added, 2 * (i - 1) + m - 5)
                elif i:
                    act.wait_ge(x_added, ADDED[i] + m + 1)
                act.wait_ge(sq_summed, 6 * i + m - 1)
                nc.scalar.activation(tmp_b[:, m % 2, tok], x[:, m, cols], ACT.Square).then_inc(sqp_made[j], 1)

            def norm_root(i, j):
                c = slice(part(i, j)[3].start // P, part(i, j)[3].stop // P)
                act.wait_ge(norm_sum, 2 * i + j + 1)
                nc.scalar.activation(stat[:, 40 + c.start:40 + c.stop], ps[:, 6 + j, 0:width(c)],
                                     ACT.Sqrt, bias=eps_c[:, 0:1], scale=1.0 / D).then_inc(norm_sqrt, 1)

            def tail(i):
                squares_part(i, 6, 0)
                squares_part(i, 7, 0)
                squares_part(i, 6, 1)
                norm_root(i, 0)
                squares_part(i, 7, 1)
                norm_root(i, 1)

            def norm(i):
                n = NORM_TOK[i]
                for k in range(KT):
                    if k == 0:
                        for j in range(2):
                            _, v, _, tok = part(i, j)
                            act.wait_ge(first_t if j == 0 else t_made, i + 1 if j == 0 else KT * i + 1)
                            ins = nc.scalar.activation(tmp_b[:, 0, tok], tmp_a[:, 0, tok], ACT.Identity,
                                                       scale=gs[:, i, v, 0:1], bias=gate(i // 2, 3 * (i % 2), v, 0))
                        ins.then_inc(aff_made, 1)
                        continue
                    act.wait_ge(t_made, KT * i + k + 1)
                    if k >= 2:
                        act.wait_ge(h_made, KT * i + k - 1)
                    for _, v, cols in parts(n):
                        ins = nc.scalar.activation(tmp_b[:, k % 2, cols], tmp_a[:, k % 2, cols], ACT.Identity,
                                                   scale=gs[:, i, v, k:k + 1],
                                                   bias=gate(i // 2, 3 * (i % 2), v, k))
                    ins.then_inc(aff_made, 1)

            def mlp(layer):
                u0 = FIRST[f"mlp{layer}"]

                def blk(b, last):
                    for i in range(16):
                        u = u0 + i
                        if not (last and (i == 15 or layer == 1 and i + AHEAD >= 16)):
                            high_b(u + AHEAD, b)
                        if i < 8:
                            act.wait_ge(unit_done, u + 16 * b + 1)
                            a = ha(layer, b, i)
                            if i >= 2:
                                act.wait_ge(relu_used, a - 1)
                            for bank, c0, n in both[:2 - layer]:
                                ins = nc.scalar.activation(tmp_a[:, i % 2, c0:c0 + n],
                                                           ps[:, 2 * (u % 2) + bank, 0:n], ACT.Relu)
                            ins.then_inc(relu_made, 1)
                        elif last and i < 14:
                            squares(2 + 2 * layer, i - 8)
                    if last:
                        tail(2 + 2 * layer)

                with act.Fori(0, HID_BLOCKS - 1) as b:
                    blk(b, False)
                blk(HID_BLOCKS - 1, True)

            act.wait_ge(consts_in, 16 * 7)
            nc.scalar.activation(ctmp[:], cond[:], ACT.Exp, scale=-1.0).then_inc(exp_c, 1)
            act.wait_ge(lam_mm, 1)
            nc.scalar.activation(lam_t[:, 2:4], ps[:, 6, 0:2], ACT.Exp).then_inc(lam_exp, 1)

            def half_rows(m):
                act.wait_ge(half_summed, m + 1)
                if m >= 2:
                    act.wait_ge(half_turned, m - 1)
                nc.scalar.activation(mod_acc[0:2, m % 2], ps[0:2, m % 2], ACT.Copy).then_inc(half_out, 1)

            half_rows(0)
            half_rows(1)
            act.wait_ge(x_in, 32)
            for m in range(6):
                squares(0, m)
            for m in (6, 7):
                for j in range(2):
                    squares_part(0, m, j)
            half_rows(2)
            norm_root(0, 0)
            norm_root(0, 1)
            high_u(0)
            high_u(1)
            half_rows(3)
            high_u(2)
            norm(0)
            for i in range(4):
                u = FIRST["f"] + i
                high_u(u + AHEAD)
                act.wait_ge(unit_done, u + 1)
                for bank, c0, n in both:
                    ins = nc.scalar.activation(f_hi[:, i, c0:c0 + n], ps[:, 2 * (u % 2) + bank, 0:n], ACT.Copy)
                ins.then_inc(f_hi_s, 1)
            act.wait_ge(table_in, 16)
            nc.scalar.activation(dft_hi[:], dft_raw[:], ACT.Copy).then_inc(dft_hi_s, 1)
            for name, dst, scale in (("q0", q0, -1.0 / 8), ("k0", k0, 1.0)):
                for i in range(4):
                    u = FIRST[name] + i
                    high_u(u + AHEAD)
                    act.wait_ge(unit_done, u + 1)
                    for bank, c0, n in both:
                        ins = nc.scalar.activation(dst[:, i, c0:c0 + n], ps[:, 2 * (u % 2) + bank, 0:n],
                                                   ACT.Copy, scale=scale)
                    ins.then_inc(qk_out, 1)
            act.wait_ge(dft_lo_s, 1)
            for n in range(2 * NT):
                act.wait_ge(u_mm, n + 1)
                nc.scalar.activation(u_hi[:, n // 2, 2 * (n % 2):2 * (n % 2) + 2].rearrange("p g c -> p (g c)"),
                                     ps[:, V_BANK[n % 6]], ACT.Copy).then_inc(u_hi_s, 1)
            for i in range(5):
                high_u(FIRST["dft"] + i + AHEAD)
            for g in range(4):
                act.wait_ge(unit_done, FIRST["dft"] + 4)
                nc.scalar.activation(y_hi[:, g, 0:LAT], ps[:, g], ACT.Copy).then_inc(y_hi_s, 1)
            for g in range(2):
                act.wait_ge(unit_done, FIRST["dft"] + 5)
                nc.scalar.activation(y_hi[:, 2 * g:2 * g + 2, LAT:TOK],
                                     ps[:, 6 + g].rearrange("p (g c) -> p g c", g=2), ACT.Copy).then_inc(y_hi_s, 1)
            for i in range(4):
                high_u(FIRST["v0"] + i + AHEAD)

            def swaps(h):
                e, o = 64 * (h % 2), 64 - 64 * (h % 2)
                act.wait_ge(jl, h + 1)
                nc.scalar.activation(q2a[o:o + 64, h % 2], q2b[e:e + 64, h % 2].bitcast(F32), ACT.Copy)
                nc.scalar.activation(q2b[o:o + 64, h % 2], q2a[e:e + 64, h % 2].bitcast(F32),
                                     ACT.Copy).then_inc(js, 1)

            def p_high(n):
                c = 4 if n % NT < 4 else 2
                act.wait_ge(tr_made, n + 1)
                if n >= 2:
                    act.wait_ge(pv_made, n - 1)
                nc.scalar.activation(pt0[:, n % 2, 0:c, 0:P], ps[:, 3 + n % 2, 0:128 * c].rearrange("p (c q) -> p c q", c=c),
                                     ACT.Copy).then_inc(th_made, 1)

            def bias_high(h, v):
                if h:
                    act.wait_ge(s_made, 6 * h - 2)
                act.wait_ge(bias_ok, h + 1)
                nc.scalar.activation(bias_hi[v][:], bias[:, h % 2, v], ACT.Copy).then_inc(bh_made, 1)

            def out_half(r):
                h, j, e = r // 3, r % 3, 64 * (r // 3 % 2)
                act.wait_ge(pv_made, 2 * r + 2)
                if h >= 2 and j == 0:
                    act.wait_ge(ol_made, h - 1)
                nc.scalar.activation(osum[e:e + 64, h % 2, 256 * j:256 * j + 256].rearrange("p (t q) -> p t q", q=P),
                                     pv_ps[64:128, 2 * j:2 * j + 2, 0:P], ACT.Copy).then_inc(oc_made, 1)

            def out_high(r):
                h, j, e = r // 3, r % 3, 64 * (r // 3 % 2)
                act.wait_ge(od_made, r + 1)
                sl = slice(256 * j, 256 * j + 256)
                nc.scalar.activation(o0_hi[e:e + 64, h // 2, sl], osum[e:e + 64, h % 2, sl], ACT.Copy).then_inc(oh_made, 1)

            act.wait_ge(mod_done, 10)
            nc.scalar.activation(ident_r[:], ident[:], ACT.Copy).then_inc(ident_ok, 1)
            for v in range(3):
                bias_high(0, v)
            act.wait_ge(unit_done, FIRST["out0"])
            for n in range(NT):
                nc.scalar.activation(v0[:, n, :, 0:HD], ps[:, V_BANK[n]].rearrange("p (h d) -> p h d", d=HD),
                                     ACT.Copy).then_inc(v0_hi_s, 1)
                if n == 1:
                    swaps(0)
            N0 = 6 * HEADS
            for n in range(N0 + 5):
                h, t_ = n // 6, n % 6
                if n < N0:
                    act.wait_ge(m_made, n + 1)
                    if n >= PROBS:
                        act.wait_ge(tr_made, n - PROBS + 1)
                    w = 512 if t_ < 4 else 256
                    nc.scalar.activation(prob0[:, n % PROBS, 0:w], ps[:, n % 3, 0:w], ACT.Exp, scale=-1.0,
                                         bias=stat[:, n % 4:n % 4 + 1],
                                         accum_out=stat[:, 4 + n % 4:5 + n % 4]).then_inc(e_made, 1)
                if 1 <= n <= N0:
                    p_high(n - 1)
                if h + 1 < HEADS and t_ == 2:
                    swaps(h + 1)
                if h + 1 < HEADS and 2 <= t_ < 5:
                    bias_high(h + 1, t_ - 2)
                if n >= 5 and n % 2 == 1:
                    out_high((n - 5) // 2)
                if n >= 3 and n % 2 == 1 and n < N0 + 3:
                    out_half((n - 3) // 2)
            for i in range(8):
                u = FIRST["out0"] + i
                if i < 7:
                    high_u(u + AHEAD)
                if i < 6:
                    squares(1, i)
            tail(1)
            norm(1)
            high_u(FIRST["mlp0"] + AHEAD - 1)
            mlp(0)
            norm(2)
            high_u(FIRST["k1"] + AHEAD - 1)
            for i in range(16):
                u = FIRST["k1"] + i
                high_u(u + AHEAD)
                if i < 8:
                    act.wait_ge(unit_done, u + 1)
                    nc.scalar.activation(k1[:, i, LAT:TOK], ps[:, 2 * (u % 2) + 1, 0:CTX], ACT.Copy).then_inc(kc_out, 1)
            def keys_high1(h, i):
                e = 64 * i
                if h >= 2 and i == 0:
                    act.wait_ge(s1, 8 * (h - 1))
                nc.scalar.activation(ak2[h % 2][i][e:e + 64], k1[e:e + 64, h], ACT.Copy).then_inc(kh1, 1)

            def swaps1(h, i):
                e, o, a, b = 64 * i, 64 - 64 * i, aq2a[h % 2][i], aq2b[h % 2][i]
                act.wait_ge(jl1, 2 * h + i + 1)
                nc.scalar.activation(a[o:o + 64], b[e:e + 64].bitcast(F32), ACT.Copy)
                nc.scalar.activation(b[o:o + 64], a[e:e + 64].bitcast(F32), ACT.Copy).then_inc(js1, 1)

            for j in range(2):
                for i in range(4):
                    high_u(FIRST["v1"] + 4 * j + i + AHEAD)
                if j == 0:
                    act.wait_ge(rope_done, 1)
                else:
                    act.wait_ge(unit_done, FIRST["v1"] + 5)
                    for i in range(2):
                        keys_high1(0, i)
                        swaps1(0, i)
                act.wait_ge(unit_done, FIRST["v1"] + 4 * j + 4)
                for n in range(NT):
                    nc.scalar.activation(v1[:, n, 512 * j:512 * j + 512], ps[:, V_BANK[n]], ACT.Copy).then_inc(v1_out, 1)

            def p_high1(n):
                act.wait_ge(tr1, n + 1)
                if n % 2 == 0 and n >= 2:
                    act.wait_ge(pv1, n // 2)
                for j in range(2):
                    ins = nc.scalar.activation(at_hi[:, 3 * j:3 * j + 3, P * (n % 2):P * (n % 2) + P],
                                               ps[:, 4 + j, 0:384].rearrange("p (c q) -> p c q", c=3), ACT.Copy)
                ins.then_inc(th1, 1)

            def out_copy(m):
                act.wait_ge(pv1, m + 1)
                nc.scalar.activation(o_raw[:, m // 2, 256 * (m % 2):256 * (m % 2) + 256], ps[:, 6 + m % 2, 0:256],
                                     ACT.Copy).then_inc(o1, 1)

            def exps(n, i):
                act.wait_ge(m1, 2 * n + i + 1)
                if n >= 3 and i == 0:
                    act.wait_ge(tr1, n - 2)
                c = 16 + 2 * (n % 3) + i
                nc.scalar.activation(aprob[:, n % 3, i], ps2(2 * i), ACT.Exp, scale=-1.0,
                                     bias=stat[:, c:c + 1], accum_out=stat[:, c + 6:c + 7]).then_inc(e1, 1)

            def scale_second(n):
                act.wait_ge(c1, n + 1)
                c = 29 + 2 * (n % 3)
                nc.scalar.activation(aprob[:, n % 3, 1], aprob[:, n % 3, 1], ACT.Copy,
                                     scale=stat[:, c:c + 1]).then_inc(g1, 1)

            N1 = 4 * HEADS
            for n in range(N1 + 5):
                h = n // 4
                if 1 <= n <= N1:
                    scale_second(n - 1)
                if n < N1:
                    exps(n, 0)
                if 2 <= n <= N1 + 1:
                    p_high1(n - 2)
                if n < N1:
                    exps(n, 1)
                if h + 1 < HEADS and n % 4 < 2:
                    keys_high1(h + 1, n % 4)
                if h + 1 < HEADS and 1 <= n % 4 < 3:
                    swaps1(h + 1, n % 4 - 1)
                if n == N1 + 1:
                    act.wait_ge(sub_mm, HEADS - 1)
                    nc.scalar.activation(sub_r[0:HEADS, 0], ps[0:HEADS, 0], ACT.Sqrt, bias=eps_c[0:HEADS, 1:2],
                                         scale=1.0 / P).then_inc(sub_sqrt, 1)
                if n >= 5 and n % 2 == 1:
                    out_copy((n - 5) // 2)
            act.wait_ge(sub_sq, HEADS - 1)
            act.wait_ge(o1, HEADS * PAIRS)
            nc.scalar.activation(osq[HEADS - 1][:], o_raw[:, HEADS - 1], ACT.Square).then_inc(sub_sq, 1)
            act.wait_ge(sub_mm, HEADS)
            nc.scalar.activation(sub_last[:, 0], ps[0:1, 1], ACT.Sqrt, bias=eps_c[0:1, 1:2],
                                 scale=1.0 / P).then_inc(sub_sqrt, 1)
            for h in range(HEADS):
                act.wait_ge(sub_t, h + 1)
                nc.scalar.activation(o1_hi[:, h], sub_x[:, h % 2], ACT.Copy, scale=subg[:, 1:2]).then_inc(sub_hi, 1)
            for i in range(8):
                u = FIRST["out1"] + i
                if i < 7:
                    high_u(u + AHEAD)
                if i < 6:
                    squares(3, i)
            tail(3)
            norm(3)
            high_u(FIRST["mlp1"] + AHEAD - 1)
            mlp(1)

        @block.vector
        def _(dve):
            st = Steps(dve, dsteps)
            V = nc.vector
            tt = V.tensor_tensor

            def mod_step(k, target, split=True):
                dve.wait_ge(mod_in[k % RING], target)
                w = mod_ring[:, k % RING]
                for v in range(2):
                    if k == 0:
                        ins = V.tensor_scalar(mod_acc[:, v], w, cact[:, 0, v:v + 1], None, ALU.mult)
                    else:
                        dve.wait_ge(dsteps, st.n - 1)
                        ins = V.scalar_tensor_tensor(out=mod_acc[:, v], in0=w, scalar=cact[:, k, v:v + 1],
                                                     in1=mod_acc[:, v], op0=ALU.mult, op1=ALU.add)
                    ins.then_inc(dsteps, 1)
                    st.n = st.n + 1
                dve.wait_ge(dsteps, st.n)
                dve.sem_inc(mod_used, 1)
                if k == KT - 1 and not split:
                    dve.sem_inc(mod_summed, 1)
                elif k == KT - 1:
                    st.wait(V.tensor_copy(acc_hi[:], mod_acc[:]))
                    tt(acc_lo[:], mod_acc[:], acc_hi[:].bitcast(F32), op=ALU.subtract).then_inc(mod_summed, 1)

            def mod_steps(steps):
                for m, k in steps:
                    mod_step(k, 16 * ((8 * (m - 4) + k) // RING + 1), m >= SPLIT_HALF)

            def extract(m):
                dve.wait_ge(mod_rows, m - 3)
                idb = ident[:].unsqueeze(1).broadcast_to([P, 4, P])
                acc = mod_acc[:].rearrange("p v (c q) -> p v c q", c=4)
                for v in range(2):
                    ins = tt(acc[:, v], ps[:, 4 + v].rearrange("p (c q) -> p c q", c=4), idb, op=ALU.mult)
                    ins.then_inc(dsteps, 1)
                    st.n = st.n + 1
                dve.wait_ge(dsteps, st.n)
                st.wait(V.tensor_reduce(modr[:], acc, AX.X, ALU.add))
                one = bass.ds(m, 1)
                for v in range(2):
                    ins = tt(mods[:, one, v, :], modr[:, v:v + 1, :], b_mod[:, one, :], op=ALU.add)
                ins.then_inc(mod_done, 1)

            def scales(i):
                m = 12 * (i // 2) + 2 * (1 + 3 * (i % 2))
                dve.wait_ge(mod_done, m + 2)
                for v in range(2):
                    ins = V.scalar_tensor_tensor(out=gs[:, i, v].rearrange("p (a b) -> p a b", a=2),
                                                 in0=mods[:, m:m + 2, v, :], scalar=1.0,
                                                 in1=gains[:, i].rearrange("p (a b) -> p a b", a=2),
                                                 op0=ALU.add, op1=ALU.mult)
                st.wait(ins)

            def sum_squares(i, m):
                n = NORM_TOK[i]
                dve.wait_ge(sq_made, 6 * i + m + 1)
                if m == 0:
                    V.tensor_copy(ssum[:, 0:n], tmp_b[:, 0, 0:n]).then_inc(sq_summed, 1)
                else:
                    dve.wait_ge(sq_summed, 6 * i + m)
                    tt(ssum[:, 0:n], ssum[:, 0:n], tmp_b[:, m % 2, 0:n], op=ALU.add).then_inc(sq_summed, 1)

            def sum_part(i, m, j):
                tok = part(i, j)[3]
                dve.wait_ge(sqp_made[j], 2 * i + m - 5)
                dve.wait_ge(sq_summed, 6 * i + 6)
                if m == 7:
                    dve.wait_ge(sqp_summed[j], 2 * i + 1)
                tt(ssum[:, tok], ssum[:, tok], tmp_b[:, m % 2, tok], op=ALU.add).then_inc(sqp_summed[j], 1)

            def norm_root(i, j):
                c0, c1 = part(i, j)[3].start // P, part(i, j)[3].stop // P
                dve.wait_ge(norm_sqrt, 2 * i + j + 1)
                st.wait(V.reciprocal(stat[:, 48 + c0:48 + c1], stat[:, 40 + c0:40 + c1]))
                for c in range(c0, c1):
                    ins = V.tensor_scalar(diag[:, c], ident[:], stat[:, 48 + c:49 + c], None, ALU.mult)
                ins.then_inc(norm_diag, 1)

            def add_part(i, m, j):
                x, v, cols, _ = part(i, j)
                u = FIRST[{1: "mlp0", 2: "k1", 3: "mlp1"}[i]] - 8 + m if i < 4 else UNITS - 8 + m
                if j == 0:
                    dve.wait_ge(first_done, 2 * (i - 1) + m - 5)
                    dve.wait_ge(x_added, ADDED[i] + 6)
                else:
                    dve.wait_ge(unit_done, u + 1)
                    dve.wait_ge(x_added, ADDED[i] + m)
                V.scalar_tensor_tensor(out=x[:, m, cols], in0=ps[:, 2 * (u % 2) + j, 0:width(cols)],
                                       scalar=gate((i - 1) // 2, 2 if i % 2 else 5, v, m), in1=x[:, m, cols],
                                       op0=ALU.mult, op1=ALU.add).then_inc(x_added if j else first_added, 1)

            def tail(i):
                add_part(i, 6, 0)
                sum_squares(i, 5)
                sum_part(i, 6, 0)
                add_part(i, 7, 0)
                sum_part(i, 7, 0)
                add_part(i, 6, 1)
                norm_root(i, 0)
                sum_part(i, 6, 1)
                add_part(i, 7, 1)
                sum_part(i, 7, 1)
                norm_root(i, 1)

            def norm(i):
                n = NORM_TOK[i]
                for k in range(KT + 1):
                    if k < KT:
                        if k >= 2:
                            dve.wait_ge(aff_made, KT * i + k - 1)
                        for j in range(2):
                            x, _, cols, tok = part(i, j)
                            if k == 0:
                                dve.wait_ge(norm_rows, 2 * i + j + 1)
                            ins = tt(tmp_a[:, k % 2, tok], x[:, k, cols], ps[:, 6 + j, 0:width(cols)], op=ALU.mult)
                            if k == 0 and j == 0:
                                ins.then_inc(first_t, 1)
                        ins.then_inc(t_made, 1)
                    if k >= 1:
                        dve.wait_ge(aff_made, KT * i + k)
                        V.tensor_copy(h_hi[:, k - 1, 0:n], tmp_b[:, (k - 1) % 2, 0:n]).then_inc(hh_made, 1)
                    if k == 1:
                        dve.wait_ge(hh_made, KT * i + 1)
                        tt(h_lo[:, 0, 0:n], tmp_b[:, 0, 0:n], h_hi[:, 0, 0:n].bitcast(F32),
                           op=ALU.subtract).then_inc(h_made, 1)

            def add_x(layer, units, par, i, m, count):
                dve.wait_ge(unit_done, units)
                if not isinstance(count, int) or count:
                    dve.wait_ge(x_added, count)
                for (x, v, _), (bank, _, n) in zip(parts(TOK if layer == 0 else LAT), both):
                    ins = V.scalar_tensor_tensor(out=x[:, i], in0=ps[:, 2 * par + bank, 0:n], scalar=gate(layer, m, v, i),
                                                 in1=x[:, i], op0=ALU.mult, op1=ALU.add)
                ins.then_inc(x_added, 1)

            def hidden(layer, b, i):
                a = ha(layer, b, i)
                n = TOK if layer == 0 else LAT
                dve.wait_ge(relu_made, a + 1)
                if i >= 2:
                    dve.wait_ge(hid_made, a - 1)
                ins = tt(tmp_b[:, i % 2, 0:n], tmp_a[:, i % 2, 0:n], tmp_a[:, i % 2, 0:n], op=ALU.mult)
                ins.then_inc(relu_used, 1)
                dve.wait_ge(relu_used, a + 1)
                st.wait(V.tensor_copy(hid_hi[:, i, 0:n], tmp_b[:, i % 2, 0:n]))
                tt(hid_lo[:, i, 0:n], tmp_b[:, i % 2, 0:n], hid_hi[:, i, 0:n].bitcast(F32),
                   op=ALU.subtract).then_inc(hid_made, 1)

            def mlp(layer):
                u0 = FIRST[f"mlp{layer}"]

                def blk(b, last):
                    for i in range(16):
                        u = u0 + i
                        def steps():
                            for k in MOD_AT[i % 4]:
                                mod_step(k, 16 * ((8 * (8 + i // 4) + k) // RING + 1) + 8 * 16 * b)

                        mod = layer == 0 and not last
                        if mod and i == 0:
                            steps()
                        if i < 8:
                            hidden(layer, b, i)
                        elif last and i >= 14:
                            pass
                        else:
                            add_x(layer, u + 16 * b + 1, u % 2, i - 8, 5, xa(layer, b, i - 8))
                            if last and i > 8:
                                sum_squares(2 + 2 * layer, i - 9)
                        if mod:
                            if i:
                                steps()
                            if i % 4 == 3:
                                extract(12 + i // 4 + 4 * b)
                    if last:
                        tail(2 + 2 * layer)

                if layer == 0:
                    per = 8 + 4 * (16 + 4)
                else:
                    per = 8
                with st.loop(HID_BLOCKS - 1, per) as b:
                    blk(b, False)
                blk(HID_BLOCKS - 1, True)

            st.wait(V.memset(mod_acc[:, 0, 0:P], 1.0))
            st.wait(V.tensor_copy(ones_r[:], mod_acc[:, 0, 0:P]))
            V.memset(eps_c[:, 0:1], EPS)
            st.wait(V.memset(eps_c[:, 1:2], SUB_EPS))
            dve.sem_inc(ones_ok, 1)
            dve.wait_ge(consts_in, 16 * 7)
            lam = lam_in[:].rearrange("p (a b) -> p a b", b=2)
            tt(lam_t[0:HD, 0:2], lam[:, :, 0], lam[:, :, 1], op=ALU.mult).then_inc(lam_ok, 1)
            dve.wait_ge(exp_c, 1)
            st.wait(V.tensor_scalar(ctmp[:], ctmp[:], 1.0, None, ALU.add))
            st.wait(V.reciprocal(ctmp[:], ctmp[:]))
            tt(cact[:], cond[:], ctmp[:], op=ALU.mult).then_inc(cact_ok, 1)
            dve.wait_ge(cact_ok, 1)
            V.tensor_scalar(subg[:, 1:2], subg[:, 0:1], 1.0 - LAM_INIT, None, ALU.mult)
            dve.wait_ge(lam_exp, 1)
            st.wait(V.scalar_tensor_tensor(out=lam_t[:, 4:5], in0=lam_t[:, 3:4], scalar=LAM_INIT,
                                           in1=lam_t[:, 2:3], op0=ALU.subtract, op1=ALU.subtract))
            def half_add(m):
                dve.wait_ge(half_turned, m + 1)
                tt(mods[:, m], ps[:, 2 + m % 2, 0:8].rearrange("p (c v) -> p v c", v=2),
                   b_mod[:, m].unsqueeze(1).broadcast_to([P, 2, 4]), op=ALU.add).then_inc(mod_done, 1)

            half_add(0)
            for k in range(6):
                sum_squares(0, k)
            for m in (6, 7):
                for j in range(2):
                    sum_part(0, m, j)
            half_add(1)
            norm_root(0, 0)
            norm_root(0, 1)
            half_add(2)
            half_add(3)
            scales(0)
            norm(0)
            mod_steps(mix_mods(-1))
            for i in range(12):
                u = FIRST["f"] + i
                if i < 4:
                    dve.wait_ge(f_hi_s, i + 1)
                    for bank, c0, n in both:
                        ins = tt(f_lo[:, i, c0:c0 + n], ps[:, 2 * (u % 2) + bank, 0:n],
                                 f_hi[:, i, c0:c0 + n].bitcast(F32), op=ALU.subtract)
                    ins.then_inc(f_out, 1)
                if i == 4:
                    dve.wait_ge(dft_hi_s, 1)
                    tt(dft_lo[:], dft_raw[:], dft_hi[:].bitcast(F32), op=ALU.subtract).then_inc(dft_lo_s, 1)
                    dve.wait_ge(dft_lo_s, 1)
                if i == 2:
                    extract(4)
                elif i >= 4 and i % 2 == 0:
                    extract(3 + i // 2)
                mod_steps(mix_mods(i))
            for n in range(2 * NT):
                sl = slice(2 * (n % 2), 2 * (n % 2) + 2)
                dve.wait_ge(u_hi_s, n + 1)
                tt(u_lo[:, n // 2, sl].rearrange("p g c -> p (g c)"), ps[:, V_BANK[n % 6]],
                   u_hi[:, n // 2, sl].rearrange("p g c -> p (g c)").bitcast(F32), op=ALU.subtract).then_inc(u_lo_s, 1)
            extract(9)
            scales(1)
            for g in range(4):
                dve.wait_ge(y_hi_s, g + 1)
                tt(y_lo[:, g, 0:LAT], ps[:, g], y_hi[:, g, 0:LAT].bitcast(F32), op=ALU.subtract).then_inc(y_lo_s, 1)
            for g in range(2):
                dve.wait_ge(y_hi_s, 5 + g)
                sl = slice(2 * g, 2 * g + 2)
                tt(y_lo[:, sl, LAT:TOK], ps[:, 6 + g].rearrange("p (g c) -> p g c", g=2),
                   y_hi[:, sl, LAT:TOK].bitcast(F32), op=ALU.subtract).then_inc(y_lo_s, 1)

            def heads_high(h):
                e, p = 64 * (h % 2), h % 2
                if h >= 2:
                    dve.wait_ge(s_made, 6 * (h - 1))
                V.tensor_copy(q2a[e:e + 64, p], q0[e:e + 64, h // 2]).then_inc(jh, 1)
                V.tensor_copy(k2[e:e + 64, p], k0[e:e + 64, h // 2]).then_inc(kh0, 1)

            def keys_low(h):
                e, o, p = 64 * (h % 2), 64 - 64 * (h % 2), h % 2
                dve.wait_ge(kh0, h + 1)
                tt(k2[o:o + 64, p], k0[e:e + 64, h // 2], k2[e:e + 64, p].bitcast(F32), op=ALU.subtract).then_inc(jk, 1)

            def least(n):
                dve.wait_ge(s_made, n + 1)
                w = 512 if n % 6 < 4 else 256
                V.tensor_reduce(stat[:, n % 4:n % 4 + 1], ps[:, n % 3, 0:w], AX.X, ALU.min).then_inc(m_made, 1)

            def normalise(n):
                w = 512 if n % 6 < 4 else 256
                dve.wait_ge(e_made, n + 1)
                st.wait(V.reciprocal(stat[:, 8 + n % 4:9 + n % 4], stat[:, 4 + n % 4:5 + n % 4]))
                V.tensor_scalar(prob0[:, n % PROBS, 0:w], prob0[:, n % PROBS, 0:w], stat[:, 8 + n % 4:9 + n % 4],
                                None, ALU.mult).then_inc(p_made, 1)

            def p_low(n):
                c = 4 if n % 6 < 4 else 2
                dve.wait_ge(th_made, n + 1)
                tt(pt0[:, n % 2, 0:c, P:2 * P], ps[:, 3 + n % 2, 0:P * c].rearrange("p (c q) -> p c q", c=c),
                   pt0[:, n % 2, 0:c, 0:P].bitcast(F32), op=ALU.subtract).then_inc(tl_made, 1)

            def out_sum(r):
                h, j, e = r // 3, r % 3, 64 * (r // 3 % 2)
                dve.wait_ge(oc_made, r + 1)
                o = osum[e:e + 64, h % 2, 256 * j:256 * j + 256].rearrange("p (t q) -> p t q", q=P)
                st.wait(tt(o, pv_ps[0:64, 2 * j:2 * j + 2, 0:P], o, op=ALU.add))
                tt(o, pv_ps[0:64, 2 * j:2 * j + 2, P:2 * P], o, op=ALU.add).then_inc(od_made, 1)

            dve.wait_ge(unit_done, FIRST["out0"])
            heads_high(0)
            keys_low(0)

            def value_low(n):
                dve.wait_ge(v0_hi_s, n + 1)
                tt(v0[:, n, :, HD:P], ps[:, V_BANK[n]].rearrange("p (h d) -> p h d", d=HD),
                   v0[:, n, :, 0:HD].bitcast(F32), op=ALU.subtract).then_inc(v0_lo_s, 1)

            for n in range(4):
                value_low(n)
            N0 = 6 * HEADS
            for n in range(N0 + 3):
                h, t_ = n // 6, n % 6
                if n < N0:
                    least(n)
                if n < 2:
                    value_low(4 + n)
                if 1 <= n <= N0:
                    normalise(n - 1)
                if 2 <= n <= N0 + 1:
                    p_low(n - 2)
                if n >= 4 and n % 2 == 0:
                    out_sum((n - 4) // 2)
                if h + 1 < HEADS and t_ == 0:
                    heads_high(h + 1)
                if h + 1 < HEADS and t_ == 1:
                    keys_low(h + 1)
            dve.wait_ge(xr_in, 32)
            for i in range(6):
                u = FIRST["out0"] + i
                add_x(0, u + 1, u % 2, i, 2, i)
                if i:
                    sum_squares(1, i - 1)
                if i in (2, 5):
                    extract(9 + (i + 1) // 3)
                mod_steps(out_mods(i))
            tail(1)
            norm(1)
            mlp(0)
            scales(2)
            norm(2)
            scales(3)
            dve.wait_ge(table_in, 16 * 3)
            swap = [(i + 16) % 32 for i in range(32)]
            for i in range(16):
                u = FIRST["k1"] + i
                src = ps[:, 2 * (u % 2), 0:LAT]
                dst = k1[:, i, 0:LAT] if i < 8 else q1[:, i - 8]
                f = 1.0 if i < 8 else -1.0 / 8
                dve.wait_ge(unit_done, u + 1)
                st.wait(V.stream_shuffle(rt[:, 0], src, swap))
                V.scalar_tensor_tensor(out=rt[:, 1], in0=src, scalar=f, in1=cosb[:], op0=ALU.mult,
                                       op1=ALU.mult).then_inc(rope_read, 1)
                st.wait(V.scalar_tensor_tensor(out=rt[:, 2], in0=rt[:, 0], scalar=f, in1=sinb[:], op0=ALU.mult, op1=ALU.mult))
                dve.wait_ge(rope_read, i + 1)
                st.wait(tt(dst, rt[:, 1], rt[:, 2], op=ALU.add))
            dve.sem_inc(rope_done, 1)

            def keys_low1(h, i):
                e, o = 64 * i, 64 - 64 * i
                dve.wait_ge(kh1, 2 * h + i + 1)
                tt(ak2[h % 2][i][o:o + 64], k1[e:e + 64, h], ak2[h % 2][i][e:e + 64].bitcast(F32),
                   op=ALU.subtract).then_inc(jk1, 1)

            def least1(n):
                for i in range(2):
                    dve.wait_ge(s1, 2 * n + i + 1)
                    c = 16 + 2 * (n % 3) + i
                    V.tensor_reduce(stat[:, c:c + 1], ps2(2 * i), AX.X, ALU.min).then_inc(m1, 1)

            def coef(n):
                dve.wait_ge(e1, 2 * n + 2)
                c, d = 22 + 2 * (n % 3), 28 + 2 * (n % 3)
                st.wait(V.reciprocal(stat[:, d:d + 2], stat[:, c:c + 2]))
                V.tensor_scalar(stat[:, d + 1:d + 2], stat[:, d + 1:d + 2], lam_t[:, 4:5], None, ALU.mult).then_inc(c1, 1)

            def combine(n):
                d = 28 + 2 * (n % 3)
                dve.wait_ge(g1, n + 1)
                V.scalar_tensor_tensor(out=aprob[:, n % 3, 0], in0=aprob[:, n % 3, 0], scalar=stat[:, d:d + 1],
                                       in1=aprob[:, n % 3, 1], op0=ALU.mult, op1=ALU.add).then_inc(a1, 1)

            def p_low1(n):
                dve.wait_ge(th1, n + 1)
                for j in range(2):
                    sl = (slice(None), slice(3 * j, 3 * j + 3), slice(P * (n % 2), P * (n % 2) + P))
                    ins = tt(at_lo[sl], ps[:, 4 + j, 0:384].rearrange("p (c q) -> p c q", c=3),
                             at_hi[sl].bitcast(F32), op=ALU.subtract)
                ins.then_inc(tl1, 1)

            N1 = 4 * HEADS
            for i in range(2):
                keys_low1(0, i)
            for n in range(N1 + 2):
                if n < N1:
                    least1(n)
                if 1 <= n <= N1:
                    combine(n - 1)
                if n >= 2:
                    p_low1(n - 2)
                if n < N1:
                    coef(n)
                if n // 4 + 1 < HEADS and 1 <= n % 4 < 3:
                    keys_low1(n // 4 + 1, n % 4 - 1)
            dve.wait_ge(sub_sqrt, 1)
            V.reciprocal(sub_r[0:HEADS, 1], sub_r[0:HEADS, 0]).then_inc(sub_rec, 1)
            for h in range(HEADS + 1):
                if h == 3:
                    dve.wait_ge(sub_sqrt, 2)
                    V.reciprocal(sub_last[:, 1], sub_last[:, 0]).then_inc(sub_rec, 1)
                if h < HEADS:
                    dve.wait_ge(sub_bc, h + 1)
                    if h >= 2:
                        dve.wait_ge(sub_lo, h - 1)
                    tt(sub_x[:, h % 2], o_raw[:, h], ps[:, 4 + h % 2], op=ALU.mult).then_inc(sub_t, 1)
                if h >= 1:
                    dve.wait_ge(sub_hi, h)
                    V.scalar_tensor_tensor(out=o1_lo[:, h - 1], in0=sub_x[:, (h - 1) % 2], scalar=subg[:, 1:2],
                                           in1=o1_hi[:, h - 1].bitcast(F32), op0=ALU.mult,
                                           op1=ALU.subtract).then_inc(sub_lo, 1)
            for i in range(6):
                u = FIRST["out1"] + i
                add_x(1, u + 1, u % 2, i, 2, 40 + i)
                if i:
                    sum_squares(3, i - 1)
            tail(3)
            norm(3)
            mlp(1)
            for j in range(2):
                cols = part(4, j)[2]
                dve.wait_ge(norm_rows, 8 + j + 1)
                for k in range(KT):
                    V.scalar_tensor_tensor(out=out_t[:, k, cols], in0=xl[:, k, cols], scalar=gains[:, 4, k:k + 1],
                                           in1=ps[:, 6 + j, 0:width(cols)], op0=ALU.mult, op1=ALU.mult
                                           ).then_inc(out_made, 1)

        @block.tensor
        def _(pe):
            mm = nc.tensor.matmul

            def three(out, a, b, start, stop, last=None):
                mm(out, a[0], b[1], start=start, stop=False)
                mm(out, a[1], b[0], start=False, stop=False)
                return mm(out, a[0], b[0], start=False, stop=stop)

            def unit(u, s, par, hi, lo, chunks, k_wait=None):
                pe.wait_ge(lo_made, u + 1)
                for k in range(KT):
                    if k_wait:
                        k_wait(k)
                    w = (w_hi[:, s, P * k:P * k + P], w_lo[:, s, P * k:P * k + P])
                    for bank, c0, n in chunks:
                        ins = three(ps[:, 2 * par + bank, 0:n], w, (hi(k)[:, c0:c0 + n], lo(k)[:, c0:c0 + n]),
                                    k == 0, k == KT - 1)
                ins.then_inc(unit_done, 1)

            def unit_pair(u, s, par, hi, lo, chunks, second_free, k_wait):
                order = [(0, 0), (0, 1), (1, 0), (1, 1)] + [(j, k) for k in range(2, 6) for j in range(2)]
                for j, k in order + [(0, 6), (0, 7), (1, 6), (1, 7)]:
                    if k == 0:
                        if j:
                            second_free()
                        pe.wait_ge(lo_made, u + j + 1)
                    if j == 0:
                        k_wait(k)
                    w = (w_hi[:, (s + j) % SLOTS, P * k:P * k + P], w_lo[:, (s + j) % SLOTS, P * k:P * k + P])
                    for bank, c0, n in chunks:
                        ins = three(ps[:, 2 * ((par + j) % 2) + bank, 0:n], w, (hi(k)[:, c0:c0 + n], lo(k)[:, c0:c0 + n]),
                                    k == 0, k == KT - 1)
                    if k == KT - 1:
                        ins.then_inc(unit_done, 1)

            def h_wait(i):
                return lambda k: pe.wait_ge(h_made, KT * i + k + 1)

            h_t = (lambda k: h_hi[:, k], lambda k: h_lo[:, k])
            hid_t = (lambda k: hid_hi[:, k], lambda k: hid_lo[:, k])

            def mod_mm(m):
                pe.wait_ge(mod_summed, m - 3)
                for v in range(2):
                    if isinstance(m, int) and m < SPLIT_HALF:
                        ins = mm(ps[:, 4 + v], ones, mod_acc[:, v], start=True, stop=True)
                    else:
                        mm(ps[:, 4 + v], ones_r[:], acc_lo[:, v], start=True, stop=False)
                        ins = mm(ps[:, 4 + v], ones_r[:], acc_hi[:, v], start=False, stop=True)
                ins.then_inc(mod_rows, 1)

            def norm_sums(i, j):
                tok = part(i, j)[3]
                pe.wait_ge(sqp_summed[j], 2 * i + 2)
                for c in range(tok.start // P, tok.stop // P):
                    o = c - tok.start // P
                    ins = mm(ps[:, 6 + j, o:o + 1], ssum[:, P * c:P * c + P], ones[:, 0:1], start=True, stop=True)
                ins.then_inc(norm_sum, 1)

            def norm_spread(i, j):
                tok = part(i, j)[3]
                pe.wait_ge(norm_diag, 2 * i + j + 1)
                mm(ps[:, 6 + j, 0:width(tok)], ones, diag[:].rearrange("p c q -> p (c q)")[:, tok],
                   start=True, stop=True).then_inc(norm_rows, 1)

            def tail(i, u, hi, lo):
                def half(m, j):
                    s, tok = (u + m) % SLOTS, part(i, j)[3]
                    if j == 0:
                        pe.wait_ge(lo_made, u + m + 1)
                        pe.wait_ge(x_added, ADDED[i] + 5 + m)
                    for k in range(KT):
                        ins = three(ps[:, 2 * ((u + m) % 2) + j, 0:width(tok)],
                                    (w_hi[:, s, P * k:P * k + P], w_lo[:, s, P * k:P * k + P]),
                                    (hi(k)[:, tok], lo(k)[:, tok]), k == 0, k == KT - 1)
                    ins.then_inc(unit_done if j else first_done, 1)

                half(0, 0)
                half(1, 0)
                half(0, 1)
                norm_sums(i, 0)
                half(1, 1)
                norm_spread(i, 0)
                norm_sums(i, 1)
                norm_spread(i, 1)

            def values(u, j, start, stop, banks_free=None):
                s = u % SLOTS
                pe.wait_ge(lo_made, u + 1)
                for n in range(NT):
                    if banks_free:
                        banks_free(n)
                    for kk in range(2):
                        k = 2 * j + kk
                        ins = three(ps[:, V_BANK[n]], (h_hi[:, k, P * n:P * n + P], h_lo[:, k, P * n:P * n + P]),
                                    (w_hi[:, s, 512 * kk:512 * kk + 512], w_lo[:, s, 512 * kk:512 * kk + 512]),
                                    start and kk == 0, stop and kk == 1)
                ins.then_inc(unit_done, 1)

            def mlp(layer):
                u0 = FIRST[f"mlp{layer}"]
                chunks = both[:2 - layer]

                def blk(b, last):
                    for i in range(16):
                        u = u0 + i
                        if last and i >= 14:
                            break
                        if i == 0:
                            pe.wait_ge(x_added, xa(layer, b, 0) - 1)
                            unit_pair(u + 16 * b, u % SLOTS, u % 2, *h_t, chunks,
                                      lambda: pe.wait_ge(x_added, xa(layer, b, 0)), h_wait(1 + 2 * layer))
                        elif i == 1:
                            continue
                        elif i < 8:
                            pe.wait_ge(relu_made, ha(layer, b, i) - 1)
                        elif i < 10:
                            pe.wait_ge(relu_made, ha(layer, b, i) - 1)
                        else:
                            pe.wait_ge(x_added, xa(layer, b, i - 8) - 1)
                        if 2 <= i < 8:
                            unit(u + 16 * b, u % SLOTS, u % 2, *h_t, chunks)
                        elif i >= 8:
                            unit(u + 16 * b, u % SLOTS, u % 2, *hid_t, chunks,
                                 (lambda k: pe.wait_ge(hid_made, ha(layer, b, k) + 1)) if i == 8 else None)
                        if layer == 0 and not last and i % 4 == 3:
                            pe.wait_ge(mod_done, 12 + 4 * b + i // 4)
                            mod_mm(12 + 4 * b + i // 4)

                with pe.Fori(0, HID_BLOCKS - 1) as b:
                    blk(b, False)
                blk(HID_BLOCKS - 1, True)
                tail(2 + 2 * layer, u0 + 16 * HID_BLOCKS - 2, *hid_t)

            pe.wait_ge(ones_ok, 1)
            pe.wait_ge(lam_ok, 1)
            mm(ps[:, 6, 0:2], ones[0:HD, :], lam_t[0:HD, 0:2], start=True, stop=True).then_inc(lam_mm, 1)

            def half_mm(m):
                if m == 0:
                    pe.wait_ge(cact_ok, 1)
                if m >= 2:
                    pe.wait_ge(half_out, m - 1)
                for k in range(KT):
                    if k % 4 == 0:
                        pe.wait_ge(big_in[m % 3][k // 4], 16 * (m // 3 + 1))
                    ins = mm(ps[0:2, m % 2], cact[:, k], big[:, m % 3, k], start=k == 0, stop=k == KT - 1)
                ins.then_inc(half_summed, 1)

            def half_turn(m):
                pe.wait_ge(half_out, m + 1)
                if m >= 2:
                    pe.wait_ge(mod_done, m - 1)
                for c in range(4):
                    ins = mm(ps[:, 2 + m % 2, 2 * c:2 * c + 2], mod_acc[0:2, m % 2, P * c:P * c + P], ident[0:2, 0:2],
                             start=True, stop=True)
                ins.then_inc(half_turned, 1)

            half_mm(0)
            half_mm(1)
            half_turn(0)
            half_mm(2)
            half_turn(1)
            norm_sums(0, 0)
            norm_sums(0, 1)
            half_mm(3)
            norm_spread(0, 0)
            norm_spread(0, 1)
            half_turn(2)
            half_turn(3)
            pe.wait_ge(mod_done, 4)

            for i in range(12):
                u = FIRST["f"] + i
                if 2 <= i < 6:
                    pe.wait_ge(f_out, i - 1)
                elif i >= 6:
                    pe.wait_ge(qk_out, i - 5)
                if i == 0:
                    unit_pair(u, u % SLOTS, u % 2, *h_t, both, lambda: None, h_wait(0))
                elif i >= 2:
                    unit(u, u % SLOTS, u % 2, *h_t, both)
                if i == 2:
                    mod_mm(4)
                elif i >= 4 and i % 2 == 0:
                    pe.wait_ge(mod_done, 3 + i // 2)
                    mod_mm(3 + i // 2)
            pe.wait_ge(f_out, 4)
            pe.wait_ge(dft_lo_s, 1)
            pe.wait_ge(qk_out, 8)
            for n in range(2 * NT):
                tok = slice(P * (n // 2), P * (n // 2) + P)
                if n >= 6:
                    pe.wait_ge(u_lo_s, n - 5)
                for j in range(2):
                    g = 2 * (n % 2) + j
                    ins = three(ps[:, V_BANK[n % 6], 256 * j:256 * j + 256], (f_hi[:, g, tok], f_lo[:, g, tok]),
                                (dft_hi[:], dft_lo[:]), True, True)
                ins.then_inc(u_mm, 1)
            pe.wait_ge(mod_done, 9)
            mod_mm(9)
            pe.wait_ge(u_lo_s, 2 * NT)
            for i in range(4):
                u = FIRST["dft"] + i
                s = u % SLOTS
                pe.wait_ge(lo_made, u + 1)
                for g in range(4):
                    c = slice(P * (i // 2), P * (i // 2) + P)
                    for j in range(2):
                        n = 2 * (i % 2) + j
                        ins = three(ps[:, g], (u_hi[:, n, g, c], u_lo[:, n, g, c]),
                                    (w_hi[:, s, 512 * j:512 * j + 512], w_lo[:, s, 512 * j:512 * j + 512]),
                                    i == 0 and j == 0, i == 3 and j == 1)
                ins.then_inc(unit_done, 1)
            u = FIRST["dft"] + 4
            s = u % SLOTS
            pe.wait_ge(lo_made, u + 1)
            for g in range(4):
                for j in range(4):
                    c = slice(P * (j // 2), P * (j // 2) + P)
                    n = 4 + j % 2
                    ins = three(ps[:, 6 + g // 2, 256 * (g % 2):256 * (g % 2) + 256], (u_hi[:, n, g, c], u_lo[:, n, g, c]),
                                (w_hi[:, s, 256 * j:256 * j + 256], w_lo[:, s, 256 * j:256 * j + 256]), j == 0, j == 3)
            ins.then_inc(unit_done, 1)
            def y_free(n):
                pe.wait_ge(y_lo_s, min(n + 1, 4) if n < 4 else n + 1)

            for i in range(4):
                values(FIRST["v0"] + i, i, i == 0, i == 3, y_free if i == 0 else None)

            def scores(n):
                h, t_ = n // 6, n % 6
                p = h % 2
                if t_ == 0:
                    pe.wait_ge(js, h + 1)
                    pe.wait_ge(jk, h + 1)
                if n >= 3:
                    pe.wait_ge(e_made, n - 2)
                else:
                    pe.wait_ge(v0_lo_s, n + 1)
                tok = slice(P * t_, P * t_ + P)
                keys = [slice(LAT, TOK)] if t_ >= 4 else [slice(WINDOW[t_], WINDOW[t_] + 256), slice(LAT, TOK)]
                if t_ < 4:
                    v = VARIANT[t_]
                    pe.wait_ge(bl_made, 3 * h + v + 1)
                    mm(ps[:, n % 3, 0:256], ident_r[:], bias_lo[:, p, v], start=True, stop=False)
                    mm(ps[:, n % 3, 0:256], ident_r[:], bias_hi[v][:], start=False, stop=False)
                for j, ks in enumerate(keys):
                    o = ps[:, n % 3, 256 * j:256 * j + 256]
                    mm(o, q2b[:, p, tok], k2[:, p, ks], start=t_ >= 4 or j == 1, stop=False)
                    ins = mm(o, q2a[:, p, tok], k2[:, p, ks], start=False, stop=True)
                ins.then_inc(s_made, 1)

            def turn(n):
                c = 4 if n % 6 < 4 else 2
                if n == 0:
                    pe.wait_ge(v0_lo_s, 4)
                pe.wait_ge(p_made, n + 1)
                if n >= 2:
                    pe.wait_ge(tl_made, n - 1)
                for j in range(c):
                    ins = nc.tensor.transpose(ps[:, 3 + n % 2, P * j:P * j + P], prob0[:, n % PROBS, P * j:P * j + P], ident[:])
                ins.then_inc(tr_made, 1)

            def weigh(n):
                h, t_ = n // 6, n % 6
                pe.wait_ge(tl_made, n + 1)
                if n == 0:
                    pe.wait_ge(v0_lo_s, NT)
                if n == 1:
                    pe.wait_ge(shift_in[0], 32)
                    pe.wait_ge(shift_in[1], 32)
                if n == 2:
                    pe.wait_ge(shift_in[2], 32)
                if t_ % 2 == 0 and h:
                    pe.wait_ge(od_made, n // 2 - 2)
                lat = {0: (v0[:, 0], v0[:, 1]), 1: (v0s[:, 0], v0s[:, 1]), 2: (v0s[:, 1], v0s[:, 2]),
                       3: (v0[:, 2], v0[:, 3])}
                vs = (lat[t_] if t_ < 4 else ()) + (v0[:, 4], v0[:, 5])
                for c, v in enumerate(vs):
                    ins = mm(pv_ps[:, t_, :], v[:, h, :], pt0[:, n % 2, c, :], start=c == 0, stop=c == len(vs) - 1)
                ins.then_inc(pv_made, 1)

            N0 = 6 * HEADS
            pe.wait_ge(mod_done, 10)
            pe.wait_ge(ident_ok, 1)
            scores(0)
            scores(1)
            for n in range(N0 + 1):
                if n + 2 < N0:
                    scores(n + 2)
                if n < N0:
                    turn(n)
                if n >= 1:
                    weigh(n - 1)
            mix_hi = lambda k: y_hi[:, k] if k < 4 else o0_hi[:, k - 4]
            mix_lo = lambda k: y_lo[:, k] if k < 4 else o0_lo[:, k - 4]
            pe.wait_ge(e_made, N0)
            for i in range(6):
                u = FIRST["out0"] + i
                if i >= 2:
                    pe.wait_ge(x_added, i - 1)
                unit(u, u % SLOTS, u % 2, mix_hi, mix_lo, both,
                     (lambda k: pe.wait_ge(ol_made, HEADS) if k == 4 else None) if i == 0 else None)
                if i in (2, 5):
                    pe.wait_ge(mod_done, 9 + (i + 1) // 3)
                    mod_mm(9 + (i + 1) // 3)
            tail(1, FIRST["mlp0"] - 2, mix_hi, mix_lo)
            mlp(0)
            unit_pair(FIRST["k1"], FIRST["k1"] % SLOTS, FIRST["k1"] % 2, *h_t, both, lambda: None, h_wait(2))
            for i in range(2, 16):
                u = FIRST["k1"] + i
                pe.wait_ge(rope_read, i - 1)
                if i < 10:
                    pe.wait_ge(kc_out, i - 1)
                unit(u, u % SLOTS, u % 2, *h_t, both if i < 8 else both[:1])
            pe.wait_ge(rope_read, 16)
            for j in range(2):
                for i in range(4):
                    values(FIRST["v1"] + 4 * j + i, i, i == 0, i == 3,
                           (lambda n: pe.wait_ge(v1_out, n + 1)) if j == 1 and i == 0 else None)

            def scores1(n):
                h, t_ = n // 4, n % 4
                for i in range(2):
                    s = 2 * n + i
                    if t_ == 0:
                        pe.wait_ge(js1, 2 * h + i + 1)
                        pe.wait_ge(jk1, 2 * h + i + 1)
                    if s >= 2:
                        pe.wait_ge(e1, s - 1)
                    else:
                        pe.wait_ge(v1_out, NT + 2 * s + 2)
                    b0 = 2 * (s % 2)
                    tok = slice(P * t_, P * t_ + P)
                    for bank, ks in ((b0, slice(0, LAT)), (b0 + 1, slice(LAT, TOK))):
                        o = ps[:, bank, 0:ks.stop - ks.start]
                        mm(o, aq2b[h % 2][i][:, tok], ak2[h % 2][i][:, ks], start=True, stop=False)
                        ins = mm(o, aq2a[h % 2][i][:, tok], ak2[h % 2][i][:, ks], start=False, stop=True)
                    ins.then_inc(s1, 1)

            def turn1(n):
                if n == 0:
                    pe.wait_ge(v1_out, 2 * NT)
                pe.wait_ge(a1, n + 1)
                if n >= 1:
                    pe.wait_ge(tl1, n)
                for c in range(NT):
                    ins = nc.tensor.transpose(ps[:, 4 + c // 3, P * (c % 3):P * (c % 3) + P],
                                              aprob[:, n % 3, 0, P * c:P * c + P], ident[:])
                ins.then_inc(tr1, 1)

            def weigh1(m):
                pe.wait_ge(tl1, 2 * m + 2)
                if m % 2 == 0:
                    pe.wait_ge(vl1, m // 2 + 1)
                if m >= 2:
                    pe.wait_ge(o1, m - 1)
                for c in range(NT):
                    ins = three(ps[:, 6 + m % 2, 0:256], (avh[:, c], avl[:, c]), (at_hi[:, c], at_lo[:, c]), c == 0, c == NT - 1)
                ins.then_inc(pv1, 1)

            def sub_sums(h):
                pe.wait_ge(sub_sq, h + 1)
                if h < HEADS - 1:
                    mm(ps[0:HEADS, 0], oneh[:, h], osq[h][:], start=h == 0, stop=h == HEADS - 2).then_inc(sub_mm, 1)
                else:
                    mm(ps[0:1, 1], ones[:, 0:1], osq[h][:], start=True, stop=True).then_inc(sub_mm, 1)

            N1 = 4 * HEADS
            scores1(0)
            for n in range(N1 + 4):
                if n >= 4 and n % 2 == 0:
                    weigh1((n - 4) // 2)
                if n + 1 < N1:
                    scores1(n + 1)
                if n == N1:
                    pe.wait_ge(e1, 2 * N1)
                    pe.wait_ge(oneh_in, 32)
                    for h in range(5):
                        sub_sums(h)
                if 1 <= n <= N1:
                    turn1(n - 1)
                if n == N1:
                    for h in range(5, HEADS - 1):
                        sub_sums(h)
            sub_sums(HEADS - 1)
            pe.wait_ge(sub_rec, 1)

            def spread_head(h):
                if h >= 2:
                    pe.wait_ge(sub_t, h - 1)
                if h < HEADS - 1:
                    mm(ps[:, 4 + h % 2], selh[:, h], sub_r[0:HEADS, 1], start=True, stop=True).then_inc(sub_bc, 1)
                else:
                    pe.wait_ge(sub_rec, 2)
                    mm(ps[:, 4 + h % 2], ones[0:1, :], sub_last[:, 1], start=True, stop=True).then_inc(sub_bc, 1)

            def head_wait(k):
                if k + 2 < HEADS:
                    spread_head(k + 2)
                pe.wait_ge(sub_lo, k + 1)

            spread_head(0)
            spread_head(1)
            o_t = (lambda k: o1_hi[:, k], lambda k: o1_lo[:, k])
            u = FIRST["out1"]
            unit_pair(u, u % SLOTS, u % 2, *o_t, both[:1], lambda: None, head_wait)
            for i in range(2, 6):
                u = FIRST["out1"] + i
                pe.wait_ge(x_added, 40 + i - 1)
                unit(u, u % SLOTS, u % 2, *o_t, both[:1])
            tail(3, FIRST["mlp1"] - 2, *o_t)
            mlp(1)


_OUT = (P, KT, LAT)


def _order():
    t = np.arange(LAT)
    return (t % ROWS) * COLS + t // ROWS


def _stationary(w):
    n = w.shape[1] // P
    return w.reshape(KT, P, n, P).transpose(2, 1, 0, 3).reshape(n, P, D)


def _moving(w):
    n = w.shape[1] // 512
    return w.reshape(4, 2, P, n, 512).transpose(3, 0, 2, 1, 4).reshape(4 * n, P, D)


def _mlp(w_in, w_out):
    u = []
    for b in range(HID_BLOCKS):
        u += [_stationary(w_in[:, D * b:D * b + D]), _stationary(w_out[D * b:D * b + D])]
    return u


def _dft(n, order, scale):
    a = 2 * np.pi * (np.outer(order, order) % n) / n
    return np.stack([np.cos(a), -np.sin(a)]) * scale


def _tables():
    order = _order()
    cs = _dft(LAT, order, (LAT * P) ** -0.5).reshape(2, 2, 2, P, LAT).transpose(0, 1, 3, 2, 4).reshape(4, P, D)
    cc = _dft(CTX, np.arange(CTX), (CTX * P) ** -0.5).reshape(4, P, CTX).transpose(1, 0, 2).reshape(1, P, D)
    units = np.concatenate([cs, cc]).astype(np.float32)
    a = 2 * np.pi * (np.outer(np.arange(P), np.arange(P)) % P) / P
    dft128 = np.concatenate([np.cos(a), np.sin(a)], axis=1).astype(np.float32)
    nf = HD // 4
    freq = np.float32(10000.0) ** (-np.arange(nf, dtype=np.float32) / np.float32(nf))
    ang = np.zeros((P, LAT), np.float32)
    sign = np.zeros((P, 1), np.float32)
    for p in range(P):
        pos = order // COLS if p % 64 < 32 else order % COLS
        ang[p] = pos.astype(np.float32) * freq[p % nf]
        sign[p] = -1.0 if p % 32 < nf else 1.0
    cos = np.cos(ang.astype(np.float64)).astype(np.float32)
    sin = (np.sin(ang.astype(np.float64)) * sign).astype(np.float32)
    mask = np.zeros((P, 3, 32), np.float32)
    for v, qt in ((0, 0), (1, 1), (2, 3)):
        col = 16 * qt + np.arange(P) // ROWS
        start = np.clip(col - 8, 0, COLS - 16)
        key = WINDOW[qt] // ROWS + np.arange(32)
        ok = (key[None] >= start[:, None]) & (key[None] < start[:, None] + 16)
        mask[:, v] = np.where(ok, 0.0, -NEG)
    oneh = np.zeros((P, HEADS, HEADS), np.float32)
    selh = np.zeros((HEADS, HEADS, P), np.float32)
    for h in range(HEADS):
        oneh[:, h, h] = 1.0
        selh[h, h] = 1.0
    return units, dict(dft128=dft128, cos=cos, sin=sin, mask=mask, ident=np.eye(P, dtype=np.float32),
                       oneh=oneh, selh=selh)


def _bias(rpb):
    q = np.arange(P)
    k = np.arange(256)
    out = []
    for v, qt in ((0, 0), (1, 1), (2, 3)):
        qc, qr = 16 * qt + q // ROWS, q % ROWS
        kc, kr = WINDOW[qt] // ROWS + k // ROWS, k % ROWS
        dr = kr[None] - qr[:, None] + 7
        dc = np.clip(kc[None] - qc[:, None], -15, 15) + 15
        out.append(rpb[:, dr, dc])
    return np.stack(out, axis=2)


def _columns(v):
    v = v.reshape(v.shape[:-1] + (v.shape[-1] // P, P))
    return np.moveaxis(v, -1, 0)


def _layout(i):
    order = _order()
    tables, d = _tables()
    w_ab, w_qkv = i["w_in_ab"][0], i["w_qkv_diff"][0]
    units = ([_stationary(w_ab[:, :1536])] + [tables] + [_moving(w_ab[:, 1536:])] + [_stationary(i["w_out_ab"][0])]
             + _mlp(i["w_mlp_in"][0], i["w_mlp_out"][0])
             + [_stationary(w_qkv[:, D:2 * D]), _stationary(w_qkv[:, :D]), _moving(w_qkv[:, 2048:]), _stationary(i["w_out_diff"][0])]
             + _mlp(i["w_mlp_in"][1], i["w_mlp_out"][1]))
    d["units"] = np.concatenate(units)
    d["x"] = i["x"][0][order].T.reshape(KT, P, LAT).transpose(1, 0, 2)
    d["ctx"] = i["ctx"][0].T.reshape(KT, P, CTX).transpose(1, 0, 2)
    d["w_mod"] = i["w_mod"].reshape(2, KT, P, 12, 512).transpose(0, 3, 2, 1, 4).reshape(24, P, KT, 512)
    d["b_mod"] = _columns(i["b_mod"].reshape(24, 512))
    d["gains"] = _columns(np.stack([i["norm_mix_g"][0], i["norm_mlp_g"][0], i["norm_mix_g"][1], i["norm_mlp_g"][1],
                                    i["final_norm_g"]]))
    d["cond"] = np.stack([_columns(i["c"][0]), _columns(i["c_ctx"])], axis=2)
    d["lam"] = np.stack([i["diff_lq1"][0], i["diff_lk1"][0], i["diff_lq2"][0], i["diff_lk2"][0]], axis=1)
    d["subln"] = np.stack([i["diff_subln_g"][0]] * 2, axis=1)
    d["bias"] = _bias(i["na_rpb"][0])
    return {k: np.ascontiguousarray(v) for k, v in d.items()}


def kernel(**inputs):
    import concourse.bacc as bacc
    from concourse.bass_utils import run_bass_kernel_spmd

    nc = bacc.Bacc("TRN2", target_bir_lowering=False, num_devices=1)
    data = _layout({k: np.asarray(v) for k, v in inputs.items()})
    t = {k: nc.dram_tensor(k + "_dram", v.shape, mybir.dt.from_np(v.dtype), kind="ExternalInput").ap()
         for k, v in data.items()}
    t["out"] = nc.dram_tensor("out_dram", _OUT, F32, kind="ExternalOutput").ap()
    build(nc, t)
    r = run_bass_kernel_spmd(nc, [{k + "_dram": v for k, v in data.items()}], core_ids=[0])
    out = np.asarray(r.results[0]["out_dram"]).transpose(2, 1, 0).reshape(LAT, D)
    back = np.empty_like(out)
    back[_order()] = out
    return back[None]
```
